# Optimizing a Trainium2 kernel written in Bass

```python
import jax, jax.numpy as jnp
from jax import lax
import numpy as np
import math

D_MODEL = 1024
BATCH = 1
SEQ = 256
DEPTH = 2

D_FF = 2816
FFN_RESID = 0.5
EPS = 1e-6
GM_WIDTH = 512
GM_GROUPS = 4
GM_GROUP_DIM = GM_WIDTH // GM_GROUPS
GM_CHUNK = 128
MLA_HEADS = 8
MLA_Q_RANK = 384
MLA_KV_RANK = 256
MLA_NOPE = 64
MLA_ROPE = 32
MLA_QK_DIM = MLA_NOPE + MLA_ROPE
MLA_V = 64
MLA_WIDTH = MLA_HEADS * MLA_V
ROPE_THETA = 10000.0
Q_BLOCK = 128
SSD_HEADS = 8
SSD_HEAD_DIM = 64
SSD_INNER = SSD_HEADS * SSD_HEAD_DIM
SSD_GROUPS = 2
SSD_STATE = 128
SSD_CONV = 4
SSD_CHUNK = 128
SSD_CONV_DIM = SSD_INNER + 2 * SSD_GROUPS * SSD_STATE
N_BRANCH = 3
BRANCH_WIDTH = 512
IN_WIDTHS = (2 * GM_WIDTH, MLA_Q_RANK, MLA_KV_RANK, MLA_ROPE, SSD_INNER, SSD_CONV_DIM, SSD_HEADS, N_BRANCH * D_MODEL)
IN_COLS = sum(IN_WIDTHS)
IN_OFFSETS = tuple(int(v) for v in np.cumsum(IN_WIDTHS)[:-1])


def rms_norm(x, gain):
    xf = x.astype(jnp.float32)
    y = xf * lax.rsqrt(jnp.mean(xf * xf, axis=-1, keepdims=True) + EPS)
    return (y * gain.astype(jnp.float32)).astype(x.dtype)

def swiglu_ffn(h, w_in, w_out):
    gate, up = jnp.split(h @ w_in, 2, axis=-1)
    return (jax.nn.silu(gate) * up) @ w_out

def apply_rope(x, cos, sin):
    x1, x2 = jnp.split(x, 2, axis=-1)
    return jnp.concatenate([x1 * cos - x2 * sin, x2 * cos + x1 * sin], axis=-1)

def gmlp_mixer(uv, v_gain, w_s, b_s):
    bsz, s, _ = uv.shape
    u, v = jnp.split(jax.nn.gelu(uv, approximate=False), 2, axis=-1)
    v = rms_norm(v, v_gain).reshape(bsz, s // GM_CHUNK, GM_CHUNK, GM_GROUPS, GM_GROUP_DIM)
    causal = jnp.tril(jnp.ones((GM_CHUNK, GM_CHUNK), dtype=bool))
    w = jnp.where(causal[None], w_s, 0.0).astype(v.dtype)
    sp = jnp.einsum('gts,bcsgd->bctgd', w, v) + b_s.T[:, :, None].astype(v.dtype)
    return u * sp.reshape(bsz, s, GM_WIDTH)

def blocked_causal_attention(q, k, v):
    bsz, s, nh, dqk = q.shape
    dv = v.shape[-1]
    nb = s // Q_BLOCK
    scale = dqk ** -0.5
    qb = q.reshape(bsz, nb, Q_BLOCK, nh, dqk).transpose(1, 0, 3, 2, 4)
    kt = k.transpose(0, 2, 1, 3)
    vt = v.transpose(0, 2, 1, 3)
    kpos = jnp.arange(s)

    def one_block(args):
        qi, i = args
        sc = jnp.einsum('bhqd,bhkd->bhqk', qi, kt, preferred_element_type=jnp.float32) * scale
        qpos = i * Q_BLOCK + jnp.arange(Q_BLOCK)
        sc = jnp.where(kpos[None, :] <= qpos[:, None], sc, -jnp.inf)
        p = jax.nn.softmax(sc, axis=-1).astype(vt.dtype)
        return jnp.einsum('bhqk,bhkd->bhqd', p, vt)

    out = lax.map(one_block, (qb, jnp.arange(nb)))
    return out.transpose(1, 0, 3, 2, 4).reshape(bsz, s, nh * dv)

def mla_mixer(c_q, c_kv, k_rope, cos, sin, q_norm, kv_norm, w_uq, w_ukv, q_gain, k_gain):
    bsz, s, _ = c_q.shape
    q = (rms_norm(c_q, q_norm) @ w_uq).reshape(bsz, s, MLA_HEADS, MLA_QK_DIM)
    kv = (rms_norm(c_kv, kv_norm) @ w_ukv).reshape(bsz, s, MLA_HEADS, MLA_NOPE + MLA_V)
    k_nope, v = jnp.split(kv, [MLA_NOPE], axis=-1)
    k_pe = jnp.broadcast_to(k_rope[:, :, None, :], (bsz, s, MLA_HEADS, MLA_ROPE))
    k = jnp.concatenate([k_nope, k_pe], axis=-1)
    q = rms_norm(q, q_gain)
    k = rms_norm(k, k_gain)
    q = jnp.concatenate([q[..., :MLA_NOPE], apply_rope(q[..., MLA_NOPE:], cos, sin)], axis=-1)
    k = jnp.concatenate([k[..., :MLA_NOPE], apply_rope(k[..., MLA_NOPE:], cos, sin)], axis=-1)
    return blocked_causal_attention(q, k, v)

def segsum(a):
    t = a.shape[-1]
    idx = jnp.arange(t)
    ax = jnp.where(idx[:, None] > idx[None, :], a[..., :, None], 0.0)
    ss = jnp.cumsum(ax, axis=-2)
    return jnp.where(idx[:, None] >= idx[None, :], ss, -jnp.inf)

def ssd_scan(xs, dt, a_log, b_in, c_in):
    bsz, s, nh, hp = xs.shape
    ng, ns = b_in.shape[2], b_in.shape[3]
    nr = nh // ng
    nc = s // SSD_CHUNK
    a = -jnp.exp(a_log.astype(jnp.float32))
    da = (dt * a).reshape(bsz, nc, SSD_CHUNK, ng, nr).transpose(0, 3, 4, 1, 2)
    xdt = (xs * dt[..., None].astype(xs.dtype)).reshape(bsz, nc, SSD_CHUNK, ng, nr, hp)
    bc = b_in.reshape(bsz, nc, SSD_CHUNK, ng, ns)
    cc = c_in.reshape(bsz, nc, SSD_CHUNK, ng, ns)
    cs = jnp.cumsum(da, axis=-1)
    dt_ = xs.dtype
    lmat = jnp.exp(segsum(da)).astype(dt_)
    cb = jnp.einsum('bclgn,bcsgn->bgcls', cc, bc)
    y_diag = jnp.einsum('bgrcls,bcsgrp->bclgrp', cb[:, :, None] * lmat, xdt)
    decay_states = jnp.exp(cs[..., -1:] - cs).astype(dt_)
    states = jnp.einsum('bclgn,bgrcl,bclgrp->bcgrpn', bc, decay_states, xdt)
    chunk_tot = jnp.pad(cs[..., -1], ((0, 0), (0, 0), (0, 0), (1, 0)))
    decay_chunk = jnp.exp(segsum(chunk_tot)).astype(dt_)
    states0 = jnp.concatenate([jnp.zeros_like(states[:, :1]), states], axis=1)
    new_states = jnp.einsum('bgrzc,bcgrpn->bzgrpn', decay_chunk, states0)
    states_in = new_states[:, :-1]
    y_off = jnp.einsum('bclgn,bcgrpn,bgrcl->bclgrp', cc, states_in, jnp.exp(cs).astype(dt_))
    return (y_diag + y_off).reshape(bsz, s, nh, hp)

def ssd_mixer(z, xbc, dt_raw, conv_w, conv_b, dt_bias, a_log, d_skip, norm_gain):
    bsz, s, _ = xbc.shape
    xbc = lax.conv_general_dilated(xbc, conv_w[:, None, :].astype(xbc.dtype), (1,), [(SSD_CONV - 1, 0)],
                                   dimension_numbers=('NWC', 'WIO', 'NWC'), feature_group_count=SSD_CONV_DIM)
    xbc = jax.nn.silu(xbc + conv_b.astype(xbc.dtype))
    xs, b_in, c_in = jnp.split(xbc, [SSD_INNER, SSD_INNER + SSD_GROUPS * SSD_STATE], axis=-1)
    xs = xs.reshape(bsz, s, SSD_HEADS, SSD_HEAD_DIM)
    b_in = b_in.reshape(bsz, s, SSD_GROUPS, SSD_STATE)
    c_in = c_in.reshape(bsz, s, SSD_GROUPS, SSD_STATE)
    dt = jax.nn.softplus(dt_raw.astype(jnp.float32) + dt_bias.astype(jnp.float32))
    y = ssd_scan(xs, dt, a_log, b_in, c_in) + xs * d_skip[:, None].astype(xs.dtype)
    y = y.reshape(bsz, s, SSD_INNER) * jax.nn.silu(z)
    y = rms_norm(y.reshape(bsz, s, SSD_GROUPS, SSD_INNER // SSD_GROUPS), norm_gain.reshape(SSD_GROUPS, -1))
    return y.reshape(bsz, s, SSD_INNER)

def first_inputs(seed: int = 0) -> dict:
    key = jax.random.key(seed)
    ks = jax.random.split(key, 32)
    f32 = jnp.float32

    def nrm(k, shape, scale):
        return jax.random.normal(k, shape, f32) * scale

    def gain(k, shape):
        return 1.0 + 0.05 * jax.random.normal(k, shape, f32)

    L = DEPTH
    x = jax.random.normal(ks[0], (BATCH, SEQ, D_MODEL), f32)
    offsets = jax.random.randint(ks[1], (BATCH, 1), 0, SEQ, dtype=jnp.int32)
    positions = offsets + jnp.arange(SEQ, dtype=jnp.int32)[None, :]
    dt0 = jnp.exp(jax.random.uniform(ks[2], (L, SSD_HEADS), f32, np.log(1e-3), np.log(1e-1)))
    return {
        'x': x,
        'positions': positions,
        'ffn1_norm': gain(ks[3], (L, D_MODEL)),
        'ffn1_w_in': nrm(ks[4], (L, D_MODEL, 2 * D_FF), D_MODEL ** -0.5),
        'ffn1_w_out': nrm(ks[5], (L, D_FF, D_MODEL), D_FF ** -0.5),
        'mix_norm': gain(ks[6], (L, D_MODEL)),
        'w_in': nrm(ks[7], (L, D_MODEL, IN_COLS), D_MODEL ** -0.5),
        'gm_v_norm': gain(ks[8], (L, GM_WIDTH)),
        'gm_w_s': nrm(ks[9], (L, GM_GROUPS, GM_CHUNK, GM_CHUNK), 0.5 * GM_CHUNK ** -0.5),
        'gm_b_s': 1.0 + 0.1 * jax.random.normal(ks[10], (L, GM_GROUPS, GM_CHUNK), f32),
        'mla_q_norm': gain(ks[11], (L, MLA_Q_RANK)),
        'mla_kv_norm': gain(ks[12], (L, MLA_KV_RANK)),
        'mla_w_uq': nrm(ks[13], (L, MLA_Q_RANK, MLA_HEADS * MLA_QK_DIM), MLA_Q_RANK ** -0.5),
        'mla_w_ukv': nrm(ks[14], (L, MLA_KV_RANK, MLA_HEADS * (MLA_NOPE + MLA_V)), MLA_KV_RANK ** -0.5),
        'mla_q_gain': gain(ks[15], (L, MLA_QK_DIM)),
        'mla_k_gain': gain(ks[16], (L, MLA_QK_DIM)),
        'ssd_conv_w': nrm(ks[17], (L, SSD_CONV, SSD_CONV_DIM), SSD_CONV ** -0.5),
        'ssd_conv_b': nrm(ks[18], (L, SSD_CONV_DIM), 0.02),
        'ssd_dt_bias': dt0 + jnp.log(-jnp.expm1(-dt0)),
        'ssd_a_log': jnp.log(jax.random.uniform(ks[19], (L, SSD_HEADS), f32, 1.0, 16.0)),
        'ssd_d': 1.0 + 0.1 * jax.random.normal(ks[20], (L, SSD_HEADS), f32),
        'ssd_norm': gain(ks[21], (L, SSD_INNER)),
        'w_branch': nrm(ks[22], (L, N_BRANCH, BRANCH_WIDTH, D_MODEL), BRANCH_WIDTH ** -0.5),
        'w_out': nrm(ks[23], (L, D_MODEL, D_MODEL), D_MODEL ** -0.5),
        'ffn2_norm': gain(ks[24], (L, D_MODEL)),
        'ffn2_w_in': nrm(ks[25], (L, D_MODEL, 2 * D_FF), D_MODEL ** -0.5),
        'ffn2_w_out': nrm(ks[26], (L, D_FF, D_MODEL), D_FF ** -0.5),
    }

def first_block(x, positions, ffn1_norm, ffn1_w_in, ffn1_w_out, mix_norm, w_in, gm_v_norm, gm_w_s, gm_b_s,
              mla_q_norm, mla_kv_norm, mla_w_uq, mla_w_ukv, mla_q_gain, mla_k_gain,
              ssd_conv_w, ssd_conv_b, ssd_dt_bias, ssd_a_log, ssd_d, ssd_norm,
              w_branch, w_out, ffn2_norm, ffn2_w_in, ffn2_w_out):
    bsz, s, _ = x.shape
    inv_freq = 1.0 / (ROPE_THETA ** (jnp.arange(0, MLA_ROPE, 2, dtype=jnp.float32) / MLA_ROPE))
    ang = positions.astype(jnp.float32)[..., None] * inv_freq
    cos = jnp.cos(ang)[:, :, None, :].astype(x.dtype)
    sin = jnp.sin(ang)[:, :, None, :].astype(x.dtype)
    for l in range(DEPTH):
        x = x + FFN_RESID * swiglu_ffn(rms_norm(x, ffn1_norm[l]), ffn1_w_in[l], ffn1_w_out[l])
        h = rms_norm(x, mix_norm[l])
        uv, c_q, c_kv, k_rope, z, xbc, dt_raw, gates = jnp.split(h @ w_in[l], IN_OFFSETS, axis=-1)
        y_a = gmlp_mixer(uv, gm_v_norm[l], gm_w_s[l], gm_b_s[l])
        y_b = mla_mixer(c_q, c_kv, k_rope, cos, sin, mla_q_norm[l], mla_kv_norm[l], mla_w_uq[l], mla_w_ukv[l],
                        mla_q_gain[l], mla_k_gain[l])
        y_c = ssd_mixer(z, xbc, dt_raw, ssd_conv_w[l], ssd_conv_b[l], ssd_dt_bias[l], ssd_a_log[l], ssd_d[l],
                        ssd_norm[l])
        g = jax.nn.sigmoid(gates).reshape(bsz, s, N_BRANCH, D_MODEL)
        merged = (g[:, :, 0] * (y_a @ w_branch[l, 0])
                  + g[:, :, 1] * (y_b @ w_branch[l, 1])
                  + g[:, :, 2] * (y_c @ w_branch[l, 2]))
        x = x + merged @ w_out[l]
        x = x + FFN_RESID * swiglu_ffn(rms_norm(x, ffn2_norm[l]), ffn2_w_in[l], ffn2_w_out[l])
    return x


DEPTH_2 = 1

N_MEM = 256
D_MIX = D_MODEL
DN_HEADS = 4
DN_HEAD_DIM = 128
DN_WIDTH = DN_HEADS * DN_HEAD_DIM
CONV_WIDTH = 4
CHUNK = 64
S5_WIDTH = D_MIX - DN_WIDTH
S5_CH_PER_GROUP = 16
S5_GROUPS = S5_WIDTH // S5_CH_PER_GROUP
S5_STATE = 64
X_HEADS = 4
X_HEAD_DIM = D_MODEL // X_HEADS
D_FF_2 = -(-8 * D_MODEL // (3 * 256)) * 256

OFF_Q = 0
OFF_K = OFF_Q + DN_WIDTH
OFF_V = OFF_K + DN_WIDTH
OFF_Z = OFF_V + DN_WIDTH
OFF_A = OFF_Z + DN_WIDTH
OFF_B = OFF_A + DN_HEADS
OFF_U = OFF_B + DN_HEADS
D_IN = OFF_U + S5_WIDTH


def _rmsnorm(x, gain):
    x32 = x.astype(jnp.float32)
    y = x32 * lax.rsqrt(jnp.mean(x32 * x32, axis=-1, keepdims=True) + EPS)
    return (y * gain.astype(jnp.float32)).astype(x.dtype)

def _l2norm(x):
    return x * lax.rsqrt(jnp.sum(x * x, axis=-1, keepdims=True) + EPS)

def _causal_dwconv(x, w):
    c = x.shape[-1]
    return lax.conv_general_dilated(
        x, w.astype(x.dtype)[:, None, :], window_strides=(1,),
        padding=((CONV_WIDTH - 1, 0),),
        dimension_numbers=("NWC", "WIO", "NWC"), feature_group_count=c)

def _gated_delta_rule(q, k, v, g, beta):
    bsz, t, h, dk = q.shape
    dv = v.shape[-1]
    n = t // CHUNK

    def chunk(a):
        a = a.reshape((bsz, n, CHUNK, h) + a.shape[3:])
        return jnp.moveaxis(a, 3, 2)

    q, k, v, g, beta = chunk(q), chunk(k), chunk(v), chunk(g), chunk(beta)
    g_cum = jnp.cumsum(g, axis=-1)
    causal = jnp.tril(jnp.ones((CHUNK, CHUNK), dtype=bool))
    strict = jnp.tril(jnp.ones((CHUNK, CHUNK), dtype=bool), k=-1)
    decay = jnp.exp(jnp.where(causal, g_cum[..., :, None] - g_cum[..., None, :], -jnp.inf))

    kb = k * beta[..., None]
    lower = jnp.where(strict, jnp.einsum("bnhcd,bnhsd->bnhcs", kb, k) * decay, 0.0)
    tmat = jnp.eye(CHUNK, dtype=jnp.float32) + lower
    rhs = jnp.concatenate([v * beta[..., None], kb * jnp.exp(g_cum)[..., None]], axis=-1)
    sol = lax.linalg.triangular_solve(tmat, rhs, left_side=True, lower=True)
    u, w = sol[..., :dv], sol[..., dv:]

    attn = jnp.where(causal, jnp.einsum("bnhcd,bnhsd->bnhcs", q, k) * decay, 0.0)
    qg = q * jnp.exp(g_cum)[..., None]
    g_last = g_cum[..., -1]
    k_dec = k * jnp.exp(g_last[..., None] - g_cum)[..., None]
    a_last = jnp.exp(g_last)

    def step(s, inp):
        qg_c, kd_c, u_c, w_c, at_c, al_c = inp
        v_new = u_c - jnp.einsum("bhck,bhkv->bhcv", w_c, s)
        o_c = jnp.einsum("bhck,bhkv->bhcv", qg_c, s) + jnp.einsum("bhcs,bhsv->bhcv", at_c, v_new)
        s = s * al_c[..., None, None] + jnp.einsum("bhck,bhcv->bhkv", kd_c, v_new)
        return s, o_c

    xs = tuple(jnp.moveaxis(a, 1, 0) for a in (qg, k_dec, u, w, attn, a_last))
    s0 = jnp.zeros((bsz, h, dk, dv), jnp.float32)
    _, o = lax.scan(step, s0, xs)
    o = jnp.transpose(o, (1, 0, 3, 2, 4))
    return o.reshape(bsz, t, h, dv)

def _s5(u, a_re, a_im, b_re, b_im, c_re, c_im, d, log_dt):
    f = jnp.float32
    u = u.astype(f)
    a_re, a_im = a_re.astype(f), a_im.astype(f)
    b_re, b_im = b_re.astype(f), b_im.astype(f)
    dt = jnp.exp(log_dt.astype(f))[:, None]
    mag = jnp.exp(a_re * dt)
    ab_re, ab_im = mag * jnp.cos(a_im * dt), mag * jnp.sin(a_im * dt)
    den = a_re * a_re + a_im * a_im
    nr, ni = ab_re - 1.0, ab_im
    co_re = (nr * a_re + ni * a_im) / den
    co_im = (ni * a_re - nr * a_im) / den
    bb_re = co_re[..., None] * b_re - co_im[..., None] * b_im
    bb_im = co_re[..., None] * b_im + co_im[..., None] * b_re
    bu_re = jnp.einsum("btgc,gpc->tbgp", u, bb_re)
    bu_im = jnp.einsum("btgc,gpc->tbgp", u, bb_im)
    t = u.shape[1]
    la_re = jnp.broadcast_to(ab_re, (t, 1) + ab_re.shape)
    la_im = jnp.broadcast_to(ab_im, (t, 1) + ab_im.shape)

    def combine(e1, e2):
        a1r, a1i, b1r, b1i = e1
        a2r, a2i, b2r, b2i = e2
        return (a1r * a2r - a1i * a2i,
                a1r * a2i + a1i * a2r,
                a2r * b1r - a2i * b1i + b2r,
                a2r * b1i + a2i * b1r + b2i)

    _, _, x_re, x_im = lax.associative_scan(combine, (la_re, la_im, bu_re, bu_im), axis=0)
    y = (jnp.einsum("tbgp,gcp->btgc", x_re, c_re.astype(f))
         - jnp.einsum("tbgp,gcp->btgc", x_im, c_im.astype(f)))
    return y + d.astype(f) * u

def _mixer(xn, w_in, conv_w, dn_a_log, dn_dt_bias, dn_norm_g,
           s5_a_re, s5_a_im, s5_b_re, s5_b_im, s5_c_re, s5_c_im, s5_d, s5_log_dt,
           s5_w_glu, s5_b_glu, w_out):
    bsz, t, _ = xn.shape
    dt_ = xn.dtype
    proj = xn @ w_in

    qkv = jax.nn.silu(_causal_dwconv(proj[..., OFF_Q:OFF_Z], conv_w)).astype(jnp.float32)
    q = qkv[..., :DN_WIDTH].reshape(bsz, t, DN_HEADS, DN_HEAD_DIM)
    k = qkv[..., DN_WIDTH:2 * DN_WIDTH].reshape(bsz, t, DN_HEADS, DN_HEAD_DIM)
    v = qkv[..., 2 * DN_WIDTH:].reshape(bsz, t, DN_HEADS, DN_HEAD_DIM)
    q = _l2norm(q) * (DN_HEAD_DIM ** -0.5)
    k = _l2norm(k)
    z = proj[..., OFF_Z:OFF_A].astype(jnp.float32).reshape(bsz, t, DN_HEADS, DN_HEAD_DIM)
    a = proj[..., OFF_A:OFF_B].astype(jnp.float32)
    b = proj[..., OFF_B:OFF_U].astype(jnp.float32)
    g = -jnp.exp(dn_a_log.astype(jnp.float32)) * jax.nn.softplus(a + dn_dt_bias.astype(jnp.float32))
    beta = jax.nn.sigmoid(b)
    o = _gated_delta_rule(q, k, v, g, beta)
    o = o * lax.rsqrt(jnp.mean(o * o, axis=-1, keepdims=True) + EPS)
    o = o * dn_norm_g.astype(jnp.float32) * jax.nn.silu(z)
    o = o.reshape(bsz, t, DN_WIDTH).astype(dt_)

    u = proj[..., OFF_U:].reshape(bsz, t, S5_GROUPS, S5_CH_PER_GROUP)
    y = _s5(u, s5_a_re, s5_a_im, s5_b_re, s5_b_im, s5_c_re, s5_c_im, s5_d, s5_log_dt)
    y = jax.nn.gelu(y.reshape(bsz, t, S5_WIDTH)).astype(dt_)
    y = y * jax.nn.sigmoid(y @ s5_w_glu + s5_b_glu)

    return jnp.concatenate([o, y], axis=-1) @ w_out

def _cross_attn(hn, mem, norm_mem_g, w_xq, w_xk, w_xv, w_xo):
    bsz, t, _ = hn.shape
    mn = _rmsnorm(mem, norm_mem_g)
    q = (hn @ w_xq).reshape(bsz, t, X_HEADS, X_HEAD_DIM)
    k = (mn @ w_xk).reshape(bsz, N_MEM, X_HEADS, X_HEAD_DIM)
    v = (mn @ w_xv).reshape(bsz, N_MEM, X_HEADS, X_HEAD_DIM)
    s = jnp.einsum("bthd,bmhd->bhtm", q, k).astype(jnp.float32) * (X_HEAD_DIM ** -0.5)
    p = jax.nn.softmax(s, axis=-1).astype(hn.dtype)
    o = jnp.einsum("bhtm,bmhd->bthd", p, v).reshape(bsz, t, D_MODEL)
    return o @ w_xo

def _swiglu(hn, w_gate, w_up, w_down):
    return (jax.nn.silu(hn @ w_gate) * (hn @ w_up)) @ w_down

def second_inputs(seed: int = 0) -> dict:
    key = jax.random.key(seed)
    ks = iter(jax.random.split(key, 40))
    nrm = lambda shape, scale: jax.random.normal(next(ks), shape, jnp.float32) * scale
    unif = lambda shape, lo, hi: jax.random.uniform(next(ks), shape, jnp.float32, lo, hi)
    L = DEPTH_2
    x = nrm((BATCH, SEQ, D_MODEL), 1.0)
    mem = nrm((BATCH, N_MEM, D_MODEL), 1.0)
    gain = lambda n: 1.0 + nrm((L, n), 0.02)
    dt_dn = jnp.exp(unif((L, DN_HEADS), math.log(1e-3), math.log(1e-1)))
    n_idx = jnp.arange(S5_STATE, dtype=jnp.float32)
    return {
        "x": x,
        "mem": mem,
        "norm_mix_g": gain(D_MODEL),
        "w_in": nrm((L, D_MODEL, D_IN), D_MODEL ** -0.5),
        "conv_w": nrm((L, CONV_WIDTH, 3 * DN_WIDTH), CONV_WIDTH ** -0.5),
        "dn_a_log": jnp.log(unif((L, DN_HEADS), 1.0, 16.0)),
        "dn_dt_bias": dt_dn + jnp.log(-jnp.expm1(-dt_dn)),
        "dn_norm_g": gain(DN_HEAD_DIM),
        "s5_a_re": -0.5 + nrm((L, S5_GROUPS, S5_STATE), 0.01),
        "s5_a_im": math.pi * n_idx + nrm((L, S5_GROUPS, S5_STATE), 0.01),
        "s5_b_re": nrm((L, S5_GROUPS, S5_STATE, S5_CH_PER_GROUP), (2 * S5_CH_PER_GROUP) ** -0.5),
        "s5_b_im": nrm((L, S5_GROUPS, S5_STATE, S5_CH_PER_GROUP), (2 * S5_CH_PER_GROUP) ** -0.5),
        "s5_c_re": nrm((L, S5_GROUPS, S5_CH_PER_GROUP, S5_STATE), (2 * S5_STATE) ** -0.5),
        "s5_c_im": nrm((L, S5_GROUPS, S5_CH_PER_GROUP, S5_STATE), (2 * S5_STATE) ** -0.5),
        "s5_d": nrm((L, S5_GROUPS, S5_CH_PER_GROUP), 1.0),
        "s5_log_dt": unif((L, S5_GROUPS), math.log(1e-3), math.log(1e-1)),
        "s5_w_glu": nrm((L, S5_WIDTH, S5_WIDTH), S5_WIDTH ** -0.5),
        "s5_b_glu": nrm((L, S5_WIDTH), 0.01),
        "w_out": nrm((L, D_MIX, D_MODEL), D_MIX ** -0.5),
        "norm_x_g": gain(D_MODEL),
        "norm_mem_g": gain(D_MODEL),
        "w_xq": nrm((L, D_MODEL, D_MODEL), D_MODEL ** -0.5),
        "w_xk": nrm((L, D_MODEL, D_MODEL), D_MODEL ** -0.5),
        "w_xv": nrm((L, D_MODEL, D_MODEL), D_MODEL ** -0.5),
        "w_xo": nrm((L, D_MODEL, D_MODEL), D_MODEL ** -0.5),
        "norm_ffn_g": gain(D_MODEL),
        "w_gate": nrm((L, D_MODEL, D_FF_2), D_MODEL ** -0.5),
        "w_up": nrm((L, D_MODEL, D_FF_2), D_MODEL ** -0.5),
        "w_down": nrm((L, D_FF_2, D_MODEL), D_FF_2 ** -0.5),
        "norm_final_g": 1.0 + nrm((D_MODEL,), 0.02),
    }

def second_block(x, mem, norm_mix_g, w_in, conv_w, dn_a_log, dn_dt_bias, dn_norm_g,
              s5_a_re, s5_a_im, s5_b_re, s5_b_im, s5_c_re, s5_c_im, s5_d, s5_log_dt,
              s5_w_glu, s5_b_glu, w_out, norm_x_g, norm_mem_g, w_xq, w_xk, w_xv, w_xo,
              norm_ffn_g, w_gate, w_up, w_down, norm_final_g):
    h = x
    for l in range(DEPTH_2):
        h = h + _mixer(_rmsnorm(h, norm_mix_g[l]), w_in[l], conv_w[l], dn_a_log[l],
                       dn_dt_bias[l], dn_norm_g[l], s5_a_re[l], s5_a_im[l], s5_b_re[l],
                       s5_b_im[l], s5_c_re[l], s5_c_im[l], s5_d[l], s5_log_dt[l],
                       s5_w_glu[l], s5_b_glu[l], w_out[l])
        h = h + _cross_attn(_rmsnorm(h, norm_x_g[l]), mem, norm_mem_g[l],
                            w_xq[l], w_xk[l], w_xv[l], w_xo[l])
        h = h + _swiglu(_rmsnorm(h, norm_ffn_g[l]), w_gate[l], w_up[l], w_down[l])
    return _rmsnorm(h, norm_final_g)


def setup_inputs(seed=0):
    out = dict(first_inputs(seed))
    for name, value in second_inputs(seed + 1).items():
        if name != "x":
            out[name + "_2"] = value
    return out


def reference(
    x, positions, ffn1_norm, ffn1_w_in, ffn1_w_out, mix_norm, w_in, gm_v_norm, gm_w_s, gm_b_s,
    mla_q_norm, mla_kv_norm, mla_w_uq, mla_w_ukv, mla_q_gain, mla_k_gain, ssd_conv_w,
    ssd_conv_b, ssd_dt_bias, ssd_a_log, ssd_d, ssd_norm, w_branch, w_out, ffn2_norm, ffn2_w_in,
    ffn2_w_out, mem_2, norm_mix_g_2, w_in_2, conv_w_2, dn_a_log_2, dn_dt_bias_2, dn_norm_g_2,
    s5_a_re_2, s5_a_im_2, s5_b_re_2, s5_b_im_2, s5_c_re_2, s5_c_im_2, s5_d_2, s5_log_dt_2,
    s5_w_glu_2, s5_b_glu_2, w_out_2, norm_x_g_2, norm_mem_g_2, w_xq_2, w_xk_2, w_xv_2, w_xo_2,
    norm_ffn_g_2, w_gate_2, w_up_2, w_down_2, norm_final_g_2,
):
    x = first_block(
        x, positions, ffn1_norm, ffn1_w_in, ffn1_w_out, mix_norm, w_in, gm_v_norm, gm_w_s,
        gm_b_s, mla_q_norm, mla_kv_norm, mla_w_uq, mla_w_ukv, mla_q_gain, mla_k_gain,
        ssd_conv_w, ssd_conv_b, ssd_dt_bias, ssd_a_log, ssd_d, ssd_norm, w_branch, w_out,
        ffn2_norm, ffn2_w_in, ffn2_w_out,
    )
    return second_block(
        x, mem_2, norm_mix_g_2, w_in_2, conv_w_2, dn_a_log_2, dn_dt_bias_2, dn_norm_g_2,
        s5_a_re_2, s5_a_im_2, s5_b_re_2, s5_b_im_2, s5_c_re_2, s5_c_im_2, s5_d_2, s5_log_dt_2,
        s5_w_glu_2, s5_b_glu_2, w_out_2, norm_x_g_2, norm_mem_g_2, w_xq_2, w_xk_2, w_xv_2,
        w_xo_2, norm_ffn_g_2, w_gate_2, w_up_2, w_down_2, norm_final_g_2,
    )


_drawn_inputs = setup_inputs


def setup_inputs(seed=0):
    import zlib

    import numpy as np

    out = dict(_drawn_inputs(seed))
    spreads = {}
    factors = {'gm_v_norm': 7.163,
     'mla_q_norm': 8.0,
     'mla_kv_norm': 5.54,
     'mla_q_gain': 8.0,
     'mla_k_gain': 8.0,
     'ssd_conv_b': 2.825,
     'norm_mix_g_2': 5.725,
     'dn_norm_g_2': 8.0,
     's5_a_re_2': 64.0,
     's5_a_im_2': 48.664,
     's5_b_re_2': 64.0,
     's5_b_im_2': 64.0,
     's5_c_re_2': 64.0,
     's5_c_im_2': 64.0,
     's5_log_dt_2': 50.08,
     's5_b_glu_2': 64.0,
     'norm_x_g_2': 8.0,
     'norm_mem_g_2': 8.0,
     'norm_ffn_g_2': 16.153,
     'norm_final_g_2': 7.766}
    for name, (base, spread) in spreads.items():
        noise = np.random.default_rng([zlib.crc32(name.encode()), seed]).standard_normal(out[name].shape)
        drawn = base * np.exp(spread * noise) if base else spread * noise
        out[name] = __import__('jax').numpy.asarray(drawn.astype(out[name].dtype))
    for name, factor in factors.items():
        out[name] = (out[name] * factor).astype(out[name].dtype)
    return out
```

```python
import math
from contextlib import ExitStack

import numpy as np

import concourse.bass as bass
from concourse import mybir

F32 = mybir.dt.float32
F32R = mybir.dt.float32r
I32 = mybir.dt.int32
ALU = mybir.AluOpType
ACT = mybir.ActivationFunctionType
AX = mybir.AxisListType.X

P = 128
TOK = 256
MT = TOK // P
D = 1024
KD = D // P
FF = 2816
FB = 256
NFB = FF // FB
KF = FF // P
DEPTH = 2
EPS = 1e-6
RING = 4
SLOT = 2080
N_CHUNK_FFN = 2 * NFB + KF // 2
N_GROUP_FFN = NFB + 2

INPUTS = [
    "x", "positions", "ffn1_norm", "ffn1_w_in", "ffn1_w_out", "mix_norm", "w_in", "gm_v_norm", "gm_w_s", "gm_b_s",
    "mla_q_norm", "mla_kv_norm", "mla_w_uq", "mla_w_ukv", "mla_q_gain", "mla_k_gain", "ssd_conv_w",
    "ssd_conv_b", "ssd_dt_bias", "ssd_a_log", "ssd_d", "ssd_norm", "w_branch", "w_out", "ffn2_norm", "ffn2_w_in",
    "ffn2_w_out", "mem_2", "norm_mix_g_2", "w_in_2", "conv_w_2", "dn_a_log_2", "dn_dt_bias_2", "dn_norm_g_2",
    "s5_a_re_2", "s5_a_im_2", "s5_b_re_2", "s5_b_im_2", "s5_c_re_2", "s5_c_im_2", "s5_d_2", "s5_log_dt_2",
    "s5_w_glu_2", "s5_b_glu_2", "w_out_2", "norm_x_g_2", "norm_mem_g_2", "w_xq_2", "w_xk_2", "w_xv_2", "w_xo_2",
    "norm_ffn_g_2", "w_gate_2", "w_up_2", "w_down_2", "norm_final_g_2",
]


class Counters:

    def __init__(self, act=None, vec=None, pe=None, pool=None, silu=None, turned=None, hT=None, hT_lo=None,
                 hi=None, lo=None):
        self.act, self.vec, self.pe, self.pool = act, vec, pe, pool
        self.silu, self.turned, self.hT, self.hT_lo, self.hi, self.lo = silu, turned, hT, hT_lo, hi, lo


def bank(G, m):
    return 2 * (G % 2) + m


def build(nc, t, out):
    with ExitStack() as ctx:
        def sb(name, shape, dt=F32):
            return ctx.enter_context(nc.sbuf_tensor(name, shape, dt))

        all_sems = []

        def sem(name):
            s = ctx.enter_context(nc.semaphore(name))
            all_sems.append(s)
            return s

        def steps(name, engines="act vec pe"):
            return Counters(**{e: sem(f"{name}_{e}_steps") for e in engines.split()})

        acc = [ctx.enter_context(nc.psum_tensor(f"acc{i}", [P, 512], F32)) for i in range(4)]
        turn = [ctx.enter_context(nc.psum_tensor(f"turn{i}", [P, 512], F32)) for i in range(4)]

        ring = sb("ring", [P, RING, SLOT])
        x = sb("x", [P, MT, D])
        xn = sb("xn", [P, MT, D])
        xT = sb("xT", [P, KD, TOK])
        junk = sb("junk", [P, 512])
        stat = sb("stat", [P, 64])
        ident = sb("ident", [P, P])
        ones = sb("ones", [P, P])
        upper = sb("upper", [P, P])
        causal = sb("causal", [P, TOK])
        eps_col = sb("eps_col", [P, 1])
        cos = sb("cos", [P, MT, 16])
        sin = sb("sin", [P, MT, 16])
        big_at = nc.sbuf_base
        BIG = sb("big", [P, 34392])

        def big(off, *shape):
            n = int(np.prod(shape))
            assert off + n <= 34392
            v = BIG[:, off:off + n]
            if len(shape) == 1:
                return v
            names = "abcd"[:len(shape)]
            return v.rearrange("p (" + " ".join(names) + ") -> p " + " ".join(names),
                               **dict(zip(names, shape)))

        def over_big(name, off, *shape):
            assert off + int(np.prod(shape)) <= 34392
            return nc.alloc_sbuf_tensor_at(name, [P] + list(shape), F32R, offset=big_at + 4 * off)

        hT_hi = over_big("hT_hi", 0, KF, TOK)
        hT_lo = over_big("hT_lo", 7680, KF, TOK)
        xT_hi = over_big("xT_hi", 13312, KD, TOK)
        xT_lo = over_big("xT_lo", 15360, KD, TOK)
        w_hi = over_big("w_hi", 17408, RING * 2048)
        w_lo = over_big("w_lo", 25600, RING * 2048)
        gate_s = big(5632, 2, MT, FB)
        h_s = big(6656, 2, MT, FB)

        landed = [sem(f"chunk_landed{i}") for i in range(RING)]
        products_done = sem("products_done")
        acc_read = [sem(f"acc_read{i}") for i in range(4)]
        const_in = sem("const_in")

        def slot(c, k, n):
            return ring[:, c % RING, 0:k * n].rearrange("p (k n) -> p k n", k=k)

        def load(sync, c, src, k, n, turns=0):
            sync.wait_ge(products_done, c + 1 + RING * turns)
            sync.dma_start(slot(c, k, n), src).then_inc(landed[c % RING], 16)

        def wait_chunk(pe, c, turns=0):
            pe.wait_ge(landed[c % RING], 16 * (c // RING + 1 + turns))

        def wait_products(eng, c, turns=0):
            eng.wait_ge(products_done, RING + c + 1 + RING * turns)

        def wait_acc_free(pe, G, m, turns=0):
            pe.wait_ge(acc_read[bank(G, m)], G // 2 + 1 + turns)

        def wait_acc_read(eng, G, m, turns=0):
            eng.wait_ge(acc_read[bank(G, m)], G // 2 + 2 + turns)

        def group_pe(pe, G, c, aT, ks, n, n_used=None):
            k0, K, nu = 0, sum(ks), n_used or n
            for i, kc in enumerate(ks):
                wait_chunk(pe, c + i)
                w = slot(c + i, kc, n)
                for m in range(MT):
                    if i == 0:
                        wait_acc_free(pe, G, m)
                    for k in range(kc):
                        ins = pe.matmul(acc[bank(G, m)][:, 0:nu], aT[:, k0 + k, m * P:(m + 1) * P], w[:, k, 0:nu],
                                        start=(k0 + k == 0), stop=(k0 + k == K - 1))
                ins.then_inc(products_done, 1)
                k0 += kc

        def turned_group_pe(pe, G, c, aT, n_tiles, n, K=KD):
            kc = K // 2 if K == KD else K
            nch = K // kc
            for i in range(nch):
                wait_chunk(pe, c + i)
            for f in range(n_tiles):
                q = f // 2
                if f % 2 == 0:
                    wait_acc_free(pe, G, q)
                for k in range(K):
                    w = slot(c + k // kc, kc, n)
                    ins = pe.matmul(acc[bank(G, q)][:, (f % 2) * TOK:(f % 2) * TOK + TOK],
                                    w[:, k % kc, f * P:(f + 1) * P], aT[:, k, :],
                                    start=(k == 0), stop=(k == K - 1))
                    if f == n_tiles - 1 and k % kc == kc - 1:
                        ins.then_inc(products_done, 1)

        def norm_act(act, s, src=x, wait_src=None, width=D):
            if wait_src:
                wait_src(act)
            for m in range(MT):
                act.activation(xn[:, m, 0:width], src[:, m, :], ACT.Square,
                               accum_out=stat[:, m:m + 1]).then_inc(s.act, 1)
                act.wait_ge(s.act, m + 1)
            act.activation(stat[:, 2:4], stat[:, 0:2], ACT.Sqrt, bias=eps_col[:, 0:1],
                           scale=1.0 / width).then_inc(s.act, 1)

        def norm_vec(vec, s, gain, src=x, nb=xn, dst=xT):
            vec.wait_ge(s.act, 3)
            vec.reciprocal(stat[:, 4:6], stat[:, 2:4]).then_inc(s.vec, 1)
            vec.wait_ge(s.vec, 1)
            for m in range(MT):
                vec.tensor_scalar(nb[:, m, :], src[:, m, :], stat[:, 4 + m:5 + m], None, ALU.mult).then_inc(s.vec, 1)
            for b in range(4):
                m, hf = b // 2, b % 2
                vec.wait_ge(s.pe, b + 1)
                vec.tensor_tensor(dst[:, 4 * hf:4 * hf + 4, m * P:(m + 1) * P],
                                  turn[b][:, :].rearrange("p (k n) -> p k n", k=4),
                                  gain.unsqueeze(2).broadcast_to([P, KD, P])[:, 4 * hf:4 * hf + 4, :],
                                  ALU.mult).then_inc(s.vec, 1)

        def norm_pe(pe, s, nb=xn):
            for b in range(4):
                m, hf = b // 2, b % 2
                pe.wait_ge(s.vec, 2 + m)
                for k in range(4):
                    ins = pe.transpose(turn[b][:, k * P:(k + 1) * P],
                                       nb[:, m, (4 * hf + k) * P:(4 * hf + k + 1) * P], ident[:, :])
                ins.then_inc(s.pe, 1)

        NORM_DONE = 7

        def quarter(a, b):
            m, hf = b // 2, b % 2
            return a[:, 4 * hf:4 * hf + 4, m * P:(m + 1) * P]

        def split_x_act(act, s):
            for b in range(4):
                act.wait_ge(s.vec, 4 + b)
                act.activation(quarter(xT_hi, b), quarter(xT, b), ACT.Copy).then_inc(s.act, 1)

        def split_x_vec(vec, s):
            for b in range(4):
                vec.wait_ge(s.act, 4 + b)
                vec.tensor_tensor(quarter(xT_lo, b), quarter(xT, b), quarter(xT_hi, b).bitcast(F32),
                                  ALU.subtract).then_inc(s.vec, 1)

        SPLIT_DONE = 11

        def ffn_sems(name):
            return Counters(silu=sem(name + "_silu_done"), turned=sem(name + "_h_turned"), hT=sem(name + "_hT_hi_ready"),
                            hT_lo=sem(name + "_hT_lo_ready"), hi=sem(name + "_w_hi_ready"), lo=sem(name + "_w_lo_ready"))

        PAIRS = NFB // 2
        N_IN = 2 * NFB

        def w_part(w, r):
            if r < N_IN:
                pair = w[:, (r // 2 % 2) * 4096:(r // 2 % 2 + 1) * 4096].rearrange("p (k n) -> p k n", k=KD)
                return pair[:, :, (r % 2) * FB:(r % 2 + 1) * FB]
            return w[:, (r % RING) * 2048:(r % RING + 1) * 2048].rearrange("p (k n) -> p k n", k=2)

        def raw_part(c0, r):
            return slot(c0 + r, KD, FB) if r < N_IN else slot(c0 + r, 2, D)

        def ffn_sync(sync, f, c0, w_gate, w_up, w_down):
            def chunk(r, src, i=0):
                sync.wait_ge(f.lo, r + 1 + RING * i)
                sync.dma_start(raw_part(c0, r), src).then_inc(landed[(c0 + r) % RING], 16)

            sync.sem_inc(f.lo, RING)
            if c0 > 0:
                wait_products(sync, c0 - 1)
            with sync.Fori(0, PAIRS) as i:
                for jj in range(2):
                    chunk(2 * jj, w_gate(jj + 2 * i), i)
                    chunk(2 * jj + 1, w_up(jj + 2 * i), i)
            chunk(N_IN - 2, w_gate(NFB - 1))
            chunk(N_IN - 1, w_up(NFB - 1))
            for i in range(KF // 2):
                chunk(N_IN + i, w_down(i))

        def split_act(act, f, c0, r, i=0):
            wait_chunk(act, c0 + r, i)
            act.wait_ge(products_done, c0 + r + 1 + RING * i)
            act.activation(w_part(w_hi, r), raw_part(c0, r), ACT.Copy).then_inc(f.hi, 1)

        def split_vec(vec, f, c0, r, i=0):
            vec.wait_ge(f.hi, r + 1 + RING * i)
            vec.tensor_tensor(w_part(w_lo, r), raw_part(c0, r), w_part(w_hi, r).bitcast(F32), ALU.subtract).then_inc(f.lo, 1)

        def three(pe, o, a_hi, a_lo, wh, wl, start, stop):
            pe.matmul(o, a_hi, wh, start=start, stop=False)
            pe.matmul(o, a_hi, wl, start=False, stop=False)
            return pe.matmul(o, a_lo, wh, start=False, stop=stop)

        def ffn_pe(pe, f, n, c0, G0):
            def block(jj, i=0):
                G, p = G0 + jj, jj % 2
                wh = w_hi[:, p * 4096:(p + 1) * 4096].rearrange("p (k n) -> p k n", k=KD)
                wl = w_lo[:, p * 4096:(p + 1) * 4096].rearrange("p (k n) -> p k n", k=KD)
                pe.wait_ge(f.lo, RING + 2 * jj + 2 + RING * i)
                for m in range(MT):
                    wait_acc_free(pe, G, m, i)
                    for k in range(KD):
                        ms = slice(m * P, (m + 1) * P)
                        ins = three(pe, acc[bank(G, m)][:, :], xT_hi[:, k, ms], xT_lo[:, k, ms], wh[:, k, :], wl[:, k, :],
                                    k == 0, k == KD - 1)
                    if m == 1:
                        ins.then_inc(products_done, 2)

            def turn_block(jj, i=0):
                wait_acc_read(pe, G0 + jj, 1, i)
                pe.wait_ge(f.hT_lo, jj + 1 + 2 * i)
                for k in range(2):
                    for m in range(MT):
                        ins = pe.transpose(turn[jj % 2][:, k * TOK + m * P:k * TOK + (m + 1) * P],
                                           h_s[:, jj % 2, m, k * P:(k + 1) * P], ident[:, :])
                ins.then_inc(f.turned, 1)

            pe.sem_inc(f.hT_lo, 2)
            pe.wait_ge(n.vec, SPLIT_DONE)
            with pe.Fori(0, PAIRS) as i:
                block(0, i)
                block(1, i)
                turn_block(0, i)
                turn_block(1, i)
            block(NFB - 1)
            turn_block(NFB - 1)
            pe.wait_ge(f.hT_lo, 2 + NFB)
            for i in range(KF // 2):
                r = N_IN + i
                pe.wait_ge(f.lo, RING + r + 1)
                for m in range(MT):
                    for k in range(2):
                        ms = slice(m * P, (m + 1) * P)
                        for hf in range(2):
                            G = G0 + NFB + hf
                            if i == 0 and k == 0:
                                wait_acc_free(pe, G, m)
                            ns = slice(hf * 512, (hf + 1) * 512)
                            ins = three(pe, acc[bank(G, m)][:, :], hT_hi[:, 2 * i + k, ms], hT_lo[:, 2 * i + k, ms],
                                        w_part(w_hi, r)[:, k, ns], w_part(w_lo, r)[:, k, ns],
                                        i == 0 and k == 0, i == KF // 2 - 1 and k == 1)
                ins.then_inc(products_done, 1)

        def ffn_act(act, f, c0, G0):
            def split(jj, i=0):
                split_act(act, f, c0, 2 * jj, i)
                split_act(act, f, c0, 2 * jj + 1, i)

            def silu(jj, i=0):
                wait_products(act, c0 + 2 * jj + 1, i)
                for m in range(MT):
                    act.activation(gate_s[:, jj % 2, m, :], acc[bank(G0 + jj, m)][:, 0:FB], ACT.Silu).then_inc(f.silu, 1)

            def copy_hT(jj, i=0):
                act.wait_ge(f.turned, jj + 1 + 2 * i)
                act.activation(hT_hi[:, bass.ds(2 * jj + 4 * i, 2), :],
                               turn[jj % 2][:, :].rearrange("p (k n) -> p k n", k=2), ACT.Copy).then_inc(f.hT, 1)

            split(0)
            with act.Fori(0, PAIRS) as i:
                split(1, i)
                silu(0, i)
                split(2, i)
                silu(1, i)
                copy_hT(0, i)
                copy_hT(1, i)
            split_act(act, f, c0, N_IN)
            split_act(act, f, c0, N_IN + 1)
            silu(NFB - 1)
            copy_hT(NFB - 1)
            for r in range(N_IN + 2, N_IN + KF // 2):
                split_act(act, f, c0, r)

        def ffn_vec(vec, f, c0, G0, factor):
            def split(jj, i=0):
                split_vec(vec, f, c0, 2 * jj, i)
                split_vec(vec, f, c0, 2 * jj + 1, i)

            def hidden(jj, i=0):
                for m in range(MT):
                    vec.wait_ge(f.silu, 2 * jj + m + 1 + 4 * i)
                    vec.tensor_tensor(h_s[:, jj % 2, m, :], gate_s[:, jj % 2, m, :],
                                      acc[bank(G0 + jj, m)][:, FB:2 * FB], ALU.mult).then_inc(acc_read[bank(G0 + jj, m)], 1)

            def rest_hT(jj, i=0):
                vec.wait_ge(f.hT, jj + 1 + 2 * i)
                part = bass.ds(2 * jj + 4 * i, 2)
                vec.tensor_tensor(hT_lo[:, part, :], turn[jj % 2][:, :].rearrange("p (k n) -> p k n", k=2),
                                  hT_hi[:, part, :].bitcast(F32), ALU.subtract).then_inc(f.hT_lo, 1)

            split(0)
            with vec.Fori(0, PAIRS) as i:
                split(1, i)
                hidden(0, i)
                split(2, i)
                hidden(1, i)
                rest_hT(0, i)
                rest_hT(1, i)
            split_vec(vec, f, c0, N_IN)
            split_vec(vec, f, c0, N_IN + 1)
            hidden(NFB - 1)
            rest_hT(NFB - 1)
            for r in range(N_IN + 2, N_IN + KF // 2):
                split_vec(vec, f, c0, r)
            add_to_x(vec, c0 + N_CHUNK_FFN - 1, G0 + NFB, factor)

        def add_to_x(vec, c_last, G, factor):
            wait_products(vec, c_last)
            for hf in range(2):
                for m in range(MT):
                    xs = x[:, m, hf * 512:(hf + 1) * 512]
                    vec.scalar_tensor_tensor(out=xs, in0=acc[bank(G + hf, m)][:, :], scalar=factor, in1=xs,
                                             op0=ALU.mult, op1=ALU.add).then_inc(acc_read[bank(G + hf, m)], 1)

        def wait_x(eng, G):
            for hf in range(2):
                for m in range(MT):
                    wait_acc_read(eng, G + hf, m)

        H, NOPE, ROPE, QKD, VD = 8, 64, 32, 96, 64
        QR, KVR = 384, 256
        SCALE = QKD ** -0.5
        C_MIX, G_MIX = N_CHUNK_FFN, N_GROUP_FFN
        (G_U, C_U), (G_V, C_V), (G_CQ, C_CQ), (G_KV, C_KV), (G_XBC0, C_XBC0), (G_XBC1, C_XBC1), (G_Z, C_Z) = [
            (G_MIX + i, C_MIX + 2 * i) for i in range(7)]
        G_UQ, C_UQ = G_MIX + 7, C_MIX + 14
        G_UKV, C_UKV = G_UQ + 2, C_UQ + 2
        G_GATE, C_GATE = G_UKV + 2, C_UKV + 1
        G_BR, C_BR = G_GATE + 6, C_GATE + 12
        BRANCHES = (0, 2, 1)
        G_WO, C_WO = G_BR + 6, C_BR + 6
        G_FFN2, C_FFN2 = G_WO + 2, C_WO + 4
        COLS = dict(u=0, v=512, cq=1024, ckv=1408, z=1696, xbc0=2208, xbc1=2720, gate=3240)

        R = dict(ffn1=0, mix=8, ffn2=16, qn=24, kvn=27, ssdn=29, convb=33, gmb=41, convw=45)
        N_ROWS = 77
        vecs = sb("vecs", [P, P])
        col = sb("col", [P, P])
        ws_in = sb("ws_in", [P, 4, P])
        wsT = sb("wsT", [P, 4, P])
        gmv = sb("gmv", [P, 512])
        qk_gain = sb("qk_gain", [P, 2, QKD])
        small = sb("small", [P, 24])
        neg_a = sb("neg_a", [P, 8])

        gates = big(0, MT, 3 * D)
        u_s = big(6144, MT, 512)
        v_s = big(7168, MT, 512)
        cqn = big(8192, MT, QR)
        ckvn = big(8960, MT, KVR)
        cqT = big(9472, 3, TOK)
        ckvT = big(10240, 2, TOK)
        sc0 = big(6144, H, P)
        sc1 = big(7168, H, TOK)
        kpe = big(10752, MT, ROPE)
        qk = big(10816, MT, 2 * H, QKD)
        PT0 = big(10816, H, P)
        PT1 = big(11840, 2, H, P)
        vtok = big(13888, MT, H, VD)
        qT = big(14912, H, TOK)
        kT = big(16960, H, TOK)
        Ld = big(19008, 2 * H, P)
        sq = big(21056, 2 * H * QKD)
        rope_t = big(21056, MT, 4, 2 * H, 16)
        br_t = big(21056, 2, MT, 512)
        xpad = big(23104, 8, TOK + 3)
        conv = big(25176, 8, TOK)
        xs_tok = big(23104, MT, 512)
        B_tok = big(24128, MT, 2, P)
        S0 = big(24640, 512)
        cbm = big(27224, MT, 2, P)
        xdt = big(27736, MT, 512)
        xdtd = big(28760, 512)
        sz = big(29272, MT, 512)
        yc = big(30296, MT, 512)
        yT = big(31320, 3, 4, TOK)
        dtw = sb("dtw", [P, 12, 16])
        csv = sb("csv", [P, 40])
        att = sb("att", [P, 5, 16])
        dt_v, da = dtw[:, 10, :], dtw[:, 11, :]

        par_in = sem("params_in")
        par = steps("params")
        mix_norm = steps("mix_norm")
        gm, cq, xb, dts, sd, qs, br, mt = (steps(n) for n in
                                           ("gmlp", "latent", "conv", "dt", "ssd", "attn", "branch", "merged"))
        n1, n2 = steps("ffn1_norm"), steps("ffn2_norm")
        f1, f2 = ffn_sems("ffn1"), ffn_sems("ffn2")
        N_PAR = 0

        def lay(name, l):
            return t[name][bass.ds(l, 1)]

        def params_act(act, l):
            n = 0
            for name, r, k in (("ffn1_norm", "ffn1", 8), ("mix_norm", "mix", 8), ("ffn2_norm", "ffn2", 8),
                               ("mla_q_norm", "qn", 3), ("mla_kv_norm", "kvn", 2), ("ssd_norm", "ssdn", 4),
                               ("ssd_conv_b", "convb", 8)):
                act.dma_start(vecs[R[r]:R[r] + k, :], lay(name, l).rearrange("o (k p) -> (o k) p", p=P)).then_inc(par_in, 16)
                n += 1
            act.dma_start(vecs[R["gmb"]:R["gmb"] + 4, :], lay("gm_b_s", l).rearrange("o g t -> (o g) t")).then_inc(par_in, 16)
            act.dma_start(vecs[R["convw"]:R["convw"] + 32, :],
                          lay("ssd_conv_w", l).rearrange("o j (k p) -> (o j k) p", p=P)).then_inc(par_in, 16)
            act.dma_start(ws_in[:, :, :], lay("gm_w_s", l).rearrange("o g t s -> t (o g) s")).then_inc(par_in, 16)
            act.dma_start(gmv[:, :], lay("gm_v_norm", l).broadcast_to([P, 512])).then_inc(par_in, 16)
            act.dma_start(qk_gain[:, 0, :], lay("mla_q_gain", l).broadcast_to([P, QKD])).then_inc(par_in, 16)
            act.dma_start(qk_gain[:, 1, :], lay("mla_k_gain", l).broadcast_to([P, QKD])).then_inc(par_in, 16)
            act.dma_start(small[:, 0:8], lay("ssd_dt_bias", l).broadcast_to([P, 8])).then_inc(par_in, 16)
            act.dma_start(small[:, 8:16], lay("ssd_a_log", l).broadcast_to([P, 8])).then_inc(par_in, 16)
            act.dma_start(small[:, 16:24], lay("ssd_d", l).broadcast_to([P, 8])).then_inc(par_in, 16)
            act.wait_ge(par_in, 16 * (n + 9))
            act.activation(neg_a[:, :], small[:, 8:16], ACT.Exp).then_inc(par.act, 1)

        def params_pe(pe):
            pe.wait_ge(par.act, 1)
            pe.transpose(turn[0][:, 0:N_ROWS], vecs[0:N_ROWS, :], ident[0:N_ROWS, 0:N_ROWS]).then_inc(par.pe, 1)
            for g in range(4):
                ins = pe.transpose(turn[1][:, g * P:(g + 1) * P], ws_in[:, g, :], ident[:, :])
            ins.then_inc(par.pe, 1)

        def params_vec(vec):
            vec.wait_ge(par.act, 1)
            vec.tensor_scalar(neg_a[:, :], neg_a[:, :], -1.0, None, ALU.mult).then_inc(par.vec, 1)
            vec.wait_ge(par.pe, 1)
            vec.tensor_copy(col[:, 0:N_ROWS], turn[0][:, 0:N_ROWS]).then_inc(par.vec, 1)
            vec.wait_ge(par.pe, 2)
            vec.tensor_tensor(wsT[:, :, :], turn[1][:, :].rearrange("p (g n) -> p g n", g=4),
                              upper[:, :].unsqueeze(1).broadcast_to([P, 4, P]), ALU.mult).then_inc(par.vec, 1)
            vec.wait_ge(par.vec, 3)

        def mixer_sync(sync, l):
            def w_in(c, name, n, kc=4):
                for i in range(2):
                    load(sync, c + i, lay("w_in", l)[:, i * 512:(i + 1) * 512, COLS[name]:COLS[name] + n]
                         .rearrange("o (k p) n -> p (o k) n", p=P), 4, n)
            w_in(C_U, "u", 512)
            w_in(C_V, "v", 512)
            w_in(C_CQ, "cq", QR)
            w_in(C_KV, "ckv", KVR + ROPE)
            w_in(C_XBC0, "xbc0", 512)
            w_in(C_XBC1, "xbc1", 520)
            w_in(C_Z, "z", 512)
            for i in range(2):
                load(sync, C_UQ + i, lay("mla_w_uq", l)[:, :, i * 384:(i + 1) * 384]
                     .rearrange("o (k p) n -> p (o k) n", p=P), 3, 384)
            load(sync, C_UKV, lay("mla_w_ukv", l).rearrange("o (k p) n -> p (o k) n", p=P), 2, D)
            for g in range(6):
                for i in range(2):
                    load(sync, C_GATE + 2 * g + i,
                         lay("w_in", l)[:, i * 512:(i + 1) * 512, COLS["gate"] + 512 * g:COLS["gate"] + 512 * (g + 1)]
                         .rearrange("o (k p) n -> p (o k) n", p=P), 4, 512)
            for j, b in enumerate(BRANCHES):
                for i in range(2):
                    load(sync, C_BR + 2 * j + i, lay("w_branch", l)[:, b, :, 512 * i:512 * (i + 1)]
                         .rearrange("o (k p) n -> p (o k) n", p=P), 4, 512)
            for n in range(2):
                for i in range(2):
                    load(sync, C_WO + 2 * n + i, lay("w_out", l)[:, i * 512:(i + 1) * 512, n * 512:(n + 1) * 512]
                         .rearrange("o (k p) n -> p (o k) n", p=P), 4, 512)

        def gm_act(act):
            for G, c, dst in ((G_U, C_U, u_s), (G_V, C_V, v_s)):
                wait_products(act, c + 1)
                for m in range(MT):
                    act.activation(dst[:, m, :], acc[bank(G, m)][:, :], ACT.Gelu).then_inc(acc_read[bank(G, m)], 1)
            for m in range(MT):
                wait_acc_read(act, G_V, m)
                act.activation(junk[:, 0:512], v_s[:, m, :], ACT.Square, accum_out=stat[:, 8 + m:9 + m]).then_inc(gm.act, 1)
                act.wait_ge(gm.act, m + 1)
            act.activation(stat[:, 10:12], stat[:, 8:10], ACT.Sqrt, bias=eps_col[:, 0:1], scale=1.0 / 512).then_inc(gm.act, 1)

        def gm_vec1(vec):
            vec.wait_ge(gm.act, 3)
            vec.reciprocal(stat[:, 12:14], stat[:, 10:12]).then_inc(gm.vec, 1)
            vec.wait_ge(gm.vec, 1)
            for m in range(MT):
                vec.scalar_tensor_tensor(out=v_s[:, m, :], in0=v_s[:, m, :], scalar=stat[:, 12 + m:13 + m],
                                         in1=gmv[:, :], op0=ALU.mult, op1=ALU.mult).then_inc(gm.vec, 1)

        def gm_mix_pe(pe):
            for m in range(MT):
                pe.wait_ge(gm.vec, 2 + m)
                for g in range(4):
                    ins = pe.matmul(turn[m][:, g * P:(g + 1) * P], wsT[:, g, :], v_s[:, m, g * P:(g + 1) * P],
                                    start=True, stop=True)
                ins.then_inc(gm.pe, 1)

        def gm_vec2(vec):
            for m in range(MT):
                vec.wait_ge(gm.pe, 1 + m)
                for g in range(4):
                    ug = u_s[:, m, g * P:(g + 1) * P]
                    ins = vec.scalar_tensor_tensor(out=ug, in0=turn[m][:, g * P:(g + 1) * P],
                                                   scalar=col[:, R["gmb"] + g:R["gmb"] + g + 1], in1=ug,
                                                   op0=ALU.add, op1=ALU.mult)
                ins.then_inc(gm.vec, 1)

        def gm_turn_pe(pe):
            pe.wait_ge(cq.vec, 7)
            for m in range(MT):
                pe.wait_ge(gm.vec, 4 + m)
                for k in range(4):
                    ins = pe.transpose(turn[2 + m][:, k * P:(k + 1) * P], u_s[:, m, k * P:(k + 1) * P], ident[:, :])
                ins.then_inc(gm.pe, 1)

        def gm_vec3(vec):
            for m in range(MT):
                vec.wait_ge(gm.pe, 3 + m)
                vec.tensor_copy(yT[:, 0, :, m * P:(m + 1) * P],
                                turn[2 + m][:, :].rearrange("p (k n) -> p k n", k=4)).then_inc(gm.vec, 1)

        def cq_act(act):
            for i, (G, c, w) in enumerate(((G_CQ, C_CQ, QR), (G_KV, C_KV, KVR))):
                wait_products(act, c + 1)
                for m in range(MT):
                    act.activation(junk[:, 0:w], acc[bank(G, m)][:, 0:w], ACT.Square,
                                   accum_out=stat[:, 16 + 2 * i + m:17 + 2 * i + m]).then_inc(cq.act, 1)
                    act.wait_ge(cq.act, 2 * i + m + 1)
            act.activation(stat[:, 20:22], stat[:, 16:18], ACT.Sqrt, bias=eps_col[:, 0:1], scale=1.0 / QR).then_inc(cq.act, 1)
            act.activation(stat[:, 22:24], stat[:, 18:20], ACT.Sqrt, bias=eps_col[:, 0:1], scale=1.0 / KVR).then_inc(cq.act, 1)

        def cq_vec1(vec):
            vec.wait_ge(cq.act, 6)
            vec.reciprocal(stat[:, 24:28], stat[:, 20:24]).then_inc(cq.vec, 1)
            vec.wait_ge(cq.vec, 1)
            for m in range(MT):
                vec.tensor_scalar(cqn[:, m, :], acc[bank(G_CQ, m)][:, 0:QR], stat[:, 24 + m:25 + m], None,
                                  ALU.mult).then_inc(acc_read[bank(G_CQ, m)], 1)
            for m in range(MT):
                vec.tensor_scalar(ckvn[:, m, :], acc[bank(G_KV, m)][:, 0:KVR], stat[:, 26 + m:27 + m], None,
                                  ALU.mult).then_inc(cq.vec, 1)
                vec.tensor_copy(kpe[:, m, :], acc[bank(G_KV, m)][:, KVR:KVR + ROPE]).then_inc(acc_read[bank(G_KV, m)], 1)

        def cq_pe(pe):
            for m in range(MT):
                wait_acc_read(pe, G_CQ, m)
                for k in range(3):
                    ins = pe.transpose(turn[m][:, k * P:(k + 1) * P], cqn[:, m, k * P:(k + 1) * P], ident[:, :])
                ins.then_inc(cq.pe, 1)
            for m in range(MT):
                pe.wait_ge(cq.vec, 2 + m)
                for k in range(2):
                    ins = pe.transpose(turn[2 + m][:, k * P:(k + 1) * P], ckvn[:, m, k * P:(k + 1) * P], ident[:, :])
                ins.then_inc(cq.pe, 1)

        def cq_vec2(vec):
            for i, (dst, r, kk) in enumerate(((cqT, R["qn"], 3), (ckvT, R["kvn"], 2))):
                for m in range(MT):
                    vec.wait_ge(cq.pe, 2 * i + m + 1)
                    vec.tensor_tensor(dst[:, :, m * P:(m + 1) * P],
                                      turn[2 * i + m][:, 0:kk * P].rearrange("p (k n) -> p k n", k=kk),
                                      col[:, r:r + kk].unsqueeze(2).broadcast_to([P, kk, P]), ALU.mult).then_inc(cq.vec, 1)

        def xbc_act1(act):
            act.wait_ge(xb.vec, 1)
            for G, c, f in ((G_XBC0, C_XBC0, 0), (G_XBC1, C_XBC1, 4)):
                wait_products(act, c + 1)
                for q in range(2):
                    act.activation(xpad[:, f + 2 * q:f + 2 * q + 2, 3:3 + TOK],
                                   acc[bank(G, q)][:, :].rearrange("p (f n) -> p f n", f=2),
                                   ACT.Copy).then_inc(acc_read[bank(G, q)], 1)

        def xbc_act2(act):
            for f in range(8):
                act.wait_ge(xb.vec, 26 + f)
                act.activation(conv[:, f, :], conv[:, f, :], ACT.Silu,
                               bias=col[:, R["convb"] + f:R["convb"] + f + 1]).then_inc(xb.act, 1)

        def xbc_vec(vec):
            for j in range(4):
                for f in range(8):
                    w = col[:, R["convw"] + 8 * j + f:R["convw"] + 8 * j + f + 1]
                    if j == 0:
                        wait_acc_read(vec, G_XBC0 + f // 4, (f % 4) // 2)
                        vec.tensor_scalar(conv[:, f, :], xpad[:, f, 0:TOK], w, None, ALU.mult).then_inc(xb.vec, 1)
                    else:
                        vec.wait_ge(xb.vec, 1 + 8 * (j - 1) + f + 1)
                        vec.scalar_tensor_tensor(out=conv[:, f, :], in0=xpad[:, f, j:j + TOK], scalar=w,
                                                 in1=conv[:, f, :], op0=ALU.mult, op1=ALU.add).then_inc(xb.vec, 1)

        def dt_pe(pe):
            wait_chunk(pe, C_XBC1)
            wait_chunk(pe, C_XBC1 + 1)
            for m in range(MT):
                for k in range(KD):
                    ins = pe.matmul(turn[m][:, 0:8], xT[:, k, m * P:(m + 1) * P],
                                    slot(C_XBC1 + k // 4, 4, 520)[:, k % 4, 512:520], start=(k == 0), stop=(k == KD - 1))
                ins.then_inc(dts.pe, 1)

        SMALL_E = 0.03

        def softplus_vec(vec, s, W, n, base):
            def w(i):
                return W[:, i, 0:n]
            vec.wait_ge(s.vec, base)
            vec.tensor_scalar(w(1), w(0), 0.0, None, ALU.max).then_inc(s.vec, 1)
            vec.tensor_scalar(w(2), w(0), -1.0, None, ALU.mult).then_inc(s.vec, 1)
            vec.wait_ge(s.vec, base + 2)
            vec.tensor_tensor(w(3), w(0), w(2), ALU.min).then_inc(s.vec, 1)
            vec.wait_ge(s.act, 1)
            vec.tensor_scalar(w(5), w(4), 1.0, None, ALU.add).then_inc(s.vec, 1)
            vec.tensor_scalar(w(7), w(4), 0.2, None, ALU.mult).then_inc(s.vec, 1)
            for i, k in enumerate((-0.25, 1 / 3, -0.5, 1.0)):
                vec.wait_ge(s.vec, base + 5 + i)
                vec.scalar_tensor_tensor(out=w(7), in0=w(7), scalar=k, in1=w(4), op0=ALU.add,
                                         op1=ALU.mult).then_inc(s.vec, 1)
            vec.wait_ge(s.vec, base + 9)
            vec.scalar_tensor_tensor(out=w(7), in0=w(4), scalar=SMALL_E, in1=w(7),
                                     op0=ALU.is_lt, op1=ALU.mult).then_inc(s.vec, 1)
            vec.wait_ge(s.act, 2)
            vec.scalar_tensor_tensor(out=w(9), in0=w(4), scalar=SMALL_E, in1=w(8),
                                     op0=ALU.is_ge, op1=ALU.mult).then_inc(s.vec, 1)
            vec.wait_ge(s.vec, base + 11)
            vec.tensor_tensor(w(9), w(9), w(7), ALU.add).then_inc(s.vec, 1)
            vec.wait_ge(s.vec, base + 12)
            vec.tensor_tensor(w(10), w(9), w(1), ALU.add).then_inc(s.vec, 1)
            vec.wait_ge(s.vec, base + 13)

        def softplus_act(act, s, W, n, base):
            act.wait_ge(s.vec, base + 3)
            act.activation(W[:, 4, 0:n], W[:, 3, 0:n], ACT.Exp).then_inc(s.act, 1)
            act.wait_ge(s.vec, base + 4)
            act.activation(W[:, 8, 0:n], W[:, 5, 0:n], ACT.Ln).then_inc(s.act, 1)

        def dt_vec(vec):
            for m in range(MT):
                vec.wait_ge(dts.pe, 1 + m)
                vec.tensor_tensor(dtw[:, 0, 8 * m:8 * m + 8], turn[m][:, 0:8], small[:, 0:8], ALU.add).then_inc(dts.vec, 1)
            softplus_vec(vec, dts, dtw, 16, 2)
            vec.tensor_tensor(da.rearrange("p (m h) -> p m h", m=MT), dt_v.rearrange("p (m h) -> p m h", m=MT),
                              neg_a[:, :].unsqueeze(1).broadcast_to([P, MT, 8]), ALU.mult).then_inc(dts.vec, 1)

        def sd_cs_pe(pe):
            pe.wait_ge(dts.vec, 16)
            for m in range(MT):
                pe.matmul(turn[2][:, 8 * m:8 * m + 8], upper[:, :], da[:, 8 * m:8 * m + 8], start=True, stop=True)
            pe.matmul(turn[2][:, 16:24], ones[:, :], da[:, 0:8], start=True, stop=True).then_inc(sd.pe, 1)

        def sd_rows_pe(pe):
            pe.wait_ge(sd.vec, 1)
            for r in range(4):
                for h in range(4):
                    j = 4 * r + h
                    ins = pe.matmul(turn[r][:, h * P:(h + 1) * P], da[:, j:j + 1].broadcast_to([P, P]), upper[:, :],
                                    start=True, stop=True)
                ins.then_inc(sd.pe, 1)

        def sd_turn_pe(pe):
            pe.wait_ge(xb.act, 8)
            pe.wait_ge(sd.vec, 6)
            for m in range(MT):
                for f in range(4):
                    ins = pe.transpose(turn[m][:, f * P:(f + 1) * P], conv[:, f, m * P:(m + 1) * P], ident[:, :])
                ins.then_inc(sd.pe, 1)
            for m in range(MT):
                for g in range(2):
                    ins = pe.transpose(turn[2][:, (2 * m + g) * P:(2 * m + g + 1) * P],
                                       conv[:, 4 + g, m * P:(m + 1) * P], ident[:, :])
            ins.then_inc(sd.pe, 1)
            for m in range(MT):
                for g in range(2):
                    ins = pe.matmul(turn[3][:, (2 * m + g) * P:(2 * m + g + 1) * P],
                                    conv[:, 4 + g, m * P:(m + 1) * P], conv[:, 6 + g, m * P:(m + 1) * P],
                                    start=True, stop=True)
            ins.then_inc(sd.pe, 1)

        def sd_y_pe(pe):
            for m in range(MT):
                pe.wait_ge(sd.vec, 15 + m)
                for h in range(H):
                    ins = pe.matmul(turn[m][:, h * VD:(h + 1) * VD], Ld[:, 8 * m + h, :], xdt[:, m, h * VD:(h + 1) * VD],
                                    start=True, stop=True)
                ins.then_inc(sd.pe, 1)
            pe.wait_ge(sd.vec, 17)
            for g in range(2):
                ins = pe.matmul(turn[2][:, g * 256:(g + 1) * 256], B_tok[:, 0, g, :], xdtd[:, g * 256:(g + 1) * 256],
                                start=True, stop=True)
            ins.then_inc(sd.pe, 1)

        def sd_off_pe(pe):
            pe.wait_ge(sd.vec, 18)
            for g in range(2):
                ins = pe.matmul(turn[3][:, g * 256:(g + 1) * 256], conv[:, 6 + g, P:2 * P], S0[:, g * 256:(g + 1) * 256],
                                start=True, stop=True)
            ins.then_inc(sd.pe, 1)

        def sd_out_pe(pe):
            for m in range(MT):
                pe.wait_ge(sd.vec, 28 + m)
                for k in range(4):
                    ins = pe.transpose(turn[m][:, k * P:(k + 1) * P], yc[:, m, k * P:(k + 1) * P], ident[:, :])
                ins.then_inc(sd.pe, 1)

        def heads(ap, n=H):
            return ap.rearrange("p (h d) -> p h d", h=n)

        def over(ap, n, d):
            return ap.unsqueeze(2).broadcast_to([P, n, d])

        def sd_vec1(vec):
            vec.wait_ge(sd.pe, 1)
            vec.tensor_copy(csv[:, 0:24], turn[2][:, 0:24]).then_inc(sd.vec, 1)
            vec.wait_ge(sd.vec, 1)
            vec.tensor_tensor(csv[:, 24:32], csv[:, 16:24], csv[:, 0:8], ALU.subtract).then_inc(sd.vec, 1)
            for r in range(4):
                vec.wait_ge(sd.pe, 2 + r)
                for h in range(4):
                    j = 4 * r + h
                    ins = vec.tensor_scalar(Ld[:, j, :], turn[r][:, h * P:(h + 1) * P], csv[:, j:j + 1], 0.0,
                                            ALU.subtract, ALU.min)
                ins.then_inc(sd.vec, 1)

        def sd_vec2(vec):
            for m in range(MT):
                vec.wait_ge(sd.pe, 6 + m)
                vec.tensor_copy(xs_tok[:, m, :], turn[m][:, :]).then_inc(sd.vec, 1)
            vec.wait_ge(sd.pe, 8)
            vec.tensor_copy(B_tok.rearrange("p m g n -> p (m g n)"), turn[2][:, :]).then_inc(sd.vec, 1)
            vec.wait_ge(sd.pe, 9)
            vec.tensor_tensor(cbm.rearrange("p m g n -> p (m g) n"), turn[3][:, :].rearrange("p (j n) -> p j n", j=4),
                              upper[:, :].unsqueeze(1).broadcast_to([P, 4, P]), ALU.mult).then_inc(sd.vec, 1)
            vec.wait_ge(sd.vec, 10)
            for r in range(4):
                vec.wait_ge(sd.act, 3 + r)
                vec.tensor_tensor(Ld[:, 4 * r:4 * r + 4, :], Ld[:, 4 * r:4 * r + 4, :],
                                  cbm[:, r // 2, r % 2, :].unsqueeze(1).broadcast_to([P, 4, P]),
                                  ALU.mult).then_inc(sd.vec, 1)
            for m in range(MT):
                vec.tensor_tensor(heads(xdt[:, m, :]), heads(xs_tok[:, m, :]), over(dt_v[:, 8 * m:8 * m + 8], H, VD),
                                  ALU.mult).then_inc(sd.vec, 1)
            vec.wait_ge(sd.vec, 16)
            vec.wait_ge(sd.act, 2)
            vec.tensor_tensor(heads(xdtd), heads(xdt[:, 0, :]), over(csv[:, 24:32], H, VD), ALU.mult).then_inc(sd.vec, 1)

        def sd_vec3(vec):
            vec.wait_ge(sd.pe, 12)
            vec.tensor_copy(S0, turn[2][:, :]).then_inc(sd.vec, 1)
            for m in range(MT):
                vec.tensor_tensor(heads(yc[:, m, :]), heads(xs_tok[:, m, :]), over(small[:, 16:24], H, VD),
                                  ALU.mult).then_inc(sd.vec, 1)
            vec.wait_ge(sd.vec, 20)
            for m in range(MT):
                vec.tensor_tensor(yc[:, m, :], yc[:, m, :], turn[m][:, :], ALU.add).then_inc(sd.vec, 1)
            vec.wait_ge(sd.pe, 13)
            vec.wait_ge(sd.act, 1)
            vec.tensor_tensor(heads(xdt[:, 0, :]), heads(turn[3][:, :]), over(csv[:, 32:40], H, VD), ALU.mult).then_inc(sd.vec, 1)
            vec.wait_ge(sd.vec, 23)
            vec.tensor_tensor(yc[:, 1, :], yc[:, 1, :], xdt[:, 0, :], ALU.add).then_inc(sd.vec, 1)
            vec.wait_ge(sd.vec, 24)
            for m in range(MT):
                wait_acc_read(vec, G_Z, m)
                vec.tensor_tensor(yc[:, m, :], yc[:, m, :], sz[:, m, :], ALU.mult).then_inc(sd.vec, 1)
            vec.wait_ge(sd.act, 11)
            vec.reciprocal(stat[:, 40:44], stat[:, 36:40]).then_inc(sd.vec, 1)
            vec.wait_ge(sd.vec, 27)
            for m in range(MT):
                vec.tensor_tensor(heads(yc[:, m, :], 2), heads(yc[:, m, :], 2), over(stat[:, 40 + 2 * m:42 + 2 * m], 2, 256),
                                  ALU.mult).then_inc(sd.vec, 1)

        def sd_vec4(vec):
            for m in range(MT):
                vec.wait_ge(sd.pe, 14 + m)
                vec.tensor_tensor(yT[:, 2, :, m * P:(m + 1) * P], heads(turn[m][:, :], 4),
                                  over(col[:, R["ssdn"]:R["ssdn"] + 4], 4, P), ALU.mult).then_inc(sd.vec, 1)

        def z_act(act):
            wait_products(act, C_Z + 1)
            for m in range(MT):
                act.activation(sz[:, m, :], acc[bank(G_Z, m)][:, :], ACT.Silu).then_inc(acc_read[bank(G_Z, m)], 1)

        def sd_act1(act):
            act.wait_ge(sd.vec, 2)
            act.activation(csv[:, 32:40], csv[:, 8:16], ACT.Exp).then_inc(sd.act, 1)
            act.activation(csv[:, 24:32], csv[:, 24:32], ACT.Exp).then_inc(sd.act, 1)
            for r in range(4):
                act.wait_ge(sd.vec, 3 + r)
                act.activation(Ld[:, 4 * r:4 * r + 4, :], Ld[:, 4 * r:4 * r + 4, :], ACT.Exp).then_inc(sd.act, 1)

        def sd_act2(act):
            for m in range(MT):
                act.wait_ge(sd.vec, 25 + m)
                for g in range(2):
                    n = 2 * m + g
                    act.activation(junk[:, 0:256], yc[:, m, g * 256:(g + 1) * 256], ACT.Square,
                                   accum_out=stat[:, 32 + n:33 + n]).then_inc(sd.act, 1)
                    act.wait_ge(sd.act, 7 + n)
            act.activation(stat[:, 36:40], stat[:, 32:36], ACT.Sqrt, bias=eps_col[:, 0:1], scale=1.0 / 256).then_inc(sd.act, 1)

        def qs_groups_pe(pe):
            pe.wait_ge(cq.vec, 7)
            for n in range(2):
                group_pe(pe, G_UQ + n, C_UQ + n, cqT, (3,), 384)
            wait_chunk(pe, C_UKV)
            w = slot(C_UKV, 2, D)
            for n in range(2):
                for m in range(MT):
                    wait_acc_free(pe, G_UKV + n, m)
                    for k in range(2):
                        ins = pe.matmul(acc[bank(G_UKV + n, m)][:, :], ckvT[:, k, m * P:(m + 1) * P],
                                        w[:, k, n * 512:(n + 1) * 512], start=(k == 0), stop=(k == 1))
            ins.then_inc(products_done, 1)

        def qs_act1(act):
            for n in range(2):
                wait_products(act, C_UQ + n)
                for m in range(MT):
                    act.activation(qk[:, m, 4 * n:4 * n + 4, :], acc[bank(G_UQ + n, m)][:, 0:384].rearrange(
                        "p (h d) -> p h d", h=4), ACT.Copy).then_inc(acc_read[bank(G_UQ + n, m)], 1)
            wait_products(act, C_UKV)
            for n in range(2):
                for m in range(MT):
                    kv = acc[bank(G_UKV + n, m)][:, :].rearrange("p (h d) -> p h d", h=4)
                    act.activation(qk[:, m, H + 4 * n:H + 4 * n + 4, 0:NOPE], kv[:, :, 0:NOPE], ACT.Copy)
                    act.activation(vtok[:, m, 4 * n:4 * n + 4, :], kv[:, :, NOPE:NOPE + VD],
                                   ACT.Copy).then_inc(acc_read[bank(G_UKV + n, m)], 1)

        def qs_vec1(vec):
            for m in range(MT):
                wait_acc_read(vec, G_KV, m)
                vec.tensor_copy(qk[:, m, H:2 * H, NOPE:QKD], kpe[:, m, :].unsqueeze(1).broadcast_to([P, H, ROPE])
                                ).then_inc(qs.vec, 1)
            vec.wait_ge(qs.vec, 2)
            sq_v = sq.rearrange("p (h d) -> p h d", h=2 * H)
            for m in range(MT):
                for n in range(2):
                    wait_acc_read(vec, G_UQ + n, m)
                    wait_acc_read(vec, G_UKV + n, m)
                vec.tensor_tensor(sq_v, qk[:, m, :, :], qk[:, m, :, :], ALU.mult).then_inc(qs.vec, 1)
                vec.wait_ge(qs.vec, 3 + 2 * m)
                vec.tensor_reduce(stat[:, 0:16] if m == 0 else stat[:, 16:32], sq_v, AX, ALU.add).then_inc(qs.vec, 1)
                vec.wait_ge(qs.vec, 4 + 2 * m)
            vec.wait_ge(qs.act, 1)
            vec.reciprocal(qrs[:, 0:32], qrs[:, 0:32]).then_inc(qs.vec, 1)
            vec.wait_ge(qs.vec, 7)
            for m in range(MT):
                vec.tensor_tensor(qk[:, m, :, :], qk[:, m, :, :], over(qrs[:, 16 * m:16 * m + 16], 2 * H, QKD),
                                  ALU.mult).then_inc(qs.vec, 1)
            for m in range(MT):
                vec.wait_ge(qs.vec, 8 + m)
                qv = qk[:, m, :, :].rearrange("p (s h) d -> p s h d", s=2)
                vec.tensor_tensor(qv, qv, qk_gain[:, :, :].unsqueeze(2).broadcast_to([P, 2, H, QKD]),
                                  ALU.mult).then_inc(qs.vec, 1)

        def qs_vec2(vec):
            for m in range(MT):
                vec.wait_ge(qs.vec, 10 + m)
                x1, x2 = qk[:, m, :, NOPE:NOPE + 16], qk[:, m, :, NOPE + 16:QKD]
                c = cos[:, m, :].unsqueeze(1).broadcast_to([P, 2 * H, 16])
                s = sin[:, m, :].unsqueeze(1).broadcast_to([P, 2 * H, 16])
                r = rope_t[:, m]
                for i, (a, b) in enumerate(((x1, c), (x2, s), (x2, c), (x1, s))):
                    vec.tensor_tensor(r[:, i], a, b, ALU.mult).then_inc(qs.vec, 1)
                vec.wait_ge(qs.vec, 15 + 6 * m)
                vec.tensor_tensor(x1, r[:, 0], r[:, 1], ALU.subtract).then_inc(qs.vec, 1)
                vec.tensor_tensor(x2, r[:, 2], r[:, 3], ALU.add).then_inc(qs.vec, 1)

        def qs_act2(act):
            act.wait_ge(qs.vec, 6)
            act.activation(qrs[:, 0:32], stat[:, 0:32], ACT.Sqrt, bias=eps_col[:, 0:1], scale=1.0 / QKD).then_inc(qs.act, 1)

        def qs_turn_pe(pe):
            for m in range(MT):
                pe.wait_ge(qs.vec, 17 + 6 * m)
                for kind in range(2):
                    for hf in range(2):
                        r = 4 * m + 2 * kind + hf
                        if r >= 4:
                            pe.wait_ge(qs.vec, 24 + r - 4)
                        for h in range(4):
                            ins = pe.transpose(turn[r % 4][0:QKD, h * P:(h + 1) * P],
                                               qk[:, m, H * kind + 4 * hf + h, :], ident[:, :])
                        ins.then_inc(qs.pe, 1)

        def qs_vec3(vec):
            for r in range(8):
                m, kind, hf = r // 4, r // 2 % 2, r % 2
                vec.wait_ge(qs.pe, 1 + r)
                dst = (qT, kT)[kind]
                vec.tensor_copy(dst[0:QKD, 4 * hf:4 * hf + 4, m * P:(m + 1) * P],
                                turn[r % 4][0:QKD, :].rearrange("p (h n) -> p h n", h=4)).then_inc(qs.vec, 1)

        def qs_scores_pe(pe):
            pe.wait_ge(qs.vec, 31)
            for m in range(MT):
                nk = P * (m + 1)
                for hp in range(4):
                    if m > 0:
                        pe.wait_ge(qs.vec, 32 + hp)
                    for h in range(2):
                        ins = pe.matmul(turn[hp][:, h * nk:(h + 1) * nk], qT[0:QKD, 2 * hp + h, m * P:(m + 1) * P],
                                        kT[0:QKD, 2 * hp + h, 0:nk], start=True, stop=True)
                    ins.then_inc(qs.pe, 1)

        def qs_vec4(vec):
            for m, sc in enumerate((sc0, sc1)):
                nk = P * (m + 1)
                for hp in range(4):
                    vec.wait_ge(qs.pe, 9 + 4 * m + hp)
                    vec.tensor_tensor(sc[:, 2 * hp:2 * hp + 2, :], turn[hp][:, 0:2 * nk].rearrange("p (h n) -> p h n", h=2),
                                      causal[:, TOK - nk:TOK].unsqueeze(1).broadcast_to([P, 2, nk]),
                                      ALU.add).then_inc(qs.vec, 1)
            for m, sc in enumerate((sc0, sc1)):
                vec.wait_ge(qs.vec, 35 + 4 * m)
                vec.tensor_reduce(att[:, 0, 8 * m:8 * m + 8], sc, AX, ALU.max).then_inc(qs.vec, 1)
            vec.wait_ge(qs.vec, 41)
            vec.tensor_scalar(att[:, 1, :], att[:, 0, :], -SCALE, None, ALU.mult).then_inc(qs.vec, 1)

        def qs_act3(act):
            act.wait_ge(qs.vec, 42)
            for m, sc in enumerate((sc0, sc1)):
                for h in range(H):
                    j = 8 * m + h
                    act.activation(sc[:, h, :], sc[:, h, :], ACT.Exp, bias=att[:, 1, j:j + 1], scale=SCALE,
                                   accum_out=att[:, 2, j:j + 1]).then_inc(qs.act, 1)

        def qs_vec5(vec):
            for m, sc in enumerate((sc0, sc1)):
                vec.wait_ge(qs.act, 9 + 8 * m)
                vec.reciprocal(att[:, 3, 8 * m:8 * m + 8], att[:, 2, 8 * m:8 * m + 8]).then_inc(qs.vec, 1)
                vec.wait_ge(qs.vec, 43 + 2 * m)
                vec.tensor_tensor(sc, sc, over(att[:, 3, 8 * m:8 * m + 8], H, P * (m + 1)), ALU.mult).then_inc(qs.vec, 1)

        TURNS = [(0, 0, 0), (0, 0, 1), (1, 0, 0), (1, 0, 1), (1, 1, 0), (1, 1, 1)]

        def qs_pt_pe(pe):
            for r, (m, kb, hf) in enumerate(TURNS):
                pe.wait_ge(qs.vec, 44 + 2 * m)
                if r >= 4:
                    pe.wait_ge(qs.vec, 47 + r - 4)
                for h in range(4):
                    ins = pe.transpose(turn[r % 4][:, h * P:(h + 1) * P],
                                       (sc0, sc1)[m][:, 4 * hf + h, kb * P:(kb + 1) * P], ident[:, :])
                ins.then_inc(qs.pe, 1)

        def qs_vec6(vec):
            for r, (m, kb, hf) in enumerate(TURNS):
                vec.wait_ge(qs.pe, 17 + r)
                dst = PT1[:, kb, 4 * hf:4 * hf + 4, :] if m else PT0[:, 4 * hf:4 * hf + 4, :]
                vec.tensor_copy(dst, turn[r % 4][:, :].rearrange("p (h n) -> p h n", h=4)).then_inc(qs.vec, 1)

        def qs_pv_pe(pe):
            pe.wait_ge(qs.vec, 52)
            for m in range(MT):
                for h in range(H):
                    o = turn[2 + m][64 * (h % 2):64 * (h % 2) + 64, (h // 2) * P:(h // 2 + 1) * P]
                    for kb in range(m + 1):
                        ins = pe.matmul(o, vtok[:, kb, h, :], PT1[:, kb, h, :] if m else PT0[:, h, :],
                                        start=(kb == 0), stop=(kb == m))
                ins.then_inc(qs.pe, 1)

        def qs_vec7(vec):
            for m in range(MT):
                vec.wait_ge(qs.pe, 23 + m)
                vec.tensor_copy(yT[:, 1, :, m * P:(m + 1) * P], heads(turn[2 + m][:, :], 4)).then_inc(qs.vec, 1)

        def gate_act(act, i):
            wait_products(act, C_GATE + 2 * i + 1)
            for m in range(MT):
                act.activation(gates[:, m, i * 512:(i + 1) * 512], acc[bank(G_GATE + i, m)][:, :],
                               ACT.Sigmoid).then_inc(acc_read[bank(G_GATE + i, m)], 1)

        BRANCH_IN = {0: (gm.vec, 7), 1: (qs.vec, 54), 2: (sd.vec, 31)}

        def branch_pe(pe, j):
            pe.wait_ge(*BRANCH_IN[BRANCHES[j]])
            for n in range(2):
                group_pe(pe, G_BR + 2 * j + n, C_BR + 2 * j + n, yT[:, BRANCHES[j]], (4,), 512)

        def branch_vec(vec, j):
            b = BRANCHES[j]
            for n in range(2):
                wait_acc_read(vec, G_GATE + 2 * b + n, 0)
                wait_acc_read(vec, G_GATE + 2 * b + n, 1)
                wait_products(vec, C_BR + 2 * j + n)
                for m in range(MT):
                    g = bank(G_BR + 2 * j + n, m)
                    dst = xn[:, m, n * 512:(n + 1) * 512] if j == 0 else br_t[:, n, m, :]
                    vec.tensor_tensor(dst, acc[g][:, :], gates[:, m, b * D + n * 512:b * D + (n + 1) * 512],
                                      ALU.mult).then_inc(acc_read[g], 1)
            if j > 0:
                for n in range(2):
                    for m in range(MT):
                        wait_acc_read(vec, G_BR + 2 * j + n, m)
                        wait_acc_read(vec, G_BR + n, m)
                        dst = xn[:, m, n * 512:(n + 1) * 512]
                        vec.tensor_tensor(dst, dst, br_t[:, n, m, :], ALU.add).then_inc(br.vec, 1)
                vec.wait_ge(br.vec, 4 * j)

        def merged_pe(pe):
            pe.wait_ge(br.vec, 8)
            for b in range(4):
                m, hf = b // 2, b % 2
                for k in range(4):
                    ins = pe.transpose(turn[b][:, k * P:(k + 1) * P],
                                       xn[:, m, (4 * hf + k) * P:(4 * hf + k + 1) * P], ident[:, :])
                ins.then_inc(mt.pe, 1)

        def merged_vec(vec):
            for b in range(4):
                m, hf = b // 2, b % 2
                vec.wait_ge(mt.pe, 1 + b)
                vec.tensor_copy(xT[:, 4 * hf:4 * hf + 4, m * P:(m + 1) * P], heads(turn[b][:, :], 4)).then_inc(mt.vec, 1)

        def gate_pe(pe, i):
            group_pe(pe, G_GATE + i, C_GATE + 2 * i, xT, (4, 4), 512)

        def mixer_pe(pe):
            norm_pe(pe, mix_norm)
            pe.wait_ge(mix_norm.vec, NORM_DONE)
            group_pe(pe, G_U, C_U, xT, (4, 4), 512)
            group_pe(pe, G_V, C_V, xT, (4, 4), 512)
            group_pe(pe, G_CQ, C_CQ, xT, (4, 4), QR)
            gm_mix_pe(pe)
            group_pe(pe, G_KV, C_KV, xT, (4, 4), KVR + ROPE)
            turned_group_pe(pe, G_XBC0, C_XBC0, xT, 4, 512)
            cq_pe(pe)
            gm_turn_pe(pe)
            dt_pe(pe)
            turned_group_pe(pe, G_XBC1, C_XBC1, xT, 4, 520)
            group_pe(pe, G_Z, C_Z, xT, (4, 4), 512)
            qs_groups_pe(pe)
            gate_pe(pe, 0)
            sd_cs_pe(pe)
            gate_pe(pe, 1)
            sd_rows_pe(pe)
            sd_turn_pe(pe)
            gate_pe(pe, 2)
            sd_y_pe(pe)
            gate_pe(pe, 3)
            sd_off_pe(pe)
            sd_out_pe(pe)
            gate_pe(pe, 4)
            qs_turn_pe(pe)
            gate_pe(pe, 5)
            qs_scores_pe(pe)
            branch_pe(pe, 0)
            qs_pt_pe(pe)
            branch_pe(pe, 1)
            qs_pv_pe(pe)
            branch_pe(pe, 2)
            merged_pe(pe)
            pe.wait_ge(mt.vec, 4)
            group_pe(pe, G_WO, C_WO, xT, (4, 4), 512)
            group_pe(pe, G_WO + 1, C_WO + 2, xT, (4, 4), 512)

        def mixer_act(act):
            norm_act(act, mix_norm, wait_src=lambda e: wait_x(e, NFB))
            gm_act(act)
            cq_act(act)
            xbc_act1(act)
            softplus_act(act, dts, dtw, 16, 2)
            z_act(act)
            qs_act1(act)
            gate_act(act, 0)
            sd_act1(act)
            xbc_act2(act)
            gate_act(act, 1)
            gate_act(act, 2)
            sd_act2(act)
            gate_act(act, 3)
            qs_act2(act)
            gate_act(act, 4)
            gate_act(act, 5)
            qs_act3(act)

        def mixer_vec(vec):
            norm_vec(vec, mix_norm, col[:, R["mix"]:R["mix"] + 8])
            vec.memset(xpad[:, :, 0:3], 0.0).then_inc(xb.vec, 1)
            gm_vec1(vec)
            gm_vec2(vec)
            cq_vec1(vec)
            cq_vec2(vec)
            gm_vec3(vec)
            dt_vec(vec)
            sd_vec1(vec)
            xbc_vec(vec)
            sd_vec2(vec)
            sd_vec3(vec)
            sd_vec4(vec)
            qs_vec1(vec)
            qs_vec2(vec)
            qs_vec3(vec)
            qs_vec4(vec)
            branch_vec(vec, 0)
            qs_vec5(vec)
            qs_vec6(vec)
            branch_vec(vec, 1)
            qs_vec7(vec)
            branch_vec(vec, 2)
            merged_vec(vec)
            add_to_x(vec, C_WO + 3, G_WO, 1.0)

        INV_FREQ = [float(v) for v in (np.float32(1.0) / (np.float32(10000.0) ** (np.arange(0, 32, 2, dtype=np.float32) / np.float32(32))))]
        TWO_PI = 2 * math.pi
        PI_HI = 6.28125
        PI_MID = float(np.float32(1.9350051879882812e-3))
        PI_LO = TWO_PI - PI_HI - PI_MID
        ROUND = 1.5 * 2.0 ** 23
        PI_F = 3.1415925

        def sincos_vec(vec, s, base, a, k, r, c):
            vec.tensor_scalar(k, a, 1 / TWO_PI, ROUND, ALU.mult, ALU.add).then_inc(s.vec, 1)
            vec.wait_ge(s.vec, base + 1)
            vec.tensor_scalar(k, k, ROUND, None, ALU.subtract).then_inc(s.vec, 1)
            vec.wait_ge(s.vec, base + 2)
            vec.scalar_tensor_tensor(out=r, in0=k, scalar=-PI_HI, in1=a, op0=ALU.mult, op1=ALU.add).then_inc(s.vec, 1)
            vec.wait_ge(s.vec, base + 3)
            vec.scalar_tensor_tensor(out=r, in0=k, scalar=-PI_MID, in1=r, op0=ALU.mult, op1=ALU.add).then_inc(s.vec, 1)
            vec.wait_ge(s.vec, base + 4)
            vec.scalar_tensor_tensor(out=r, in0=k, scalar=-PI_LO, in1=r, op0=ALU.mult, op1=ALU.add).then_inc(s.vec, 1)
            vec.wait_ge(s.vec, base + 5)
            vec.tensor_scalar(r, r, PI_F, -PI_F, ALU.min, ALU.max).then_inc(s.vec, 1)
            vec.wait_ge(s.vec, base + 6)
            vec.tensor_scalar(c, r, -1.0, None, ALU.mult).then_inc(s.vec, 1)
            vec.wait_ge(s.vec, base + 7)
            vec.tensor_tensor(c, c, r, ALU.max).then_inc(s.vec, 1)
            vec.wait_ge(s.vec, base + 8)
            vec.tensor_scalar(c, c, -1.0, math.pi / 2, ALU.mult, ALU.add).then_inc(s.vec, 1)

        SINCOS = 9

        pos_i = sb("pos_i", [P, MT], I32)
        pos = sb("pos", [P, MT])
        ang = sb("ang", [P, 4, MT * 16])
        qrs = sb("qrs", [P, 32])
        cst = steps("const", "act vec pool")
        pos_in, x_in = sem("positions_in"), sem("x_in")

        with nc.Block() as block:
            @block.sync
            def _(sync):
                sync.dma_start(pos_i[:, :], t["positions"].rearrange("o (m p) -> p (o m)", p=P),
                               allow_slow_non_contiguous=True).then_inc(pos_in, 16)
                sync.dma_start(x[:, :, :], t["x"].rearrange("o (m p) d -> p (o m) d", p=P)).then_inc(x_in, 16)
                sync.wait_ge(x_in, 16)

            @block.gpsimd
            def _(pool):
                pool.memset(ones[:, :], 1.0).then_inc(cst.pool, 1)
                pool.memset(causal[:, :], 0.0).then_inc(cst.pool, 1)
                pool.wait_ge(cst.pool, 2)
                pool.affine_select(out=ident[:, :], in_=ones[:, :], compare_op=ALU.is_equal, fill=0.0, base=0,
                                   pattern=[[-1, P]], channel_multiplier=1).then_inc(cst.pool, 1)
                pool.affine_select(out=upper[:, :], in_=ones[:, :], compare_op=ALU.is_ge, fill=0.0, base=0,
                                   pattern=[[1, P]], channel_multiplier=-1).then_inc(cst.pool, 1)
                pool.affine_select(out=causal[:, P:TOK], in_=causal[:, P:TOK], compare_op=ALU.is_ge, fill=-1e30, base=0,
                                   pattern=[[-1, P]], channel_multiplier=1).then_inc(cst.pool, 1)

            @block.vector
            def _(vec):
                vec.memset(eps_col[:, :], EPS)
                for i, f in enumerate(INV_FREQ):
                    ins = vec.memset(ang[:, 0, i:i + 1], f)
                ins.then_inc(cst.vec, 1)
                vec.wait_ge(pos_in, 16)
                vec.tensor_copy(pos[:, :], pos_i[:, :]).then_inc(cst.vec, 1)
                vec.wait_ge(cst.vec, 2)
                for m in range(MT):
                    vec.tensor_scalar(ang[:, 1, 16 * m:16 * m + 16], ang[:, 0, 0:16], pos[:, m:m + 1], None,
                                      ALU.mult).then_inc(cst.vec, 1)
                vec.wait_ge(cst.vec, 4)
                sincos_vec(vec, cst, 4, ang[:, 1, :], ang[:, 0, :], ang[:, 2, :], ang[:, 3, :])

            @block.scalar
            def _(act):
                act.wait_ge(cst.vec, 4 + SINCOS)
                act.activation(sin[:, :, :].rearrange("p m n -> p (m n)"), ang[:, 2, :], ACT.Sin).then_inc(cst.act, 1)
                act.activation(cos[:, :, :].rearrange("p m n -> p (m n)"), ang[:, 3, :], ACT.Sin).then_inc(cst.act, 1)

        def clear_semaphores():
            nc.all_engine_barrier()
            for s in all_sems:
                nc.sync.sem_clear(s)
            nc.all_engine_barrier()

        clear_semaphores()

        def ffn_views(name, l):
            w = lay(name + "_w_in", l)
            d = lay(name + "_w_out", l)
            def part(first):
                return lambda j: w[:, :, bass.ds(first + FB * j, FB)].rearrange("o (k p) n -> p (o k) n", p=P)
            return part(0), part(FF), lambda i: d[:, 2 * P * i:2 * P * (i + 1), :].rearrange("o (k p) n -> p (o k) n", p=P)

        with nc.Fori(0, DEPTH) as layer:
            with nc.Block() as block:
                @block.sync
                def _(sync):
                    ffn_sync(sync, f1, 0, *ffn_views("ffn1", layer))
                    mixer_sync(sync, layer)
                    ffn_sync(sync, f2, C_FFN2, *ffn_views("ffn2", layer))

                @block.scalar
                def _(act):
                    params_act(act, layer)
                    norm_act(act, n1)
                    split_x_act(act, n1)
                    ffn_act(act, f1, 0, 0)
                    mixer_act(act)
                    norm_act(act, n2, wait_src=lambda e: wait_x(e, G_WO))
                    split_x_act(act, n2)
                    ffn_act(act, f2, C_FFN2, G_FFN2)

                @block.vector
                def _(vec):
                    for i in range(4):
                        vec.sem_inc(acc_read[i], 1)
                    params_vec(vec)
                    norm_vec(vec, n1, col[:, R["ffn1"]:R["ffn1"] + 8])
                    split_x_vec(vec, n1)
                    ffn_vec(vec, f1, 0, 0, 0.5)
                    mixer_vec(vec)
                    norm_vec(vec, n2, col[:, R["ffn2"]:R["ffn2"] + 8])
                    split_x_vec(vec, n2)
                    ffn_vec(vec, f2, C_FFN2, G_FFN2, 0.5)

                @block.tensor
                def _(pe):
                    pe.sem_inc(products_done, RING)
                    params_pe(pe)
                    pe.wait_ge(par.vec, 2)
                    norm_pe(pe, n1)
                    ffn_pe(pe, f1, n1, 0, 0)
                    mixer_pe(pe)
                    norm_pe(pe, n2)
                    ffn_pe(pe, f2, n2, C_FFN2, G_FFN2)
            clear_semaphores()


        DH = 4
        HD = 128
        CH = 64
        NS = 16
        (G_Q2, C_Q2), (G_K2, C_K2), (G_V2, C_V2), (G_Z2, C_Z2), (G_U2, C_U2) = [(i, 2 * i) for i in range(5)]
        G_MK, C_MK = 5, 10
        G_MV, C_MV = 7, 14
        G_GLU, C_GLU = 9, 18
        G_WO2, C_WO2 = 10, 19
        G_XQ, C_XQ = 12, 23
        G_XO, C_XO = 14, 27
        G_FFN3, C_FFN3 = 16, 31
        R2 = dict(mix=0, x=8, mem=16, ffn=24, convw=32, dng=80, bglu=81, d=85, are=89, aim=105)
        N_ROWS2 = 121

        rot_c = big(0, NS, TOK)
        rot_s = big(4096, NS, TOK)
        kmT = big(8192, KD, TOK)
        vm = big(10240, MT, D)
        z_s = big(12288, MT, 512)
        uT = big(13312, 4, TOK)
        A0 = 14336
        xpad2 = big(A0, 12, TOK + 3)
        conv2 = big(A0 + 3108, 12, TOK)
        b_in = big(A0, 2, NS, 16)
        c_in = big(A0 + 512, 2, 4, 64)
        bbt = big(A0 + 1024, 4, NS, 16)
        Zb = big(A0 + 2048, 2, NS, 32)
        Zc = big(A0 + 3072, 2, 4, P)
        same = big(A0 + 4096, 7, P)
        X = big(A0, 8, P)
        XT = big(A0 + 1024, 8, P)
        Y = big(A0 + 2048, 8, P)
        CT = big(A0 + 3072, 8, P)
        u_sol = big(A0 + 4096, 8, P)
        wT = big(A0 + 5120, 8, P)
        A1 = A0 + 6180
        q_tok = big(A1, MT, 512)
        k_tok = big(A1 + 1024, MT, 512)
        v_tok2 = big(A1 + 2048, MT, 512)
        kbe = big(A1 + 3072, MT, 512)
        knT = big(A1 + 4096, DH, TOK)
        kbT = big(A1 + 5120, DH, TOK)
        qnT = big(A1 + 6144, DH, TOK)
        qgT = big(A1 + 7168, DH, TOK)
        dec = big(A1 + 8192, 8, P)
        LT = big(A1 + 9216, 8, P)
        attnT = big(A1 + 10240, 8, P)
        kb = big(A1 + 10240, MT, 512)
        memx = big(A1 + 8192, MT, D)
        vnew = big(A1 + 4096, MT, 512)
        S2 = big(A1 + 5120, 512)
        sq2 = big(A1 + 5632, 512)
        o_s = big(A1 + 6144, MT, 512)
        lvl = big(A1 + 11264, 6, P)
        cTi = big(A1 + 12032, 4, P)
        bbT = (ws_in, wsT)
        cT = (gmv[:, :].rearrange("p (c n) -> p c n", c=4), cTi)
        memT = xn[:, :, :].rearrange("p m d -> p (m d)").rearrange("p (k n) -> p k n", k=KD)
        zin = big(A0, 2, 2, TOK)
        zsc = big(A0 + 1024, 2, 2, TOK)
        xst = big(A0 + 2048, 2, 2, TOK)
        tv = big(A0 + 3072, 2, 4, TOK)
        tp = big(A0 + 5120, 4, TOK)
        yg = big(A1, 4, TOK)
        ysig = big(A1 + 1024, 4, TOK)
        qcT = big(A0, KD, TOK)
        pc = big(A0 + 2048, 8, TOK)
        PTc = big(A0 + 4096, 2, 4, TOK)
        fin_g = xT[:, :, :].rearrange("p k n -> p (k n)")[:, 0:D]

        e_tmp = big(33060, 256)
        blk = big(33316, P)
        ublk = big(33444, P)
        s5w = big(33572, 26, NS)
        par2 = sb("par2", [P, 4])
        bet = sb("bet", [P, 8])
        cs2 = sb("cs2", [P, 40])
        st2 = sb("st2", [P, 96])
        small2 = sb("small2", [P, 8])

        p_in, mem_in, fin_in = sem("params2_in"), sem("memory_in"), sem("final_gain_in")
        p2, sp, dn, rc, dt2, xa = (steps(n) for n in ("params2", "s5_params", "delta", "recurrence", "dt2", "cross"))
        mk, c2, iv = steps("masks2", "vec pool"), steps("conv2", "vec act"), steps("inverse", "vec pe")
        s5, gl = steps("s5", "vec pool pe"), steps("glu", "vec act")
        rot = sem("rotations_ready")
        nm, nx, nmem, n3, nf = (steps(n) for n in ("mix2_norm", "cross_norm", "memory_norm", "ffn3_norm", "final_norm"))
        f3 = ffn_sems("ffn3")
        out_done = sem("out_done")

        def params2_act(act):
            n = 0
            for name, r, k in (("norm_mix_g_2", "mix", 8), ("norm_x_g_2", "x", 8), ("norm_mem_g_2", "mem", 8),
                               ("norm_ffn_g_2", "ffn", 8), ("dn_norm_g_2", "dng", 1), ("s5_b_glu_2", "bglu", 4)):
                act.dma_start(vecs[R2[r]:R2[r] + k, :], t[name].rearrange("o (k p) -> (o k) p", p=P)).then_inc(p_in, 16)
                n += 1
            act.dma_start(vecs[R2["convw"]:R2["convw"] + 48, :],
                          t["conv_w_2"].rearrange("o j (k p) -> (o j k) p", p=P)).then_inc(p_in, 16)
            act.dma_start(vecs[R2["d"]:R2["d"] + 4, :],
                          t["s5_d_2"].rearrange("o (k g) c -> (o k) (g c)", g=8)).then_inc(p_in, 16)
            for name, r in (("s5_a_re_2", "are"), ("s5_a_im_2", "aim")):
                act.dma_start(vecs[R2[r]:R2[r] + NS, :],
                              t[name].rearrange("o (k g) p -> (o k) (g p)", g=2)).then_inc(p_in, 16)
            for i, name in enumerate(("s5_b_re_2", "s5_b_im_2")):
                act.dma_start(b_in[:, i], t[name].rearrange("o (k g) p c -> (o g p) k c", g=2)).then_inc(p_in, 16)
            for i, name in enumerate(("s5_c_re_2", "s5_c_im_2")):
                act.dma_start(c_in[:, i], t[name].rearrange("o (k g) c p -> (o g c) k p", g=8)).then_inc(p_in, 16)
            for g in range(2):
                act.dma_start(s5w[64 * g:64 * g + 64, 0, :],
                              t["s5_log_dt_2"].rearrange("o (k g) -> g (o k)", g=2)[g:g + 1, :].broadcast_to([64, NS]),
                              allow_slow_non_contiguous=True).then_inc(p_in, 16)
            act.dma_start(small2[:, 0:4], t["dn_dt_bias_2"].broadcast_to([P, 4])).then_inc(p_in, 16)
            act.dma_start(small2[:, 4:8], t["dn_a_log_2"].broadcast_to([P, 4])).then_inc(p_in, 16)
            act.wait_ge(p_in, 16 * (n + 12))
            act.activation(small2[:, 4:8], small2[:, 4:8], ACT.Exp).then_inc(p2.act, 1)

        def masks_pool(pool):
            pool.memset(Zb, 0.0).then_inc(mk.pool, 1)
            for i in range(1, 7):
                b = 2 ** i
                v = same[:, i].rearrange("p (n b) -> p n b", b=b)
                pool.affine_select(out=v, in_=ones[:, :].rearrange("p (n b) -> p n b", b=b), compare_op=ALU.is_ge,
                                   fill=0.0, base=0, pattern=[[-b, P // b], [0, b]], channel_multiplier=1).then_inc(mk.pool, 1)
            for i in range(1, 7):
                b = 2 ** i
                v = same[:, i].rearrange("p (n b) -> p n b", b=b)
                pool.wait_ge(mk.pool, 1 + i)
                pool.affine_select(out=v, in_=v, compare_op=ALU.is_ge, fill=0.0, base=b - 1,
                                   pattern=[[b, P // b], [0, b]], channel_multiplier=-1).then_inc(mk.pool, 1)

        def masks_vec(vec):
            vec.tensor_copy(same[:, 0], ident[:, :]).then_inc(mk.vec, 1)
            vec.wait_ge(mk.vec, 1)
            vec.wait_ge(mk.pool, 13)
            vec.tensor_copy(blk[:, :], same[:, 6]).then_inc(mk.vec, 1)
            vec.tensor_tensor(ublk[:, :], same[:, 6], upper[:, :], ALU.mult).then_inc(mk.vec, 1)
            vec.tensor_tensor(lvl, same[:, 1:7], same[:, 0:6], ALU.subtract).then_inc(mk.vec, 1)
            vec.wait_ge(mk.vec, 4)
            vec.tensor_tensor(lvl, lvl, upper[:, :].unsqueeze(1).broadcast_to([P, 6, P]), ALU.mult).then_inc(mk.vec, 1)
            vec.tensor_reduce(par2[:, 0:1], same[:, 4, 0:P:32], AX, ALU.add).then_inc(mk.vec, 1)
            vec.wait_ge(mk.vec, 6)
            vec.tensor_scalar(par2[:, 1:2], par2[:, 0:1], -1.0, 1.0, ALU.mult, ALU.add).then_inc(mk.vec, 1)
            vec.wait_ge(mk.vec, 7)
            vec.tensor_scalar(par2[:, 2:4], par2[:, 0:2], -1.0, None, ALU.mult).then_inc(mk.vec, 1)
            vec.wait_ge(mk.vec, 8)

        def params2_pe(pe):
            pe.wait_ge(p2.act, 1)
            pe.transpose(turn[0][:, 0:N_ROWS2], vecs[0:N_ROWS2, :], ident[0:N_ROWS2, 0:N_ROWS2]).then_inc(p2.pe, 1)

        def params2_vec(vec):
            vec.wait_ge(p2.pe, 1)
            vec.tensor_copy(col[:, 0:N_ROWS2], turn[0][:, 0:N_ROWS2]).then_inc(p2.vec, 1)
            vec.tensor_scalar(small2[:, 4:8], small2[:, 4:8], -1.0, None, ALU.mult).then_inc(p2.vec, 1)
            vec.wait_ge(p2.vec, 2)

        LDT, DTS, AR, AI, MAG, KR, SR, CR, SI, CO, ABR, ABI, NR, DEN, T1, T2, COR, COI = range(18)
        PW = 18

        def s5p_act(act):
            act.wait_ge(p2.act, 1)
            act.activation(s5w[:, DTS], s5w[:, LDT], ACT.Exp).then_inc(sp.act, 1)
            act.wait_ge(sp.vec, 1)
            act.activation(s5w[:, MAG], s5w[:, AR], ACT.Exp).then_inc(sp.act, 1)
            act.wait_ge(sp.vec, 2 + SINCOS)
            act.activation(s5w[:, SI], s5w[:, SR], ACT.Sin).then_inc(sp.act, 1)
            act.activation(s5w[:, CO], s5w[:, CR], ACT.Sin).then_inc(sp.act, 1)

        def s5p_vec(vec):
            a_re, a_im = col[:, R2["are"]:R2["are"] + NS], col[:, R2["aim"]:R2["aim"] + NS]

            def w(i):
                return s5w[:, i]
            vec.wait_ge(sp.act, 1)
            vec.tensor_tensor(w(AR), a_re, w(DTS), ALU.mult).then_inc(sp.vec, 1)
            vec.tensor_tensor(w(AI), a_im, w(DTS), ALU.mult).then_inc(sp.vec, 1)
            vec.wait_ge(sp.vec, 2)
            sincos_vec(vec, sp, 2, w(AI), w(KR), w(SR), w(CR))
            vec.wait_ge(sp.act, 4)
            vec.tensor_tensor(w(ABR), w(MAG), w(CO), ALU.mult).then_inc(sp.vec, 1)
            vec.tensor_tensor(w(ABI), w(MAG), w(SI), ALU.mult).then_inc(sp.vec, 1)
            vec.tensor_tensor(w(T1), a_re, a_re, ALU.mult).then_inc(sp.vec, 1)
            vec.tensor_tensor(w(T2), a_im, a_im, ALU.mult).then_inc(sp.vec, 1)
            vec.wait_ge(sp.vec, 15)
            vec.tensor_scalar(w(NR), w(ABR), 1.0, None, ALU.subtract).then_inc(sp.vec, 1)
            vec.tensor_tensor(w(DEN), w(T1), w(T2), ALU.add).then_inc(sp.vec, 1)
            vec.wait_ge(sp.vec, 17)
            vec.reciprocal(w(DEN), w(DEN)).then_inc(sp.vec, 1)
            vec.tensor_tensor(w(T1), w(NR), a_re, ALU.mult).then_inc(sp.vec, 1)
            vec.tensor_tensor(w(T2), w(ABI), a_im, ALU.mult).then_inc(sp.vec, 1)
            vec.wait_ge(sp.vec, 20)
            vec.tensor_tensor(w(COR), w(T1), w(T2), ALU.add).then_inc(sp.vec, 1)
            vec.wait_ge(sp.vec, 21)
            vec.tensor_tensor(w(COR), w(COR), w(DEN), ALU.mult).then_inc(sp.vec, 1)
            vec.tensor_tensor(w(T1), w(ABI), a_re, ALU.mult).then_inc(sp.vec, 1)
            vec.tensor_tensor(w(T2), w(NR), a_im, ALU.mult).then_inc(sp.vec, 1)
            vec.wait_ge(sp.vec, 24)
            vec.tensor_tensor(w(COI), w(T1), w(T2), ALU.subtract).then_inc(sp.vec, 1)
            vec.wait_ge(sp.vec, 25)
            vec.tensor_tensor(w(COI), w(COI), w(DEN), ALU.mult).then_inc(sp.vec, 1)
            vec.wait_ge(sp.vec, 26)
            for i, (b, c) in enumerate(((0, COR), (1, COI), (1, COR), (0, COI))):
                vec.tensor_tensor(bbt[:, i], b_in[:, b], over(s5w[:, c], NS, 16), ALU.mult).then_inc(sp.vec, 1)
            vec.wait_ge(sp.vec, 30)
            vec.wait_ge(mk.pool, 1)
            for g in range(2):
                half = slice(64 * g, 64 * g + 64)
                for i, op in enumerate((ALU.subtract, ALU.add)):
                    vec.tensor_tensor(Zb[half, i, :, 16 * g:16 * g + 16], bbt[half, 2 * i], bbt[half, 2 * i + 1],
                                      op).then_inc(sp.vec, 1)
            for i in range(2):
                for g in range(2):
                    vec.tensor_scalar(Zc[:, i, :, 64 * g:64 * g + 64], c_in[:, i], par2[:, 2 * i + g:2 * i + g + 1], None,
                                      ALU.mult).then_inc(sp.vec, 1)

        def s5p_pe(pe):
            pe.wait_ge(sp.vec, 38)
            for i in range(2):
                for c in range(4):
                    ins = pe.transpose(turn[i][:, c * P:(c + 1) * P],
                                       Zb[:, i, 4 * c:4 * c + 4, :].rearrange("p k c -> p (k c)"), ident[:, :])
                ins.then_inc(sp.pe, 1)
            for i in range(2):
                for c in range(4):
                    ins = pe.transpose(turn[2 + i][:, c * P:(c + 1) * P], Zc[:, i, c, :], ident[:, :])
                ins.then_inc(sp.pe, 1)

        def s5p_vec2(vec):
            for i, dst in enumerate(bbT + cT):
                vec.wait_ge(sp.pe, 1 + i)
                vec.tensor_copy(dst[:, :, :], heads(turn[i][:, :], 4)).then_inc(sp.vec, 1)

        def rotations_pool(pool):
            pool.memset(rot_c[:, :, 0:1], 1.0).then_inc(rot, 1)
            pool.memset(rot_s[:, :, 0:1], 0.0).then_inc(rot, 1)
            pool.wait_ge(sp.act, 4)
            pool.tensor_copy(s5w[:, PW], s5w[:, CO]).then_inc(rot, 1)
            pool.tensor_copy(s5w[:, PW + 1], s5w[:, SI]).then_inc(rot, 1)
            done = 4
            pool.wait_ge(rot, done)
            for k in range(8):
                n = 2 ** k
                pr, pi = s5w[:, PW + 2 * (k % 2)], s5w[:, PW + 1 + 2 * (k % 2)]
                qr, qi = s5w[:, PW + 2 - 2 * (k % 2)], s5w[:, PW + 3 - 2 * (k % 2)]
                tiles = min(NS, 256 // n)
                for t0 in range(0, NS, tiles):
                    ts = slice(t0, t0 + tiles)
                    tmp = e_tmp[:, 0:tiles * n].rearrange("p (k n) -> p k n", k=tiles)
                    er, ei = rot_c[:, ts, 0:n], rot_s[:, ts, 0:n]
                    nr_, ni_ = rot_c[:, ts, n:2 * n], rot_s[:, ts, n:2 * n]
                    c_, s_ = over(pr[:, ts], tiles, n), over(pi[:, ts], tiles, n)
                    pool.tensor_tensor(nr_, er, c_, ALU.mult).then_inc(rot, 1)
                    pool.tensor_tensor(ni_, ei, c_, ALU.mult).then_inc(rot, 1)
                    pool.tensor_tensor(tmp, ei, s_, ALU.mult).then_inc(rot, 1)
                    done += 3
                    pool.wait_ge(rot, done)
                    pool.tensor_tensor(nr_, nr_, tmp, ALU.subtract).then_inc(rot, 1)
                    done += 1
                    pool.wait_ge(rot, done)
                    pool.tensor_tensor(tmp, er, s_, ALU.mult).then_inc(rot, 1)
                    done += 1
                    pool.wait_ge(rot, done)
                    pool.tensor_tensor(ni_, ni_, tmp, ALU.add).then_inc(rot, 1)
                    done += 1
                    pool.wait_ge(rot, done)
                if k < 7:
                    for i, (a, b) in enumerate(((pr, pr), (pi, pi), (pr, pi), (pr, pi))):
                        pool.tensor_tensor(s5w[:, PW + 4 + i], a, b, ALU.mult).then_inc(rot, 1)
                    done += 4
                    pool.wait_ge(rot, done)
                    pool.tensor_tensor(qr, s5w[:, PW + 4], s5w[:, PW + 5], ALU.subtract).then_inc(rot, 1)
                    pool.tensor_tensor(qi, s5w[:, PW + 6], s5w[:, PW + 7], ALU.add).then_inc(rot, 1)
                    done += 2
                    pool.wait_ge(rot, done)

        ROT_DONE = 4 + sum(6 * max(1, NS * 2 ** k // 256) for k in range(8)) + 6 * 7

        def second_sync(sync):
            def cols(name, lo, hi, k0, k1):
                return t[name][:, k0 * P:k1 * P, lo:hi].rearrange("o (k p) n -> p (o k) n", p=P)

            def two(c, name, lo, n):
                for i in range(2):
                    load(sync, c + i, cols(name, lo, lo + n, 4 * i, 4 * i + 4), 4, n)
            sync.dma_start(memx, t["mem_2"].rearrange("o (m p) d -> p (o m) d", p=P)).then_inc(mem_in, 16)
            two(C_Q2, "w_in_2", 0, 512)
            two(C_K2, "w_in_2", 512, 512)
            two(C_V2, "w_in_2", 1024, 512)
            two(C_Z2, "w_in_2", 1536, 520)
            two(C_U2, "w_in_2", 2056, 512)
            for i in range(2):
                two(C_MK + 2 * i, "w_xk_2", 512 * i, 512)
            for i in range(2):
                two(C_MV + 2 * i, "w_xv_2", 512 * i, 512)
            load(sync, C_GLU, cols("s5_w_glu_2", 0, 512, 0, 4), 4, 512)
            for i in range(2):
                two(C_WO2 + 2 * i, "w_out_2", 512 * i, 512)
            for i in range(2):
                two(C_XQ + 2 * i, "w_xq_2", 512 * i, 512)
            for i in range(2):
                two(C_XO + 2 * i, "w_xo_2", 512 * i, 512)

            def part(name):
                return lambda j: t[name][:, :, bass.ds(FB * j, FB)].rearrange("o (k p) n -> p (o k) n", p=P)
            ffn_sync(sync, f3, C_FFN3, part("w_gate_2"), part("w_up_2"),
                     lambda i: t["w_down_2"][:, 2 * P * i:2 * P * (i + 1), :].rearrange("o (k p) n -> p (o k) n", p=P))

        CONV_GROUPS = ((G_Q2, C_Q2), (G_K2, C_K2), (G_V2, C_V2))

        def conv2_act1(act):
            act.wait_ge(sp.pe, 4)
            act.wait_ge(mk.vec, 8)
            act.wait_ge(c2.vec, 1)
            for i, (G, c) in enumerate(CONV_GROUPS):
                wait_products(act, c + 1)
                for q in range(2):
                    f = 4 * i + 2 * q
                    act.activation(xpad2[:, f:f + 2, 3:3 + TOK], heads(acc[bank(G, q)][:, :], 2),
                                   ACT.Copy).then_inc(acc_read[bank(G, q)], 1)

        def conv2_vec(vec):
            for j in range(4):
                for f in range(12):
                    w = col[:, R2["convw"] + 12 * j + f:R2["convw"] + 12 * j + f + 1]
                    if j == 0:
                        wait_acc_read(vec, CONV_GROUPS[f // 4][0], (f % 4) // 2)
                        vec.tensor_scalar(conv2[:, f, :], xpad2[:, f, 0:TOK], w, None, ALU.mult).then_inc(c2.vec, 1)
                    else:
                        vec.wait_ge(c2.vec, 1 + 12 * (j - 1) + f + 1)
                        vec.scalar_tensor_tensor(out=conv2[:, f, :], in0=xpad2[:, f, j:j + TOK], scalar=w,
                                                 in1=conv2[:, f, :], op0=ALU.mult, op1=ALU.add).then_inc(c2.vec, 1)

        def conv2_act2(act):
            for i in range(3):
                act.wait_ge(c2.vec, 37 + 4 * i + 4)
                act.activation(conv2[:, 4 * i:4 * i + 4, :], conv2[:, 4 * i:4 * i + 4, :], ACT.Silu).then_inc(c2.act, 1)

        def ab_pe(pe):
            wait_chunk(pe, C_Z2)
            wait_chunk(pe, C_Z2 + 1)
            for m in range(MT):
                for k in range(KD):
                    ins = pe.matmul(turn[m][:, 0:8], xT[:, k, m * P:(m + 1) * P],
                                    slot(C_Z2 + k // 4, 4, 520)[:, k % 4, 512:520], start=(k == 0), stop=(k == KD - 1))
                ins.then_inc(dt2.pe, 1)

        def ab_vec(vec):
            for m in range(MT):
                vec.wait_ge(dt2.pe, 1 + m)
                vec.tensor_tensor(dtw[:, 0, 4 * m:4 * m + 4], turn[m][:, 0:4], small2[:, 0:4], ALU.add).then_inc(dt2.vec, 1)
            softplus_vec(vec, dt2, dtw, 8, 2)
            vec.tensor_tensor(heads(dtw[:, 11, 0:8], MT), heads(dtw[:, 10, 0:8], MT),
                              small2[:, 4:8].unsqueeze(1).broadcast_to([P, MT, 4]), ALU.mult).then_inc(dt2.vec, 1)

        def ab_act(act):
            softplus_act(act, dt2, dtw, 8, 2)
            for m in range(MT):
                act.activation(bet[:, 4 * m:4 * m + 4], turn[m][:, 4:8], ACT.Sigmoid).then_inc(dt2.act, 1)

        g2 = dtw[:, 11, 0:8]
        GC, TOT, ALC, EG, ED = 0, 8, 16, 32, 8

        def dn_cs_pe(pe):
            pe.wait_ge(dt2.vec, 16)
            pe.wait_ge(dt2.act, 4)
            pe.wait_ge(sp.vec, 42)
            pe.matmul(turn[2][:, 0:8], ublk[:, :], g2, start=True, stop=True)
            pe.matmul(turn[2][:, 8:16], blk[:, :], g2, start=True, stop=True)
            for b in range(2):
                ins = pe.matmul(turn[2][:, 16 + 8 * b:24 + 8 * b], blk[:, CH * b:CH * b + 1].broadcast_to([P, P]), g2,
                                start=True, stop=True)
            ins.then_inc(dn.pe, 1)
            for m in range(MT):
                for h in range(DH):
                    j = 4 * m + h
                    ins = pe.matmul(turn[m][:, h * P:(h + 1) * P], g2[:, j:j + 1].broadcast_to([P, P]), ublk[:, :],
                                    start=True, stop=True)
                ins.then_inc(dn.pe, 1)

        def dn_cs_vec(vec):
            vec.wait_ge(dn.pe, 1)
            vec.tensor_copy(cs2[:, 0:32], turn[2][:, 0:32]).then_inc(dn.vec, 1)
            vec.wait_ge(dn.vec, 1)
            vec.tensor_tensor(cs2[:, 8:16], cs2[:, 8:16], cs2[:, 0:8], ALU.subtract).then_inc(dn.vec, 1)
            vec.wait_ge(nmem.pe, 4)
            for m in range(MT):
                vec.wait_ge(dn.pe, 2 + m)
                for h in range(DH):
                    j = 4 * m + h
                    ins = vec.tensor_scalar(dec[:, j, :], turn[m][:, h * P:(h + 1) * P], cs2[:, j:j + 1], 0.0,
                                            ALU.subtract, ALU.min)
                ins.then_inc(dn.vec, 1)

        def dn_cs_act(act):
            act.wait_ge(dn.vec, 2)
            act.activation(cs2[:, 32:40], cs2[:, 0:8], ACT.Exp).then_inc(dn.act, 1)
            act.activation(cs2[:, 8:32], cs2[:, 8:32], ACT.Exp).then_inc(dn.act, 1)
            for m in range(MT):
                act.wait_ge(dn.vec, 3 + m)
                act.activation(dec[:, 4 * m:4 * m + 4, :], dec[:, 4 * m:4 * m + 4, :], ACT.Exp).then_inc(dn.act, 1)

        def dn_turn_pe(pe):
            pe.wait_ge(dn.vec, 4)
            for kind in range(3):
                pe.wait_ge(c2.act, 1 + kind)
                for m in range(MT):
                    r = 2 * kind + m
                    if r >= 4:
                        pe.wait_ge(dn.vec, 5 + r - 4)
                    for f in range(4):
                        ins = pe.transpose(turn[r % 4][:, f * P:(f + 1) * P], conv2[:, 4 * kind + f, m * P:(m + 1) * P], ident[:, :])
                    ins.then_inc(dn.pe, 1)

        def dn_turn_vec(vec):
            for r in range(6):
                kind, m = r // 2, r % 2
                vec.wait_ge(dn.pe, 4 + r)
                vec.tensor_copy((q_tok, k_tok, v_tok2)[kind][:, m, :], turn[r % 4][:, :]).then_inc(dn.vec, 1)
            for r in range(4):
                vec.wait_ge(dn.act, 5 + r)
                vec.tensor_reduce(st2[:, 4 * r:4 * r + 4], heads((kbe, kb)[r // 2][:, r % 2, :], 4), AX, ALU.add).then_inc(dn.vec, 1)
            vec.wait_ge(dn.act, 9)
            vec.reciprocal(st2[:, 16:32], st2[:, 16:32]).then_inc(dn.vec, 1)
            vec.wait_ge(dn.vec, 15)
            vec.tensor_scalar(st2[:, 16:24], st2[:, 16:24], HD ** -0.5, None, ALU.mult).then_inc(dn.vec, 1)
            vec.wait_ge(dn.vec, 16)
            for r in range(4):
                d = (q_tok, k_tok)[r // 2][:, r % 2, :]
                vec.tensor_tensor(heads(d, 4), heads(d, 4), over(st2[:, 16 + 4 * r:20 + 4 * r], 4, P), ALU.mult).then_inc(dn.vec, 1)
            vec.wait_ge(dt2.act, 4)
            for m in range(MT):
                vec.wait_ge(dn.vec, 19 + m)
                vec.tensor_tensor(heads(kb[:, m, :], 4), heads(k_tok[:, m, :], 4), over(bet[:, 4 * m:4 * m + 4], 4, P),
                                  ALU.mult).then_inc(dn.vec, 1)
            vec.wait_ge(dn.act, 4)
            for m in range(MT):
                d = dec[:, 4 * m:4 * m + 4, :]
                vec.tensor_tensor(d, d, ublk[:, :].unsqueeze(1).broadcast_to([P, 4, P]), ALU.mult).then_inc(dn.vec, 1)

        def dn_turn_act(act):
            for r in range(4):
                act.wait_ge(dn.vec, 5 + r)
                act.activation((kbe, kb)[r // 2][:, r % 2, :], (q_tok, k_tok)[r // 2][:, r % 2, :], ACT.Square).then_inc(dn.act, 1)
            act.wait_ge(dn.vec, 14)
            act.activation(st2[:, 16:32], st2[:, 0:16], ACT.Sqrt, bias=eps_col[:, 0:1]).then_inc(dn.act, 1)

        def dn_turn2_pe(pe):
            for i, (src, w) in enumerate(((k_tok, 19), (kb, 21), (q_tok, 17))):
                for m in range(MT):
                    r = 2 * i + m
                    pe.wait_ge(dn.vec, w + m)
                    if r >= 4:
                        pe.wait_ge(dn.vec, 25 + r - 4)
                    for h in range(DH):
                        ins = pe.transpose(turn[r % 4][:, h * P:(h + 1) * P], src[:, m, h * P:(h + 1) * P], ident[:, :])
                    ins.then_inc(dn.pe, 1)

        def dn_turn2_vec(vec):
            for r in range(6):
                vec.wait_ge(dn.pe, 10 + r)
                vec.tensor_copy((knT, kbT, qnT)[r // 2][:, :, (r % 2) * P:(r % 2 + 1) * P], heads(turn[r % 4][:, :], 4)).then_inc(dn.vec, 1)
            vec.wait_ge(dn.act, 2)
            for m in range(MT):
                eg = over(cs2[:, EG + 4 * m:EG + 4 * m + 4], 4, P)
                vec.tensor_tensor(heads(q_tok[:, m, :], 4), heads(q_tok[:, m, :], 4), eg, ALU.mult).then_inc(dn.vec, 1)
                vec.tensor_tensor(heads(kbe[:, m, :], 4), heads(kb[:, m, :], 4), eg, ALU.mult).then_inc(dn.vec, 1)
                vec.tensor_tensor(heads(k_tok[:, m, :], 4), heads(k_tok[:, m, :], 4),
                                  over(cs2[:, ED + 4 * m:ED + 4 * m + 4], 4, P), ALU.mult).then_inc(dn.vec, 1)
                vec.tensor_tensor(heads(v_tok2[:, m, :], 4), heads(v_tok2[:, m, :], 4),
                                  over(bet[:, 4 * m:4 * m + 4], 4, P), ALU.mult).then_inc(dn.vec, 1)

        def dn_kk_pe(pe):
            pe.wait_ge(dn.vec, 30)
            for m in range(MT):
                for h in range(DH):
                    ins = pe.matmul(turn[m][:, h * P:(h + 1) * P], knT[:, h, m * P:(m + 1) * P], kbT[:, h, m * P:(m + 1) * P],
                                    start=True, stop=True)
                ins.then_inc(dn.pe, 1)
            for m in range(MT):
                for h in range(DH):
                    ins = pe.matmul(turn[2 + m][:, h * P:(h + 1) * P], knT[:, h, m * P:(m + 1) * P], qnT[:, h, m * P:(m + 1) * P],
                                    start=True, stop=True)
                ins.then_inc(dn.pe, 1)

        def dn_kk_vec(vec):
            vec.wait_ge(dn.vec, 36)
            for m in range(MT):
                vec.wait_ge(dn.pe, 16 + m)
                vec.tensor_tensor(LT[:, 4 * m:4 * m + 4, :], dec[:, 4 * m:4 * m + 4, :], heads(turn[m][:, :], 4),
                                  ALU.mult).then_inc(dn.vec, 1)
            for m in range(MT):
                vec.wait_ge(dn.pe, 18 + m)
                vec.tensor_tensor(attnT[:, 4 * m:4 * m + 4, :], dec[:, 4 * m:4 * m + 4, :], heads(turn[2 + m][:, :], 4),
                                  ALU.mult).then_inc(dn.vec, 1)

        def dn_qg_pe(pe):
            pe.wait_ge(dn.vec, 42)
            for m in range(MT):
                for h in range(DH):
                    ins = pe.transpose(turn[2 + m][:, h * P:(h + 1) * P], q_tok[:, m, h * P:(h + 1) * P], ident[:, :])
                ins.then_inc(dn.pe, 1)

        def dn_qg_vec(vec):
            for m in range(MT):
                vec.wait_ge(dn.pe, 20 + m)
                vec.tensor_copy(qgT[:, :, m * P:(m + 1) * P], heads(turn[2 + m][:, :], 4)).then_inc(dn.vec, 1)

        def mlvl(i):
            return lvl[:, i].unsqueeze(1).broadcast_to([P, 4, P])

        def quad(a, m):
            return a[:, 4 * m:4 * m + 4, :]

        def inv_vec(vec):
            vec.wait_ge(dn.vec, 42)
            for m in range(MT):
                vec.tensor_tensor(quad(CT, m), quad(LT, m), mlvl(0), ALU.mult).then_inc(iv.vec, 1)
                vec.wait_ge(iv.vec, 1 + 2 * m)
                vec.tensor_tensor(quad(XT, m), ident[:, :].unsqueeze(1).broadcast_to([P, 4, P]), quad(CT, m),
                                  ALU.subtract).then_inc(iv.vec, 1)
            for m in range(MT):
                vec.wait_ge(iv.pe, 1 + m)
                vec.tensor_copy(quad(X, m), heads(turn[m][:, :], 4)).then_inc(iv.vec, 1)
            for i in range(1, 6):
                v, p = 6 + 8 * (i - 1), 2 + 4 * (i - 1)
                for m in range(MT):
                    vec.tensor_tensor(quad(CT, m), quad(LT, m), mlvl(i), ALU.mult).then_inc(iv.vec, 1)
                for m in range(MT):
                    vec.wait_ge(iv.pe, p + 1 + m)
                    vec.tensor_copy(quad(Y, m), heads(turn[m][:, :], 4)).then_inc(iv.vec, 1)
                for m in range(MT):
                    vec.wait_ge(iv.pe, p + 3 + m)
                    vec.tensor_tensor(quad(XT, m), quad(XT, m), heads(turn[2 + m][:, :], 4), ALU.subtract).then_inc(iv.vec, 1)
                    vec.tensor_tensor(quad(X, m), quad(X, m), heads(turn[m][:, :], 4), ALU.subtract).then_inc(iv.vec, 1)

        INV_DONE = 6 + 8 * 5

        def inv_pe(pe):
            for m in range(MT):
                pe.wait_ge(iv.vec, 2 + 2 * m)
                for h in range(DH):
                    ins = pe.transpose(turn[m][:, h * P:(h + 1) * P], XT[:, 4 * m + h, :], ident[:, :])
                ins.then_inc(iv.pe, 1)
            for i in range(1, 6):
                v = 6 + 8 * (i - 1)
                for m in range(MT):
                    pe.wait_ge(iv.vec, v + 1 + m)
                    for h in range(DH):
                        j = 4 * m + h
                        ins = pe.matmul(turn[m][:, h * P:(h + 1) * P], CT[:, j, :], X[:, j, :], start=True, stop=True)
                    ins.then_inc(iv.pe, 1)
                for m in range(MT):
                    pe.wait_ge(iv.vec, v + 3 + m)
                    if i == 1:
                        pe.wait_ge(dn.vec, 44)
                    for h in range(DH):
                        j = 4 * m + h
                        pe.matmul(turn[2 + m][:, h * P:(h + 1) * P], Y[:, j, :], XT[:, j, :], start=True, stop=True)
                    for h in range(DH):
                        j = 4 * m + h
                        ins = pe.matmul(turn[m][:, h * P:(h + 1) * P], XT[:, j, :], Y[:, j, :], start=True, stop=True)
                    ins.then_inc(iv.pe, 1)

        def rc_pe(pe):
            pe.wait_ge(iv.vec, INV_DONE)
            for m in range(MT):
                for h in range(DH):
                    ins = pe.matmul(turn[m][:, h * P:(h + 1) * P], XT[:, 4 * m + h, :], v_tok2[:, m, h * P:(h + 1) * P],
                                    start=True, stop=True)
                ins.then_inc(rc.pe, 1)
            for m in range(MT):
                for h in range(DH):
                    ins = pe.matmul(turn[2 + m][:, h * P:(h + 1) * P], kbe[:, m, h * P:(h + 1) * P], XT[:, 4 * m + h, :],
                                    start=True, stop=True)
                ins.then_inc(rc.pe, 1)
            for n in range(4):
                m, b = n // 2, n % 2
                rows = slice(CH * b, CH * b + CH)
                if n > 0:
                    pe.wait_ge(rc.vec, 6 if n == 1 else 3 * n + 3)
                    for h in range(DH):
                        ins = pe.matmul(turn[0][rows, h * P:(h + 1) * P], wT[:, 4 * m + h, rows], S2[:, h * P:(h + 1) * P],
                                        start=True, stop=True)
                    ins.then_inc(rc.pe, 1)
                pe.wait_ge(rc.vec, 5 + 3 * n)
                for h in range(DH):
                    o = turn[1][rows, h * P:(h + 1) * P]
                    if n > 0:
                        pe.matmul(o, qgT[:, h, m * P + CH * b:m * P + CH * b + CH], S2[:, h * P:(h + 1) * P],
                                  start=True, stop=False)
                    ins = pe.matmul(o, attnT[rows, 4 * m + h, rows], vnew[rows, m, h * P:(h + 1) * P],
                                    start=(n == 0), stop=True)
                ins.then_inc(rc.pe, 1)
                if n < 3:
                    for h in range(DH):
                        ins = pe.matmul(turn[2][:, h * P:(h + 1) * P], k_tok[rows, m, h * P:(h + 1) * P],
                                        vnew[rows, m, h * P:(h + 1) * P], start=True, stop=True)
                    ins.then_inc(rc.pe, 1)

        def rc_vec(vec):
            for m in range(MT):
                vec.wait_ge(rc.pe, 1 + m)
                vec.tensor_copy(quad(u_sol, m), heads(turn[m][:, :], 4)).then_inc(rc.vec, 1)
            for m in range(MT):
                vec.wait_ge(rc.pe, 3 + m)
                vec.tensor_copy(quad(wT, m), heads(turn[2 + m][:, :], 4)).then_inc(rc.vec, 1)
            vec.wait_ge(rc.vec, 4)
            for n in range(4):
                m, b = n // 2, n % 2
                rows = slice(CH * b, CH * b + CH)
                v = vnew[rows, m, :].rearrange("p (h d) -> p h d", h=4)
                u = u_sol[rows, 4 * m:4 * m + 4, :]
                if n == 0:
                    vec.tensor_copy(v, u).then_inc(rc.vec, 1)
                else:
                    vec.wait_ge(rc.pe, 4 + 3 * n)
                    vec.tensor_tensor(v, u, turn[0][rows, :].rearrange("p (h d) -> p h d", h=4), ALU.subtract).then_inc(rc.vec, 1)
                if n < 3:
                    vec.wait_ge(rc.pe, 6 + 3 * n)
                    if n == 0:
                        ins = vec.tensor_copy(S2, turn[2][:, :])
                    else:
                        for h in range(DH):
                            a = ALC + 8 * b + 4 * m + h
                            sh = S2[:, h * P:(h + 1) * P]
                            ins = vec.scalar_tensor_tensor(out=sh, in0=sh, scalar=cs2[:, a:a + 1],
                                                           in1=turn[2][:, h * P:(h + 1) * P], op0=ALU.mult, op1=ALU.add)
                    ins.then_inc(rc.vec, 1)
                else:
                    vec.wait_ge(rc.pe, 14)
                vec.tensor_copy(o_s[rows, m, :], turn[1][rows, :]).then_inc(rc.vec, 1)
            for m in range(MT):
                vec.wait_ge(rc.act, 1 + m)
                vec.tensor_reduce(st2[:, 32 + 4 * m:36 + 4 * m], heads(kbe[:, m, :], 4), AX, ALU.add).then_inc(rc.vec, 1)
            vec.wait_ge(rc.act, 3)
            vec.reciprocal(st2[:, 40:48], st2[:, 40:48]).then_inc(rc.vec, 1)
            vec.wait_ge(rc.vec, 18)
            for m in range(MT):
                vec.tensor_tensor(heads(o_s[:, m, :], 4), heads(o_s[:, m, :], 4), over(st2[:, 40 + 4 * m:44 + 4 * m], 4, P),
                                  ALU.mult).then_inc(rc.vec, 1)
            for m in range(MT):
                vec.wait_ge(rc.vec, 19 + m)
                wait_acc_read(vec, G_Z2, m)
                vec.tensor_tensor(o_s[:, m, :], o_s[:, m, :], z_s[:, m, :], ALU.mult).then_inc(rc.vec, 1)
            for m in range(MT):
                vec.wait_ge(rc.pe, 15 + m)
                vec.tensor_tensor(xT[:, 0:4, m * P:(m + 1) * P], heads(turn[m][:, :], 4),
                                  col[:, R2["dng"]:R2["dng"] + 1].unsqueeze(2).broadcast_to([P, 4, P]), ALU.mult).then_inc(rc.vec, 1)

        def rc_act(act):
            act.wait_ge(rc.vec, 15)
            for m in range(MT):
                act.activation(kbe[:, m, :], o_s[:, m, :], ACT.Square).then_inc(rc.act, 1)
            act.wait_ge(rc.vec, 17)
            act.activation(st2[:, 40:48], st2[:, 32:40], ACT.Sqrt, bias=eps_col[:, 0:1], scale=1.0 / HD).then_inc(rc.act, 1)

        def rc_out_pe(pe):
            for m in range(MT):
                pe.wait_ge(rc.vec, 21 + m)
                for h in range(DH):
                    ins = pe.transpose(turn[m][:, h * P:(h + 1) * P], o_s[:, m, h * P:(h + 1) * P], ident[:, :])
                ins.then_inc(rc.pe, 1)

        def y_step(k):
            return 3 + 2 * k if k < 15 else 32

        def bu_step(k):
            return 1 + k if k < 2 else 2 * k

        def s5_bu_pe(pe, k):
            c, j = k // 4, k % 4
            rows = slice(32 * j, 32 * j + 32)
            pe.wait_ge(s5.vec, 6 * (k - 2) + 2) if k >= 2 else pe.wait_ge(rc.vec, 24)
            for i in range(2):
                ins = pe.matmul(turn[k % 2][:, i * TOK:(i + 1) * TOK], bbT[i][rows, c, :], uT[rows, c, :], start=True, stop=True)
            ins.then_inc(s5.pe, 1)

        def s5_pe(pe):
            for q in range(2):
                wait_acc_read(pe, G_U2, q)
            s5_bu_pe(pe, 0)
            s5_bu_pe(pe, 1)
            for k in range(NS):
                c, j = k // 4, k % 4
                if j == 0 and c >= 2:
                    pe.wait_ge(gl.vec, c - 1)
                pe.wait_ge(s5.pool, 4 * k + 4)
                for i in range(2):
                    ins = pe.matmul(turn[2 + c % 2][32 * j:32 * j + 32, 0:TOK], cT[i][:, c, 32 * j:32 * j + 32],
                                    xst[:, k % 2, i, :], start=(i == 0), stop=(i == 1))
                ins.then_inc(s5.pe, 1)
                if k + 2 < NS:
                    s5_bu_pe(pe, k + 2)

        def s5_y_vec(vec, c):
            vec.wait_ge(s5.pe, y_step(4 * c + 3))
            vec.scalar_tensor_tensor(out=yg[:, c, :], in0=uT[:, c, :], scalar=col[:, R2["d"] + c:R2["d"] + c + 1],
                                     in1=turn[2 + c % 2][:, 0:TOK], op0=ALU.mult, op1=ALU.add).then_inc(gl.vec, 1)

        def s5_vec(vec):
            vec.wait_ge(rot, ROT_DONE)
            for k in range(NS):
                b = k % 2
                bu = turn[b][:, :].rearrange("p (i n) -> p i n", i=2)
                vec.wait_ge(s5.pe, bu_step(k))
                vec.tensor_tensor(tv[:, b, 0:2, :], bu, rot_c[:, k, :].unsqueeze(1).broadcast_to([P, 2, TOK]), ALU.mult).then_inc(s5.vec, 1)
                vec.tensor_tensor(tv[:, b, 2:4, :], bu, rot_s[:, k, :].unsqueeze(1).broadcast_to([P, 2, TOK]), ALU.mult).then_inc(s5.vec, 1)
                vec.wait_ge(s5.vec, 6 * k + 2)
                vec.tensor_tensor(zin[:, b, 0, :], tv[:, b, 0, :], tv[:, b, 3, :], ALU.add).then_inc(s5.vec, 1)
                vec.tensor_tensor(zin[:, b, 1, :], tv[:, b, 1, :], tv[:, b, 2, :], ALU.subtract).then_inc(s5.vec, 1)
                if k >= 2:
                    vec.wait_ge(s5.pool, 4 * (k - 2) + 2)
                for i in range(2):
                    vec.wait_ge(s5.vec, 6 * k + 3 + i)
                    vec.tensor_tensor_scan(zsc[:, b, i, :], s5w[:, MAG, k:k + 1].broadcast_to([P, TOK]), zin[:, b, i, :],
                                           0.0, ALU.mult, ALU.add).then_inc(s5.vec, 1)
                if k >= 5 and k % 4 == 1:
                    s5_y_vec(vec, (k - 5) // 4)
            s5_y_vec(vec, 3)

        def s5_pool(pool):
            for k in range(NS):
                b = k % 2
                pool.wait_ge(s5.vec, 6 * k + 6)
                if k > 0:
                    pool.wait_ge(s5.pool, 4 * k)
                pool.tensor_tensor(tp[:, 0:2, :], zsc[:, b], rot_c[:, k, :].unsqueeze(1).broadcast_to([P, 2, TOK]), ALU.mult).then_inc(s5.pool, 1)
                pool.tensor_tensor(tp[:, 2:4, :], zsc[:, b], rot_s[:, k, :].unsqueeze(1).broadcast_to([P, 2, TOK]), ALU.mult).then_inc(s5.pool, 1)
                pool.wait_ge(s5.pool, 4 * k + 2)
                if k >= 2:
                    pool.wait_ge(s5.pe, y_step(k - 2))
                pool.tensor_tensor(xst[:, b, 0, :], tp[:, 0, :], tp[:, 3, :], ALU.subtract).then_inc(s5.pool, 1)
                pool.tensor_tensor(xst[:, b, 1, :], tp[:, 1, :], tp[:, 2, :], ALU.add).then_inc(s5.pool, 1)

        def glu_act(act):
            for c in range(4):
                act.wait_ge(gl.vec, 1 + c)
                act.activation(yg[:, c, :], yg[:, c, :], ACT.Gelu_apprx_tanh).then_inc(gl.act, 1)
            wait_products(act, C_GLU)
            for f in range(4):
                ins = act.activation(ysig[:, f, :], acc[bank(G_GLU, f // 2)][:, (f % 2) * TOK:(f % 2 + 1) * TOK], ACT.Sigmoid,
                                     bias=col[:, R2["bglu"] + f:R2["bglu"] + f + 1])
                if f % 2 == 1:
                    ins.then_inc(acc_read[bank(G_GLU, f // 2)], 1)

        def glu_vec(vec):
            for q in range(2):
                wait_acc_read(vec, G_GLU, q)
                vec.tensor_tensor(xT[:, 4 + 2 * q:6 + 2 * q, :], yg[:, 2 * q:2 * q + 2, :], ysig[:, 2 * q:2 * q + 2, :],
                                  ALU.mult).then_inc(gl.vec, 1)

        XS = 256 ** -0.5

        def feat_act(act, G, c, dst, f):
            wait_products(act, c + 1)
            for q in range(2):
                act.activation(dst[:, f + 2 * q:f + 2 * q + 2, :], heads(acc[bank(G, q)][:, :], 2),
                               ACT.Copy).then_inc(acc_read[bank(G, q)], 1)

        def mv_act(act, n):
            wait_products(act, C_MV + 2 * n + 1)
            for m in range(MT):
                act.activation(vm[:, m, n * 512:(n + 1) * 512], acc[bank(G_MV + n, m)][:, :],
                               ACT.Copy).then_inc(acc_read[bank(G_MV + n, m)], 1)

        def xa_scores_pe(pe):
            for G in (G_MK, G_MK + 1, G_XQ, G_XQ + 1):
                for q in range(2):
                    wait_acc_read(pe, G, q)
            for r in range(4):
                m, hp = r // 2, r % 2
                for h2 in range(2):
                    f = 2 * (2 * hp + h2)
                    for k in range(2):
                        ins = pe.matmul(turn[r][:, h2 * TOK:(h2 + 1) * TOK], qcT[:, f + k, m * P:(m + 1) * P], kmT[:, f + k, :],
                                        start=(k == 0), stop=(k == 1))
                ins.then_inc(xa.pe, 1)

        def xa_vec1(vec):
            for r in range(4):
                vec.wait_ge(xa.pe, 1 + r)
                vec.tensor_reduce(st2[:, 48 + 2 * r:50 + 2 * r], heads(turn[r][:, :], 2), AX, ALU.max).then_inc(xa.vec, 1)
            vec.wait_ge(xa.vec, 4)
            vec.tensor_scalar(st2[:, 56:64], st2[:, 48:56], -XS, None, ALU.mult).then_inc(xa.vec, 1)
            vec.wait_ge(xa.act, 8)
            vec.reciprocal(st2[:, 72:80], st2[:, 64:72]).then_inc(xa.vec, 1)
            vec.wait_ge(xa.vec, 6)
            for m in range(MT):
                vec.tensor_tensor(quad(pc, m), quad(pc, m), over(st2[:, 72 + 4 * m:76 + 4 * m], 4, TOK), ALU.mult).then_inc(xa.vec, 1)

        def xa_act(act):
            act.wait_ge(xa.vec, 5)
            for j in range(8):
                act.activation(pc[:, j, :], turn[j // 2][:, (j % 2) * TOK:(j % 2 + 1) * TOK], ACT.Exp,
                               bias=st2[:, 56 + j:57 + j], scale=XS, accum_out=st2[:, 64 + j:65 + j]).then_inc(xa.act, 1)

        def xa_turn_pe(pe):
            for r in range(4):
                m, kb_ = r // 2, r % 2
                pe.wait_ge(xa.vec, 7 + m)
                for h in range(4):
                    ins = pe.transpose(turn[r][:, h * P:(h + 1) * P], pc[:, 4 * m + h, kb_ * P:(kb_ + 1) * P], ident[:, :])
                ins.then_inc(xa.pe, 1)

        def xa_vec2(vec):
            for r in range(4):
                m, kb_ = r // 2, r % 2
                vec.wait_ge(xa.pe, 5 + r)
                vec.tensor_copy(PTc[:, kb_, :, m * P:(m + 1) * P], heads(turn[r][:, :], 4)).then_inc(xa.vec, 1)
            for r in range(4):
                vec.wait_ge(xa.pe, 9 + r)
                vec.tensor_copy(xT[:, 2 * r:2 * r + 2, :], heads(turn[r][:, :], 2)).then_inc(xa.vec, 1)

        def xa_pv_pe(pe):
            pe.wait_ge(xa.vec, 12)
            for f in range(8):
                for k in range(2):
                    ins = pe.matmul(turn[f // 2][:, (f % 2) * TOK:(f % 2 + 1) * TOK], vm[:, k, f * P:(f + 1) * P],
                                    PTc[:, k, f // 2, :], start=(k == 0), stop=(k == 1))
                if f % 2 == 1:
                    ins.then_inc(xa.pe, 1)

        def second_pe(pe):
            pe.sem_inc(products_done, RING)
            params2_pe(pe)
            pe.wait_ge(p2.vec, 2)
            norm_pe(pe, nm)
            pe.wait_ge(nm.vec, NORM_DONE)
            turned_group_pe(pe, G_Q2, C_Q2, xT, 4, 512)
            s5p_pe(pe)
            turned_group_pe(pe, G_K2, C_K2, xT, 4, 512)
            norm_pe(pe, nmem, nb=memx)
            turned_group_pe(pe, G_V2, C_V2, xT, 4, 512)
            pe.wait_ge(nmem.vec, NORM_DONE)
            ab_pe(pe)
            group_pe(pe, G_Z2, C_Z2, xT, (4, 4), 520, n_used=512)
            turned_group_pe(pe, G_U2, C_U2, xT, 4, 512)
            turned_group_pe(pe, G_MK, C_MK, memT, 4, 512)
            dn_cs_pe(pe)
            turned_group_pe(pe, G_MK + 1, C_MK + 2, memT, 4, 512)
            dn_turn_pe(pe)
            group_pe(pe, G_MV, C_MV, memT, (4, 4), 512)
            dn_turn2_pe(pe)
            dn_kk_pe(pe)
            dn_qg_pe(pe)
            group_pe(pe, G_MV + 1, C_MV + 2, memT, (4, 4), 512)
            inv_pe(pe)
            rc_pe(pe)
            rc_out_pe(pe)
            s5_pe(pe)
            pe.wait_ge(gl.act, 4)
            turned_group_pe(pe, G_GLU, C_GLU, yg, 4, 512, K=4)
            pe.wait_ge(gl.vec, 6)
            group_pe(pe, G_WO2, C_WO2, xT, (4, 4), 512)
            group_pe(pe, G_WO2 + 1, C_WO2 + 2, xT, (4, 4), 512)
            norm_pe(pe, nx)
            pe.wait_ge(nx.vec, NORM_DONE)
            turned_group_pe(pe, G_XQ, C_XQ, xT, 4, 512)
            turned_group_pe(pe, G_XQ + 1, C_XQ + 2, xT, 4, 512)
            xa_scores_pe(pe)
            xa_turn_pe(pe)
            xa_pv_pe(pe)
            pe.wait_ge(xa.vec, 16)
            group_pe(pe, G_XO, C_XO, xT, (4, 4), 512)
            group_pe(pe, G_XO + 1, C_XO + 2, xT, (4, 4), 512)
            norm_pe(pe, n3)
            ffn_pe(pe, f3, n3, C_FFN3, G_FFN3)

        def second_act(act):
            params2_act(act)
            norm_act(act, nm)
            s5p_act(act)

            def memory_there(e):
                e.wait_ge(mem_in, 16)
                e.wait_ge(nm.pe, 4)
            norm_act(act, nmem, src=memx, wait_src=memory_there)
            conv2_act1(act)
            wait_products(act, C_Z2 + 1)
            for m in range(MT):
                act.activation(z_s[:, m, :], acc[bank(G_Z2, m)][:, :], ACT.Silu).then_inc(acc_read[bank(G_Z2, m)], 1)
            feat_act(act, G_U2, C_U2, uT, 0)
            conv2_act2(act)
            ab_act(act)
            feat_act(act, G_MK, C_MK, kmT, 0)
            dn_cs_act(act)
            feat_act(act, G_MK + 1, C_MK + 2, kmT, 4)
            dn_turn_act(act)
            mv_act(act, 0)
            mv_act(act, 1)
            rc_act(act)
            glu_act(act)
            norm_act(act, nx, wait_src=lambda e: wait_x(e, G_WO2))
            feat_act(act, G_XQ, C_XQ, qcT, 0)
            feat_act(act, G_XQ + 1, C_XQ + 2, qcT, 4)
            xa_act(act)
            norm_act(act, n3, wait_src=lambda e: wait_x(e, G_XO))
            split_x_act(act, n3)
            ffn_act(act, f3, C_FFN3, G_FFN3)
            norm_act(act, nf, wait_src=lambda e: wait_x(e, G_FFN3 + NFB))

        def second_vec(vec):
            for i in range(4):
                vec.sem_inc(acc_read[i], 1)
            masks_vec(vec)
            params2_vec(vec)
            norm_vec(vec, nm, col[:, R2["mix"]:R2["mix"] + 8])
            s5p_vec(vec)
            s5p_vec2(vec)
            vec.memset(xpad2[:, :, 0:3], 0.0).then_inc(c2.vec, 1)
            norm_vec(vec, nmem, col[:, R2["mem"]:R2["mem"] + 8], src=memx, nb=memx, dst=memT)
            conv2_vec(vec)
            ab_vec(vec)
            dn_cs_vec(vec)
            dn_turn_vec(vec)
            dn_turn2_vec(vec)
            dn_kk_vec(vec)
            dn_qg_vec(vec)
            inv_vec(vec)
            rc_vec(vec)
            s5_vec(vec)
            glu_vec(vec)
            add_to_x(vec, C_WO2 + 3, G_WO2, 1.0)
            norm_vec(vec, nx, col[:, R2["x"]:R2["x"] + 8])
            xa_vec1(vec)
            xa_vec2(vec)
            add_to_x(vec, C_XO + 3, G_XO, 1.0)
            norm_vec(vec, n3, col[:, R2["ffn"]:R2["ffn"] + 8])
            split_x_vec(vec, n3)
            ffn_vec(vec, f3, C_FFN3, G_FFN3, 1.0)
            vec.wait_ge(nf.act, 3)
            vec.reciprocal(stat[:, 4:6], stat[:, 2:4]).then_inc(nf.vec, 1)
            vec.wait_ge(nf.vec, 1)
            vec.wait_ge(fin_in, 16)
            for m in range(MT):
                vec.scalar_tensor_tensor(out=xn[:, m, :], in0=x[:, m, :], scalar=stat[:, 4 + m:5 + m], in1=fin_g,
                                         op0=ALU.mult, op1=ALU.mult).then_inc(nf.vec, 1)

        with nc.Block() as block:
            @block.sync
            def _(sync):
                second_sync(sync)
                sync.wait_ge(n3.vec, SPLIT_DONE)
                sync.dma_start(fin_g, t["norm_final_g_2"].rearrange("(o d) -> o d", o=1).broadcast_to([P, D])).then_inc(fin_in, 16)
                for m in range(MT):
                    sync.wait_ge(nf.vec, 2 + m)
                    sync.dma_start(out[0, m * P:(m + 1) * P, :], xn[:, m, :]).then_inc(out_done, 16)
                sync.wait_ge(out_done, 16 * MT)

            @block.gpsimd
            def _(pool):
                masks_pool(pool)
                rotations_pool(pool)
                s5_pool(pool)

            @block.scalar
            def _(act):
                second_act(act)

            @block.vector
            def _(vec):
                second_vec(vec)

            @block.tensor
            def _(pe):
                second_pe(pe)


def kernel(**inputs):
    import concourse.bacc as bacc
    from concourse.bass_utils import run_bass_kernel_spmd

    nc = bacc.Bacc("TRN2", target_bir_lowering=False, num_devices=1)
    arrays, tensors = {}, {}
    for name in INPUTS:
        a = np.ascontiguousarray(inputs[name])
        arrays["in_" + name] = a
        tensors[name] = nc.dram_tensor("in_" + name, a.shape, mybir.dt.from_np(a.dtype), kind="ExternalInput").ap()
    out = nc.dram_tensor("out_0", (1, TOK, D), F32, kind="ExternalOutput").ap()
    build(nc, tensors, out)
    r = run_bass_kernel_spmd(nc, [arrays], core_ids=[0])
    return r.results[0]["out_0"]
```

```python
import math
from contextlib import ExitStack

import numpy as np

import concourse.bass as bass
from concourse import mybir

F32 = mybir.dt.float32
F32R = mybir.dt.float32r
I32 = mybir.dt.int32
ALU = mybir.AluOpType
ACT = mybir.ActivationFunctionType
AX = mybir.AxisListType.X

P = 128
TOK = 256
MT = TOK // P
D = 1024
KD = D // P
FF = 2816
FB = 256
NFB = FF // FB
KF = FF // P
DEPTH = 2
EPS = 1e-6
RING = 4
SLOT = 2080
N_CHUNK_FFN = 2 * NFB + KF // 2
N_GROUP_FFN = NFB + 2

INPUTS = [
    "x", "positions", "ffn1_norm", "ffn1_w_in", "ffn1_w_out", "mix_norm", "w_in", "gm_v_norm", "gm_w_s", "gm_b_s",
    "mla_q_norm", "mla_kv_norm", "mla_w_uq", "mla_w_ukv", "mla_q_gain", "mla_k_gain", "ssd_conv_w",
    "ssd_conv_b", "ssd_dt_bias", "ssd_a_log", "ssd_d", "ssd_norm", "w_branch", "w_out", "ffn2_norm", "ffn2_w_in",
    "ffn2_w_out", "mem_2", "norm_mix_g_2", "w_in_2", "conv_w_2", "dn_a_log_2", "dn_dt_bias_2", "dn_norm_g_2",
    "s5_a_re_2", "s5_a_im_2", "s5_b_re_2", "s5_b_im_2", "s5_c_re_2", "s5_c_im_2", "s5_d_2", "s5_log_dt_2",
    "s5_w_glu_2", "s5_b_glu_2", "w_out_2", "norm_x_g_2", "norm_mem_g_2", "w_xq_2", "w_xk_2", "w_xv_2", "w_xo_2",
    "norm_ffn_g_2", "w_gate_2", "w_up_2", "w_down_2", "norm_final_g_2",
]


class Counters:

    def __init__(self, act=None, vec=None, pe=None, pool=None, hT=None, hT_lo=None,
                 hi=None, lo=None):
        self.act, self.vec, self.pe, self.pool = act, vec, pe, pool
        self.hT, self.hT_lo, self.hi, self.lo = hT, hT_lo, hi, lo


def bank(G, m):
    return 2 * (G % 2) + m


def build(nc, t, out):
    with ExitStack() as ctx:
        def sb(name, shape, dt=F32):
            return ctx.enter_context(nc.sbuf_tensor(name, shape, dt))

        all_sems = []

        def sem(name):
            s = ctx.enter_context(nc.semaphore(name))
            all_sems.append(s)
            return s

        def steps(name, engines="act vec pe"):
            return Counters(**{e: sem(f"{name}_{e}_steps") for e in engines.split()})

        acc = [ctx.enter_context(nc.psum_tensor(f"acc{i}", [P, 512], F32)) for i in range(4)]
        turn = [ctx.enter_context(nc.psum_tensor(f"turn{i}", [P, 512], F32)) for i in range(4)]

        ring = sb("ring", [P, RING, SLOT])
        x = sb("x", [P, MT, D])
        xn = sb("xn", [P, MT, D])
        xT_at = nc.sbuf_base
        xT = sb("xT", [P, KD, TOK])
        junk = sb("junk", [P, 512])
        stat = sb("stat", [P, 64])
        ident = sb("ident", [P, P])
        ones = sb("ones", [P, P])
        upper = sb("upper", [P, P])
        causal = sb("causal", [P, TOK])
        eps_col = sb("eps_col", [P, 1])
        cos = sb("cos", [P, MT, 16])
        sin = sb("sin", [P, MT, 16])
        big_at = nc.sbuf_base
        BIG = sb("big", [P, 34392])

        def big(off, *shape):
            n = int(np.prod(shape))
            assert off + n <= 34392
            v = BIG[:, off:off + n]
            if len(shape) == 1:
                return v
            names = "abcd"[:len(shape)]
            return v.rearrange("p (" + " ".join(names) + ") -> p " + " ".join(names),
                               **dict(zip(names, shape)))

        def over_big(name, off, *shape):
            assert off + int(np.prod(shape)) <= 34392
            return nc.alloc_sbuf_tensor_at(name, [P] + list(shape), F32R, offset=big_at + 4 * off)

        hT_hi = over_big("hT_hi", 0, KF, TOK)
        hT_lo = over_big("hT_lo", 7680, KF, TOK)
        xT_hi = over_big("xT_hi", 13312, KD, TOK)
        xT_lo = over_big("xT_lo", 15360, KD, TOK)
        w_hi = over_big("w_hi", 17408, RING * 2048)
        w_lo = over_big("w_lo", 25600, RING * 2048)
        gate_s = big(5632, 2, 2, TOK)
        h_s = big(6656, 2, 2, TOK)

        landed = [sem(f"chunk_landed{i}") for i in range(RING)]
        products_done = sem("products_done")
        acc_read = [sem(f"acc_read{i}") for i in range(4)]
        tile0_done = sem("tile0_done")

        def slot(c, k, n):
            return ring[:, c % RING, 0:k * n].rearrange("p (k n) -> p k n", k=k)

        def load(sync, c, src, k, n, turns=0):
            sync.wait_ge(products_done, c + 1 + RING * turns)
            sync.dma_start(slot(c, k, n), src).then_inc(landed[c % RING], 16)

        def wait_chunk(pe, c, turns=0):
            pe.wait_ge(landed[c % RING], 16 * (c // RING + 1 + turns))

        def wait_products(eng, c, turns=0):
            eng.wait_ge(products_done, RING + c + 1 + RING * turns)

        def wait_acc_free(pe, G, m, turns=0):
            pe.wait_ge(acc_read[bank(G, m)], G // 2 + 1 + turns)

        def wait_acc_read(eng, G, m, turns=0):
            eng.wait_ge(acc_read[bank(G, m)], G // 2 + 2 + turns)

        def group_pe(pe, G, c, aT, ks, n, n_used=None, for_x=False):
            k0, K, nu = 0, sum(ks), n_used or n
            for i, kc in enumerate(ks):
                wait_chunk(pe, c + i)
                w = slot(c + i, kc, n)
                for m in range(MT):
                    if i == 0:
                        wait_acc_free(pe, G, m)
                    for k in range(kc):
                        ins = pe.matmul(acc[bank(G, m)][:, 0:nu], aT[:, k0 + k, m * P:(m + 1) * P], w[:, k, 0:nu],
                                        start=(k0 + k == 0), stop=(k0 + k == K - 1))
                    if for_x and i == len(ks) - 1 and m == 0:
                        ins.then_inc(tile0_done, 1)
                ins.then_inc(products_done, 1)
                k0 += kc

        def part_act(act, s, c, e, hi, k=4, n=512):
            wait_chunk(act, c)
            if e >= 2:
                wait_products(act, c - 2)
            act.activation(hi[:, e % 2], slot(c, k, n), ACT.Copy).then_inc(s.hi, 1)

        def part_vec(vec, s, c, e, hi, lo, k=4, n=512):
            vec.wait_ge(s.hi, e + 1)
            vec.tensor_tensor(lo[:, e % 2], slot(c, k, n), hi[:, e % 2].bitcast(F32), ALU.subtract).then_inc(s.lo, 1)

        def three(pe, o, a_hi, a_lo, wh, wl, start, stop):
            pe.matmul(o, a_hi, wh, start=start, stop=False)
            pe.matmul(o, a_hi, wl, start=False, stop=False)
            return pe.matmul(o, a_lo, wh, start=False, stop=stop)

        def split_group_pe(pe, s, G, c, e, a_hi, a_lo, hi, lo, n_chunks, kc=4, for_x=False):
            for i in range(n_chunks):
                pe.wait_ge(s.lo, e + i + 1)
                for m in range(MT):
                    ms = slice(m * P, (m + 1) * P)
                    if i == 0:
                        wait_acc_free(pe, G, m)
                    for k in range(kc):
                        ins = three(pe, acc[bank(G, m)][:, :], a_hi[:, i * kc + k, ms], a_lo[:, i * kc + k, ms],
                                    hi[:, (e + i) % 2, k, :], lo[:, (e + i) % 2, k, :],
                                    i == 0 and k == 0, i == n_chunks - 1 and k == kc - 1)
                    if for_x and i == n_chunks - 1 and m == 0:
                        ins.then_inc(tile0_done, 1)
                ins.then_inc(products_done, 1)

        def turned_group_pe(pe, G, c, aT, n_tiles, n, K=KD):
            kc = K // 2 if K == KD else K
            nch = K // kc
            for i in range(nch):
                wait_chunk(pe, c + i)
            for f in range(n_tiles):
                q = f // 2
                if f % 2 == 0:
                    wait_acc_free(pe, G, q)
                for k in range(K):
                    w = slot(c + k // kc, kc, n)
                    ins = pe.matmul(acc[bank(G, q)][:, (f % 2) * TOK:(f % 2) * TOK + TOK],
                                    w[:, k % kc, f * P:(f + 1) * P], aT[:, k, :],
                                    start=(k == 0), stop=(k == K - 1))
                    if f == n_tiles - 1 and k % kc == kc - 1:
                        ins.then_inc(products_done, 1)

        def norm_act(act, s, src=x, wait_src=None):
            for m in range(MT):
                if wait_src:
                    wait_src(act, m)
                act.activation(xn[:, m, :], src[:, m, :], ACT.Square,
                               accum_out=stat[:, m:m + 1]).then_inc(s.act, 1)
                act.wait_ge(s.act, 2 * m + 1)
                act.activation(stat[:, 2 + m:3 + m], stat[:, m:m + 1], ACT.Sqrt, bias=eps_col[:, 0:1],
                               scale=1.0 / D).then_inc(s.act, 1)

        def norm_vec(vec, s, gain, src=x, nb=xn, dst=xT, between=None):
            for m in range(MT):
                vec.wait_ge(s.act, 2 * m + 2)
                vec.reciprocal(stat[:, 4 + m:5 + m], stat[:, 2 + m:3 + m]).then_inc(s.vec, 1)
                vec.wait_ge(s.vec, 2 * m + 1)
                vec.tensor_scalar(nb[:, m, :], src[:, m, :], stat[:, 4 + m:5 + m], None, ALU.mult).then_inc(s.vec, 1)
            if between:
                between(vec)
            for b in range(4):
                m, hf = b // 2, b % 2
                vec.wait_ge(s.pe, b + 1)
                vec.tensor_tensor(dst[:, 4 * hf:4 * hf + 4, m * P:(m + 1) * P],
                                  turn[b][:, :].rearrange("p (k n) -> p k n", k=4),
                                  gain.unsqueeze(2).broadcast_to([P, KD, P])[:, 4 * hf:4 * hf + 4, :],
                                  ALU.mult).then_inc(s.vec, 1)

        def norm_pe(pe, s, nb=xn):
            for b in range(4):
                m, hf = b // 2, b % 2
                pe.wait_ge(s.vec, 2 + 2 * m)
                for k in range(4):
                    ins = pe.transpose(turn[b][:, k * P:(k + 1) * P],
                                       nb[:, m, (4 * hf + k) * P:(4 * hf + k + 1) * P], ident[:, :])
                ins.then_inc(s.pe, 1)

        NORM_DONE = 8

        def quarter(a, b):
            m, hf = b // 2, b % 2
            return a[:, 4 * hf:4 * hf + 4, m * P:(m + 1) * P]

        def split_x_act(act, s):
            for b in range(4):
                act.wait_ge(s.vec, 5 + b)
                act.activation(quarter(xT_hi, b), quarter(xT, b), ACT.Copy).then_inc(s.act, 1)

        def split_x_vec(vec, s):
            for b in range(4):
                vec.wait_ge(s.act, 5 + b)
                vec.tensor_tensor(quarter(xT_lo, b), quarter(xT, b), quarter(xT_hi, b).bitcast(F32),
                                  ALU.subtract).then_inc(s.vec, 1)

        SPLIT_DONE = 12

        def ffn_sems(name):
            return Counters(hT=sem(name + "_hT_hi_ready"),
                            hT_lo=sem(name + "_hT_lo_ready"), hi=sem(name + "_w_hi_ready"), lo=sem(name + "_w_lo_ready"))

        PAIRS = NFB // 2
        N_IN = 2 * NFB

        def w_part(w, r):
            if r < N_IN:
                pair = w[:, (r // 2 % 2) * 4096:(r // 2 % 2 + 1) * 4096].rearrange("p (k n) -> p k n", k=KD)
                return pair[:, :, (r % 2) * FB:(r % 2 + 1) * FB]
            return w[:, (r % RING) * 2048:(r % RING + 1) * 2048].rearrange("p (k n) -> p k n", k=2)

        def raw_part(c0, r):
            return slot(c0 + r, KD, FB) if r < N_IN else slot(c0 + r, 2, D)

        def ffn_sync(sync, f, c0, w_gate, w_up, w_down, aside=None):
            def chunk(r, src, i=0):
                sync.wait_ge(products_done, c0 + r + 1)
                sync.wait_ge(f.lo, r + 1 + RING * i)
                sync.dma_start(raw_part(c0, r), src).then_inc(landed[(c0 + r) % RING], 16)

            sync.sem_inc(f.lo, RING)
            with sync.Fori(0, PAIRS) as i:
                for jj in range(2):
                    chunk(2 * jj, w_gate(jj + 2 * i), i)
                    chunk(2 * jj + 1, w_up(jj + 2 * i), i)
            chunk(N_IN - 2, w_gate(NFB - 1))
            chunk(N_IN - 1, w_up(NFB - 1))
            if aside:
                aside(sync)
            for i in range(KF // 2):
                chunk(N_IN + i, w_down(i))

        def split_act(act, f, c0, r, i=0):
            wait_chunk(act, c0 + r, i)
            act.wait_ge(products_done, c0 + r + 1 + RING * i)
            act.activation(w_part(w_hi, r), raw_part(c0, r), ACT.Copy).then_inc(f.hi, 1)

        def split_vec(vec, f, c0, r, i=0):
            vec.wait_ge(f.hi, r + 1 + RING * i)
            vec.tensor_tensor(w_part(w_lo, r), raw_part(c0, r), w_part(w_hi, r).bitcast(F32), ALU.subtract).then_inc(f.lo, 1)

        def ffn_pe(pe, f, n, c0, G0, aside=None):
            def block(jj, i=0):
                G, p = G0 + jj, jj % 2
                wh = w_hi[:, p * 4096:(p + 1) * 4096].rearrange("p (k n) -> p k n", k=KD)
                wl = w_lo[:, p * 4096:(p + 1) * 4096].rearrange("p (k n) -> p k n", k=KD)
                for ft in range(4):
                    half, fs = ft // 2, slice(ft * P, (ft + 1) * P)
                    if ft % 2 == 0:
                        pe.wait_ge(f.lo, RING + 2 * jj + 1 + half + RING * i)
                        wait_acc_free(pe, G, half, i)
                    for k in range(KD):
                        ins = three(pe, acc[bank(G, half)][:, (ft % 2) * TOK:(ft % 2 + 1) * TOK], wh[:, k, fs], wl[:, k, fs],
                                    xT_hi[:, k, :], xT_lo[:, k, :], k == 0, k == KD - 1)
                ins.then_inc(products_done, 2)

            pe.wait_ge(n.vec, SPLIT_DONE)
            with pe.Fori(0, PAIRS) as i:
                block(0, i)
                block(1, i)
            block(NFB - 1)
            for i in range(KF // 2):
                r = N_IN + i
                if aside and i == 9:
                    aside(pe)
                pe.wait_ge(f.hT_lo, i + 1)
                pe.wait_ge(f.lo, RING + r + 1)
                for m in range(MT):
                    for k in range(2):
                        ms = slice(m * P, (m + 1) * P)
                        for hf in range(2):
                            G = G0 + NFB + hf
                            if i == 0 and k == 0:
                                wait_acc_free(pe, G, m)
                            ns = slice(hf * 512, (hf + 1) * 512)
                            ins = three(pe, acc[bank(G, m)][:, :], hT_hi[:, 2 * i + k, ms], hT_lo[:, 2 * i + k, ms],
                                        w_part(w_hi, r)[:, k, ns], w_part(w_lo, r)[:, k, ns],
                                        i == 0 and k == 0, i == KF // 2 - 1 and k == 1)
                    if i == KF // 2 - 1 and m == 0:
                        ins.then_inc(tile0_done, 1)
                ins.then_inc(products_done, 1)

        def first_split_act(act, f, c0):
            for r in range(2):
                split_act(act, f, c0, r)

        def first_split_vec(vec, f, c0):
            for r in range(2):
                split_vec(vec, f, c0, r)

        def ffn_act(act, f, c0, G0, aside=None):
            def split(jj, i=0):
                split_act(act, f, c0, 2 * jj, i)
                split_act(act, f, c0, 2 * jj + 1, i)

            def silu(jj, i=0):
                wait_products(act, c0 + 2 * jj + 1, i)
                act.activation(gate_s[:, jj % 2], acc[bank(G0 + jj, 0)][:, :].rearrange("p (k n) -> p k n", k=2),
                               ACT.Silu).then_inc(acc_read[bank(G0 + jj, 0)], 1)

            def copy_hT(jj, i=0):
                wait_acc_read(act, G0 + jj, 1, i)
                act.activation(hT_hi[:, bass.ds(2 * jj + 4 * i, 2), :], h_s[:, jj % 2], ACT.Copy).then_inc(f.hT, 1)

            with act.Fori(0, PAIRS) as i:
                split(1, i)
                silu(0, i)
                split(2, i)
                copy_hT(0, i)
                silu(1, i)
                copy_hT(1, i)
            split_act(act, f, c0, N_IN)
            split_act(act, f, c0, N_IN + 1)
            silu(NFB - 1)
            copy_hT(NFB - 1)
            for r in range(N_IN + 2, N_IN + KF // 2):
                split_act(act, f, c0, r)
                if aside and r == N_IN + 8:
                    aside(act)

        def ffn_vec(vec, f, c0, G0, factor, use, aside=None):
            def split(jj, i=0):
                split_vec(vec, f, c0, 2 * jj, i)
                split_vec(vec, f, c0, 2 * jj + 1, i)

            def hidden(jj, i=0):
                wait_acc_read(vec, G0 + jj, 0, i)
                vec.tensor_tensor(h_s[:, jj % 2], gate_s[:, jj % 2], acc[bank(G0 + jj, 1)][:, :].rearrange(
                    "p (k n) -> p k n", k=2), ALU.mult).then_inc(acc_read[bank(G0 + jj, 1)], 1)

            def rest_hT(jj, i=0):
                vec.wait_ge(f.hT, jj + 1 + 2 * i)
                part = bass.ds(2 * jj + 4 * i, 2)
                vec.tensor_tensor(hT_lo[:, part, :], h_s[:, jj % 2],
                                  hT_hi[:, part, :].bitcast(F32), ALU.subtract).then_inc(f.hT_lo, 1)

            with vec.Fori(0, PAIRS) as i:
                split(1, i)
                hidden(0, i)
                split(2, i)
                rest_hT(0, i)
                hidden(1, i)
                rest_hT(1, i)
            split_vec(vec, f, c0, N_IN)
            split_vec(vec, f, c0, N_IN + 1)
            hidden(NFB - 1)
            rest_hT(NFB - 1)
            for r in range(N_IN + 2, N_IN + KF // 2):
                split_vec(vec, f, c0, r)
                if aside and r == N_IN + 8:
                    aside(vec)
            add_to_x(vec, c0 + N_CHUNK_FFN - 1, G0 + NFB, factor, use)

        def add_to_x(vec, c_last, G, factor, use):
            for m in range(MT):
                if m == 0:
                    vec.wait_ge(tile0_done, use)
                else:
                    wait_products(vec, c_last)
                for hf in range(2):
                    xs = x[:, m, hf * 512:(hf + 1) * 512]
                    vec.scalar_tensor_tensor(out=xs, in0=acc[bank(G + hf, m)][:, :], scalar=factor, in1=xs,
                                             op0=ALU.mult, op1=ALU.add).then_inc(acc_read[bank(G + hf, m)], 1)

        def wait_x(eng, G, m):
            for hf in range(2):
                wait_acc_read(eng, G + hf, m)

        H, NOPE, ROPE, QKD, VD = 8, 64, 32, 96, 64
        QR, KVR = 384, 256
        SCALE = QKD ** -0.5
        C_MIX, G_MIX = N_CHUNK_FFN, N_GROUP_FFN
        (G_U, C_U), (G_V, C_V), (G_CQ, C_CQ), (G_KV, C_KV), (G_XBC0, C_XBC0), (G_XBC1, C_XBC1), (G_Z, C_Z) = [
            (G_MIX + i, C_MIX + 2 * i) for i in range(7)]
        G_UQ, C_UQ = G_MIX + 7, C_MIX + 14
        G_UKV, C_UKV = G_UQ + 2, C_UQ + 2
        G_GATE, C_GATE = G_UKV + 2, C_UKV + 1
        G_BR, C_BR = G_GATE + 6, C_GATE + 12
        BRANCHES = (0, 2, 1)
        G_WO, C_WO = G_BR + 6, C_BR + 6
        G_FFN2, C_FFN2 = G_WO + 2, C_WO + 4
        COLS = dict(u=0, v=512, cq=1024, ckv=1408, z=1696, xbc0=2208, xbc1=2720, gate=3240)

        R = dict(ffn1=0, mix=8, ffn2=16, qn=24, kvn=27, ssdn=29, convb=33, gmb=41, convw=45)
        N_ROWS = 77
        vecs = sb("vecs", [P, P])
        col = sb("col", [P, P])
        ws_in = sb("ws_in", [P, 4, P])
        wsT = sb("wsT", [P, 4, P])
        gmv = sb("gmv", [P, 512])
        qk_gain = sb("qk_gain", [P, 2, QKD])
        small = sb("small", [P, 24])
        neg_a = sb("neg_a", [P, 8])

        gates = big(0, MT, 3 * D)
        u_s = big(6144, MT, 512)
        v_s = big(7168, MT, 512)
        cqn = big(8192, MT, QR)
        ckvn = big(8960, MT, KVR)
        cqT = big(9472, 3, TOK)
        ckvT = big(10240, 2, TOK)
        sc0 = big(6144, H, P)
        sc1 = big(7168, H, TOK)
        kpe = big(10752, MT, ROPE)
        qk = big(10816, MT, 2 * H, QKD)
        PT0 = big(10816, H, P)
        PT1 = big(11840, 2, H, P)
        vtok = big(13888, MT, H, VD)
        qT = big(14912, H, TOK)
        kT = big(16960, H, TOK)
        Ld = big(19008, 2 * H, P)
        sq = big(21056, 2 * H * QKD)
        rope_t = big(21056, MT, 4, 2 * H, 16)
        br_t = big(19008, 2, MT, 512)
        xpad = big(23104, 8, TOK + 3)
        conv = big(25176, 8, TOK)
        xs_tok = big(23104, MT, 512)
        B_tok = big(24128, MT, 2, P)
        S0 = big(24640, 512)
        cbm = big(27224, MT, 2, P)
        xdt = big(27736, MT, 512)
        xdtd = big(28760, 512)
        sz = big(29272, MT, 512)
        yc = big(30296, MT, 512)
        yT = big(31320, 3, 4, TOK)
        C_SPLIT = C_GATE + 10
        part_hi = over_big("part_hi", 21056, 2, 4, 512)
        part_lo = over_big("part_lo", 25152, 2, 4, 512)
        normed_hi = over_big("normed_hi", 19008, KD, TOK)
        yT_hi = over_big("yT_hi", 14912, 3, 4, TOK)
        yT_lo = over_big("yT_lo", 31320, 3, 4, TOK)
        xT_rest = nc.alloc_sbuf_tensor_at("xT_rest", [P, KD, TOK], F32R, offset=xT_at)
        dtw = sb("dtw", [P, 12, 16])
        csv = sb("csv", [P, 40])
        att = sb("att", [P, 5, 16])
        dt_v, da = dtw[:, 10, :], dtw[:, 11, :]

        par_in, gain_in = sem("params_in"), sem("first_gain_in")
        par = steps("params")
        mix_norm = steps("mix_norm")
        gm, cq, xb, dts, sd, qs, br, mt = (steps(n) for n in
                                           ("gmlp", "latent", "conv", "dt", "ssd", "attn", "branch", "merged"))
        n1, n2 = steps("ffn1_norm"), steps("ffn2_norm")
        f1, f2 = ffn_sems("ffn1"), ffn_sems("ffn2")

        def lay(name, l):
            return t[name][bass.ds(l, 1)]

        def first_gain_act(act, l):
            act.dma_start(vecs[0:8, :], lay("ffn1_norm", l).rearrange("o (k p) -> (o k) p", p=P)).then_inc(gain_in, 16)

        def first_gain_pe(pe):
            pe.wait_ge(gain_in, 16)
            pe.transpose(acc[3][:, 0:8], vecs[0:8, :], ident[0:8, 0:8]).then_inc(par.pe, 1)

        def first_gain_vec(vec):
            vec.wait_ge(par.pe, 1)
            vec.tensor_copy(col[:, 0:8], acc[3][:, 0:8]).then_inc(par.vec, 1)
            vec.wait_ge(par.vec, 1)

        def params_sync(sync, l):
            for name, r, k in (("mix_norm", "mix", 8), ("ffn2_norm", "ffn2", 8),
                               ("mla_q_norm", "qn", 3), ("mla_kv_norm", "kvn", 2), ("ssd_norm", "ssdn", 4),
                               ("ssd_conv_b", "convb", 8)):
                sync.dma_start(vecs[R[r]:R[r] + k, :], lay(name, l).rearrange("o (k p) -> (o k) p", p=P)).then_inc(par_in, 16)
            sync.dma_start(vecs[R["gmb"]:R["gmb"] + 4, :], lay("gm_b_s", l).rearrange("o g t -> (o g) t")).then_inc(par_in, 16)
            sync.dma_start(vecs[R["convw"]:R["convw"] + 32, :],
                          lay("ssd_conv_w", l).rearrange("o j (k p) -> (o j k) p", p=P)).then_inc(par_in, 16)
            sync.dma_start(ws_in[:, :, :], lay("gm_w_s", l).rearrange("o g t s -> t (o g) s")).then_inc(par_in, 16)
            sync.dma_start(gmv[:, :], lay("gm_v_norm", l).broadcast_to([P, 512])).then_inc(par_in, 16)
            sync.dma_start(qk_gain[:, 0, :], lay("mla_q_gain", l).broadcast_to([P, QKD])).then_inc(par_in, 16)
            sync.dma_start(qk_gain[:, 1, :], lay("mla_k_gain", l).broadcast_to([P, QKD])).then_inc(par_in, 16)
            sync.dma_start(small[:, 0:8], lay("ssd_dt_bias", l).broadcast_to([P, 8])).then_inc(par_in, 16)
            sync.dma_start(small[:, 8:16], lay("ssd_a_log", l).broadcast_to([P, 8])).then_inc(par_in, 16)
            sync.dma_start(small[:, 16:24], lay("ssd_d", l).broadcast_to([P, 8])).then_inc(par_in, 16)

        tail = Counters(act=sem("tail_act_steps"), vec=sem("tail_vec_steps"), hi=sem("part_hi_ready"), lo=sem("part_lo_ready"))
        N_PAR = 15

        def params_act(act):
            act.wait_ge(par_in, 16 * N_PAR)
            act.activation(neg_a[:, :], small[:, 8:16], ACT.Exp).then_inc(par.act, 1)

        def params_pe(pe):
            pe.wait_ge(par.act, 1)
            pe.transpose(turn[2][:, 0:N_ROWS], vecs[0:N_ROWS, :], ident[0:N_ROWS, 0:N_ROWS]).then_inc(par.pe, 1)
            for g in range(4):
                ins = pe.transpose(turn[3][:, g * P:(g + 1) * P], ws_in[:, g, :], ident[:, :])
            ins.then_inc(par.pe, 1)

        def params_vec(vec):
            vec.wait_ge(par.act, 1)
            vec.tensor_scalar(neg_a[:, :], neg_a[:, :], -1.0, None, ALU.mult).then_inc(par.vec, 1)
            vec.wait_ge(par.pe, 2)
            vec.tensor_copy(col[:, 8:N_ROWS], turn[2][:, 8:N_ROWS]).then_inc(par.vec, 1)
            vec.wait_ge(par.pe, 3)
            vec.tensor_tensor(wsT[:, :, :], turn[3][:, :].rearrange("p (g n) -> p g n", g=4),
                              upper[:, :].unsqueeze(1).broadcast_to([P, 4, P]), ALU.mult).then_inc(par.vec, 1)
            vec.wait_ge(par.vec, 4)

        def mixer_sync(sync, l):
            def w_in(c, name, n, kc=4):
                for i in range(2):
                    load(sync, c + i, lay("w_in", l)[:, i * 512:(i + 1) * 512, COLS[name]:COLS[name] + n]
                         .rearrange("o (k p) n -> p (o k) n", p=P), 4, n)
            w_in(C_U, "u", 512)
            w_in(C_V, "v", 512)
            w_in(C_CQ, "cq", QR)
            w_in(C_KV, "ckv", KVR + ROPE)
            w_in(C_XBC0, "xbc0", 512)
            w_in(C_XBC1, "xbc1", 520)
            w_in(C_Z, "z", 512)
            for i in range(2):
                load(sync, C_UQ + i, lay("mla_w_uq", l)[:, :, i * 384:(i + 1) * 384]
                     .rearrange("o (k p) n -> p (o k) n", p=P), 3, 384)
            load(sync, C_UKV, lay("mla_w_ukv", l).rearrange("o (k p) n -> p (o k) n", p=P), 2, D)
            for g in range(6):
                for i in range(2):
                    load(sync, C_GATE + 2 * g + i,
                         lay("w_in", l)[:, i * 512:(i + 1) * 512, COLS["gate"] + 512 * g:COLS["gate"] + 512 * (g + 1)]
                         .rearrange("o (k p) n -> p (o k) n", p=P), 4, 512)
            for j, b in enumerate(BRANCHES):
                for i in range(2):
                    load(sync, C_BR + 2 * j + i, lay("w_branch", l)[:, b, :, 512 * i:512 * (i + 1)]
                         .rearrange("o (k p) n -> p (o k) n", p=P), 4, 512)
            for n in range(2):
                for i in range(2):
                    load(sync, C_WO + 2 * n + i, lay("w_out", l)[:, i * 512:(i + 1) * 512, n * 512:(n + 1) * 512]
                         .rearrange("o (k p) n -> p (o k) n", p=P), 4, 512)

        def gm_act(act):
            for G, c, dst in ((G_U, C_U, u_s), (G_V, C_V, v_s)):
                wait_products(act, c + 1)
                for m in range(MT):
                    act.activation(dst[:, m, :], acc[bank(G, m)][:, :], ACT.Gelu).then_inc(acc_read[bank(G, m)], 1)
            for m in range(MT):
                wait_acc_read(act, G_V, m)
                act.activation(junk[:, 0:512], v_s[:, m, :], ACT.Square, accum_out=stat[:, 8 + m:9 + m]).then_inc(gm.act, 1)
                act.wait_ge(gm.act, m + 1)
            act.activation(stat[:, 10:12], stat[:, 8:10], ACT.Sqrt, bias=eps_col[:, 0:1], scale=1.0 / 512).then_inc(gm.act, 1)

        def gm_vec1(vec):
            vec.wait_ge(gm.act, 3)
            vec.reciprocal(stat[:, 12:14], stat[:, 10:12]).then_inc(gm.vec, 1)
            vec.wait_ge(gm.vec, 1)
            for m in range(MT):
                vec.scalar_tensor_tensor(out=v_s[:, m, :], in0=v_s[:, m, :], scalar=stat[:, 12 + m:13 + m],
                                         in1=gmv[:, :], op0=ALU.mult, op1=ALU.mult).then_inc(gm.vec, 1)

        def gm_mix_pe(pe):
            for m in range(MT):
                pe.wait_ge(gm.vec, 2 + m)
                for g in range(4):
                    ins = pe.matmul(turn[m][:, g * P:(g + 1) * P], wsT[:, g, :], v_s[:, m, g * P:(g + 1) * P],
                                    start=True, stop=True)
                ins.then_inc(gm.pe, 1)

        def gm_vec2(vec):
            for m in range(MT):
                vec.wait_ge(gm.pe, 1 + m)
                for g in range(4):
                    ug = u_s[:, m, g * P:(g + 1) * P]
                    ins = vec.scalar_tensor_tensor(out=ug, in0=turn[m][:, g * P:(g + 1) * P],
                                                   scalar=col[:, R["gmb"] + g:R["gmb"] + g + 1], in1=ug,
                                                   op0=ALU.add, op1=ALU.mult)
                ins.then_inc(gm.vec, 1)

        def gm_turn_pe(pe):
            pe.wait_ge(cq.vec, 7)
            for m in range(MT):
                pe.wait_ge(gm.vec, 4 + m)
                for k in range(4):
                    ins = pe.transpose(turn[2 + m][:, k * P:(k + 1) * P], u_s[:, m, k * P:(k + 1) * P], ident[:, :])
                ins.then_inc(gm.pe, 1)

        def gm_vec3(vec):
            for m in range(MT):
                vec.wait_ge(gm.pe, 3 + m)
                vec.tensor_copy(yT[:, 0, :, m * P:(m + 1) * P],
                                turn[2 + m][:, :].rearrange("p (k n) -> p k n", k=4)).then_inc(gm.vec, 1)

        def cq_act(act):
            for i, (G, c, w) in enumerate(((G_CQ, C_CQ, QR), (G_KV, C_KV, KVR))):
                wait_products(act, c + 1)
                for m in range(MT):
                    act.activation(junk[:, 0:w], acc[bank(G, m)][:, 0:w], ACT.Square,
                                   accum_out=stat[:, 16 + 2 * i + m:17 + 2 * i + m]).then_inc(cq.act, 1)
                    act.wait_ge(cq.act, 2 * i + m + 1)
            act.activation(stat[:, 20:22], stat[:, 16:18], ACT.Sqrt, bias=eps_col[:, 0:1], scale=1.0 / QR).then_inc(cq.act, 1)
            act.activation(stat[:, 22:24], stat[:, 18:20], ACT.Sqrt, bias=eps_col[:, 0:1], scale=1.0 / KVR).then_inc(cq.act, 1)

        def cq_vec1(vec):
            vec.wait_ge(cq.act, 6)
            vec.reciprocal(stat[:, 24:28], stat[:, 20:24]).then_inc(cq.vec, 1)
            vec.wait_ge(cq.vec, 1)
            for m in range(MT):
                vec.tensor_scalar(cqn[:, m, :], acc[bank(G_CQ, m)][:, 0:QR], stat[:, 24 + m:25 + m], None,
                                  ALU.mult).then_inc(acc_read[bank(G_CQ, m)], 1)
            for m in range(MT):
                vec.tensor_scalar(ckvn[:, m, :], acc[bank(G_KV, m)][:, 0:KVR], stat[:, 26 + m:27 + m], None,
                                  ALU.mult).then_inc(cq.vec, 1)
                vec.tensor_copy(kpe[:, m, :], acc[bank(G_KV, m)][:, KVR:KVR + ROPE]).then_inc(acc_read[bank(G_KV, m)], 1)

        def cq_pe(pe):
            for m in range(MT):
                wait_acc_read(pe, G_CQ, m)
                for k in range(3):
                    ins = pe.transpose(turn[m][:, k * P:(k + 1) * P], cqn[:, m, k * P:(k + 1) * P], ident[:, :])
                ins.then_inc(cq.pe, 1)
            for m in range(MT):
                pe.wait_ge(cq.vec, 2 + m)
                for k in range(2):
                    ins = pe.transpose(turn[2 + m][:, k * P:(k + 1) * P], ckvn[:, m, k * P:(k + 1) * P], ident[:, :])
                ins.then_inc(cq.pe, 1)

        def cq_vec2(vec):
            for i, (dst, r, kk) in enumerate(((cqT, R["qn"], 3), (ckvT, R["kvn"], 2))):
                for m in range(MT):
                    vec.wait_ge(cq.pe, 2 * i + m + 1)
                    vec.tensor_tensor(dst[:, :, m * P:(m + 1) * P],
                                      turn[2 * i + m][:, 0:kk * P].rearrange("p (k n) -> p k n", k=kk),
                                      col[:, r:r + kk].unsqueeze(2).broadcast_to([P, kk, P]), ALU.mult).then_inc(cq.vec, 1)

        def xbc_act1(act, half):
            act.wait_ge(xb.vec, 1)
            for G, c, f in ((G_XBC0, C_XBC0, 0), (G_XBC1, C_XBC1, 4))[half:half + 1]:
                wait_products(act, c + 1)
                for q in range(2):
                    act.activation(xpad[:, f + 2 * q:f + 2 * q + 2, 3:3 + TOK],
                                   acc[bank(G, q)][:, :].rearrange("p (f n) -> p f n", f=2),
                                   ACT.Copy).then_inc(acc_read[bank(G, q)], 1)

        def xbc_act2(act):
            for f in range(8):
                act.wait_ge(xb.vec, 2 + 16 * (f // 4) + 12 + f % 4)
                act.activation(conv[:, f, :], conv[:, f, :], ACT.Silu,
                               bias=col[:, R["convb"] + f:R["convb"] + f + 1]).then_inc(xb.act, 1)

        def xbc_vec(vec, half):
            for j in range(4):
                for f in range(4 * half, 4 * half + 4):
                    w = col[:, R["convw"] + 8 * j + f:R["convw"] + 8 * j + f + 1]
                    if j == 0:
                        wait_acc_read(vec, G_XBC0 + half, (f % 4) // 2)
                        vec.tensor_scalar(conv[:, f, :], xpad[:, f, 0:TOK], w, None, ALU.mult).then_inc(xb.vec, 1)
                    else:
                        vec.wait_ge(xb.vec, 2 + 16 * half + 4 * (j - 1) + f % 4)
                        vec.scalar_tensor_tensor(out=conv[:, f, :], in0=xpad[:, f, j:j + TOK], scalar=w,
                                                 in1=conv[:, f, :], op0=ALU.mult, op1=ALU.add).then_inc(xb.vec, 1)

        def dt_pe(pe):
            wait_chunk(pe, C_XBC1)
            wait_chunk(pe, C_XBC1 + 1)
            for m in range(MT):
                for k in range(KD):
                    ins = pe.matmul(turn[m][:, 0:8], xT[:, k, m * P:(m + 1) * P],
                                    slot(C_XBC1 + k // 4, 4, 520)[:, k % 4, 512:520], start=(k == 0), stop=(k == KD - 1))
                ins.then_inc(dts.pe, 1)

        SMALL_E = 0.03

        def softplus_vec(vec, s, W, n, base):
            def w(i):
                return W[:, i, 0:n]
            vec.wait_ge(s.vec, base)
            vec.tensor_scalar(w(1), w(0), 0.0, None, ALU.max).then_inc(s.vec, 1)
            vec.tensor_scalar(w(2), w(0), -1.0, None, ALU.mult).then_inc(s.vec, 1)
            vec.wait_ge(s.vec, base + 2)
            vec.tensor_tensor(w(3), w(0), w(2), ALU.min).then_inc(s.vec, 1)
            vec.wait_ge(s.act, 1)
            vec.tensor_scalar(w(5), w(4), 1.0, None, ALU.add).then_inc(s.vec, 1)
            vec.tensor_scalar(w(7), w(4), 0.2, None, ALU.mult).then_inc(s.vec, 1)
            for i, k in enumerate((-0.25, 1 / 3, -0.5, 1.0)):
                vec.wait_ge(s.vec, base + 5 + i)
                vec.scalar_tensor_tensor(out=w(7), in0=w(7), scalar=k, in1=w(4), op0=ALU.add,
                                         op1=ALU.mult).then_inc(s.vec, 1)
            vec.wait_ge(s.vec, base + 9)
            vec.scalar_tensor_tensor(out=w(7), in0=w(4), scalar=SMALL_E, in1=w(7),
                                     op0=ALU.is_lt, op1=ALU.mult).then_inc(s.vec, 1)
            vec.wait_ge(s.act, 2)
            vec.scalar_tensor_tensor(out=w(9), in0=w(4), scalar=SMALL_E, in1=w(8),
                                     op0=ALU.is_ge, op1=ALU.mult).then_inc(s.vec, 1)
            vec.wait_ge(s.vec, base + 11)
            vec.tensor_tensor(w(9), w(9), w(7), ALU.add).then_inc(s.vec, 1)
            vec.wait_ge(s.vec, base + 12)
            vec.tensor_tensor(w(10), w(9), w(1), ALU.add).then_inc(s.vec, 1)
            vec.wait_ge(s.vec, base + 13)

        def softplus_act(act, s, W, n, base):
            act.wait_ge(s.vec, base + 3)
            act.activation(W[:, 4, 0:n], W[:, 3, 0:n], ACT.Exp).then_inc(s.act, 1)
            act.wait_ge(s.vec, base + 4)
            act.activation(W[:, 8, 0:n], W[:, 5, 0:n], ACT.Ln).then_inc(s.act, 1)

        def dt_vec(vec):
            for m in range(MT):
                vec.wait_ge(dts.pe, 1 + m)
                vec.tensor_tensor(dtw[:, 0, 8 * m:8 * m + 8], turn[m][:, 0:8], small[:, 0:8], ALU.add).then_inc(dts.vec, 1)
            softplus_vec(vec, dts, dtw, 16, 2)
            vec.tensor_tensor(da.rearrange("p (m h) -> p m h", m=MT), dt_v.rearrange("p (m h) -> p m h", m=MT),
                              neg_a[:, :].unsqueeze(1).broadcast_to([P, MT, 8]), ALU.mult).then_inc(dts.vec, 1)

        def sd_cs_pe(pe):
            pe.wait_ge(dts.vec, 16)
            for m in range(MT):
                pe.matmul(turn[2][:, 8 * m:8 * m + 8], upper[:, :], da[:, 8 * m:8 * m + 8], start=True, stop=True)
            pe.matmul(turn[2][:, 16:24], ones[:, :], da[:, 0:8], start=True, stop=True).then_inc(sd.pe, 1)

        def sd_rows_pe(pe):
            pe.wait_ge(sd.vec, 1)
            for r in range(4):
                for h in range(4):
                    j = 4 * r + h
                    ins = pe.matmul(turn[r][:, h * P:(h + 1) * P], da[:, j:j + 1].broadcast_to([P, P]), upper[:, :],
                                    start=True, stop=True)
                ins.then_inc(sd.pe, 1)

        def sd_turn_pe(pe):
            pe.wait_ge(xb.act, 8)
            pe.wait_ge(sd.vec, 6)
            for m in range(MT):
                for f in range(4):
                    ins = pe.transpose(turn[m][:, f * P:(f + 1) * P], conv[:, f, m * P:(m + 1) * P], ident[:, :])
                ins.then_inc(sd.pe, 1)
            for m in range(MT):
                for g in range(2):
                    ins = pe.transpose(turn[2][:, (2 * m + g) * P:(2 * m + g + 1) * P],
                                       conv[:, 4 + g, m * P:(m + 1) * P], ident[:, :])
            ins.then_inc(sd.pe, 1)
            for m in range(MT):
                for g in range(2):
                    ins = pe.matmul(turn[3][:, (2 * m + g) * P:(2 * m + g + 1) * P],
                                    conv[:, 4 + g, m * P:(m + 1) * P], conv[:, 6 + g, m * P:(m + 1) * P],
                                    start=True, stop=True)
            ins.then_inc(sd.pe, 1)

        def sd_y_pe(pe):
            for m in range(MT):
                pe.wait_ge(sd.vec, 15 + m)
                for h in range(H):
                    ins = pe.matmul(turn[m][:, h * VD:(h + 1) * VD], Ld[:, 8 * m + h, :], xdt[:, m, h * VD:(h + 1) * VD],
                                    start=True, stop=True)
                ins.then_inc(sd.pe, 1)
            pe.wait_ge(sd.vec, 17)
            for g in range(2):
                ins = pe.matmul(turn[2][:, g * 256:(g + 1) * 256], B_tok[:, 0, g, :], xdtd[:, g * 256:(g + 1) * 256],
                                start=True, stop=True)
            ins.then_inc(sd.pe, 1)

        def sd_off_pe(pe):
            pe.wait_ge(sd.vec, 18)
            for g in range(2):
                ins = pe.matmul(turn[3][:, g * 256:(g + 1) * 256], conv[:, 6 + g, P:2 * P], S0[:, g * 256:(g + 1) * 256],
                                start=True, stop=True)
            ins.then_inc(sd.pe, 1)

        def sd_out_pe(pe):
            for m in range(MT):
                pe.wait_ge(sd.vec, 28 + m)
                for k in range(4):
                    ins = pe.transpose(turn[m][:, k * P:(k + 1) * P], yc[:, m, k * P:(k + 1) * P], ident[:, :])
                ins.then_inc(sd.pe, 1)

        def heads(ap, n=H):
            return ap.rearrange("p (h d) -> p h d", h=n)

        def over(ap, n, d):
            return ap.unsqueeze(2).broadcast_to([P, n, d])

        def sd_vec1(vec):
            vec.wait_ge(sd.pe, 1)
            vec.tensor_copy(csv[:, 0:24], turn[2][:, 0:24]).then_inc(sd.vec, 1)
            vec.wait_ge(sd.vec, 1)
            vec.tensor_tensor(csv[:, 24:32], csv[:, 16:24], csv[:, 0:8], ALU.subtract).then_inc(sd.vec, 1)
            for r in range(4):
                vec.wait_ge(sd.pe, 2 + r)
                for h in range(4):
                    j = 4 * r + h
                    ins = vec.tensor_scalar(Ld[:, j, :], turn[r][:, h * P:(h + 1) * P], csv[:, j:j + 1], 0.0,
                                            ALU.subtract, ALU.min)
                ins.then_inc(sd.vec, 1)

        def sd_vec2(vec):
            for m in range(MT):
                vec.wait_ge(sd.pe, 6 + m)
                vec.tensor_copy(xs_tok[:, m, :], turn[m][:, :]).then_inc(sd.vec, 1)
            vec.wait_ge(sd.pe, 8)
            vec.tensor_copy(B_tok.rearrange("p m g n -> p (m g n)"), turn[2][:, :]).then_inc(sd.vec, 1)
            vec.wait_ge(sd.pe, 9)
            vec.tensor_tensor(cbm.rearrange("p m g n -> p (m g) n"), turn[3][:, :].rearrange("p (j n) -> p j n", j=4),
                              upper[:, :].unsqueeze(1).broadcast_to([P, 4, P]), ALU.mult).then_inc(sd.vec, 1)
            vec.wait_ge(sd.vec, 10)
            for r in range(4):
                vec.wait_ge(sd.act, 3 + r)
                vec.tensor_tensor(Ld[:, 4 * r:4 * r + 4, :], Ld[:, 4 * r:4 * r + 4, :],
                                  cbm[:, r // 2, r % 2, :].unsqueeze(1).broadcast_to([P, 4, P]),
                                  ALU.mult).then_inc(sd.vec, 1)
            for m in range(MT):
                vec.tensor_tensor(heads(xdt[:, m, :]), heads(xs_tok[:, m, :]), over(dt_v[:, 8 * m:8 * m + 8], H, VD),
                                  ALU.mult).then_inc(sd.vec, 1)
            vec.wait_ge(sd.vec, 16)
            vec.wait_ge(sd.act, 2)
            vec.tensor_tensor(heads(xdtd), heads(xdt[:, 0, :]), over(csv[:, 24:32], H, VD), ALU.mult).then_inc(sd.vec, 1)

        def sd_vec3(vec):
            vec.wait_ge(sd.pe, 12)
            vec.tensor_copy(S0, turn[2][:, :]).then_inc(sd.vec, 1)
            for m in range(MT):
                vec.tensor_tensor(heads(yc[:, m, :]), heads(xs_tok[:, m, :]), over(small[:, 16:24], H, VD),
                                  ALU.mult).then_inc(sd.vec, 1)
            vec.wait_ge(sd.vec, 20)
            for m in range(MT):
                vec.tensor_tensor(yc[:, m, :], yc[:, m, :], turn[m][:, :], ALU.add).then_inc(sd.vec, 1)

        def sd_vec4(vec):
            vec.wait_ge(sd.vec, 22)
            vec.wait_ge(sd.pe, 13)
            vec.wait_ge(sd.act, 1)
            vec.tensor_tensor(heads(xdt[:, 0, :]), heads(turn[3][:, :]), over(csv[:, 32:40], H, VD), ALU.mult).then_inc(sd.vec, 1)
            vec.wait_ge(sd.vec, 23)
            vec.tensor_tensor(yc[:, 1, :], yc[:, 1, :], xdt[:, 0, :], ALU.add).then_inc(sd.vec, 1)
            vec.wait_ge(sd.vec, 24)
            for m in range(MT):
                wait_acc_read(vec, G_Z, m)
                vec.tensor_tensor(yc[:, m, :], yc[:, m, :], sz[:, m, :], ALU.mult).then_inc(sd.vec, 1)
            vec.wait_ge(sd.act, 11)
            vec.reciprocal(stat[:, 40:44], stat[:, 36:40]).then_inc(sd.vec, 1)
            vec.wait_ge(sd.vec, 27)
            for m in range(MT):
                vec.tensor_tensor(heads(yc[:, m, :], 2), heads(yc[:, m, :], 2), over(stat[:, 40 + 2 * m:42 + 2 * m], 2, 256),
                                  ALU.mult).then_inc(sd.vec, 1)

        def sd_vec5(vec):
            for m in range(MT):
                vec.wait_ge(sd.pe, 14 + m)
                vec.tensor_tensor(yT[:, 2, :, m * P:(m + 1) * P], heads(turn[m][:, :], 4),
                                  over(col[:, R["ssdn"]:R["ssdn"] + 4], 4, P), ALU.mult).then_inc(sd.vec, 1)

        def z_act(act):
            wait_products(act, C_Z + 1)
            for m in range(MT):
                act.activation(sz[:, m, :], acc[bank(G_Z, m)][:, :], ACT.Silu).then_inc(acc_read[bank(G_Z, m)], 1)

        def sd_act1(act):
            act.wait_ge(sd.vec, 2)
            act.activation(csv[:, 32:40], csv[:, 8:16], ACT.Exp).then_inc(sd.act, 1)
            act.activation(csv[:, 24:32], csv[:, 24:32], ACT.Exp).then_inc(sd.act, 1)
            for r in range(4):
                act.wait_ge(sd.vec, 3 + r)
                act.activation(Ld[:, 4 * r:4 * r + 4, :], Ld[:, 4 * r:4 * r + 4, :], ACT.Exp).then_inc(sd.act, 1)

        def sd_act2(act):
            for m in range(MT):
                act.wait_ge(sd.vec, 25 + m)
                for g in range(2):
                    n = 2 * m + g
                    act.activation(junk[:, 0:256], yc[:, m, g * 256:(g + 1) * 256], ACT.Square,
                                   accum_out=stat[:, 32 + n:33 + n]).then_inc(sd.act, 1)
                    act.wait_ge(sd.act, 7 + n)
            act.activation(stat[:, 36:40], stat[:, 32:36], ACT.Sqrt, bias=eps_col[:, 0:1], scale=1.0 / 256).then_inc(sd.act, 1)

        def qs_groups_pe(pe):
            pe.wait_ge(cq.vec, 7)
            for n in range(2):
                group_pe(pe, G_UQ + n, C_UQ + n, cqT, (3,), 384)
            wait_chunk(pe, C_UKV)
            w = slot(C_UKV, 2, D)
            for n in range(2):
                for m in range(MT):
                    wait_acc_free(pe, G_UKV + n, m)
                    for k in range(2):
                        ins = pe.matmul(acc[bank(G_UKV + n, m)][:, :], ckvT[:, k, m * P:(m + 1) * P],
                                        w[:, k, n * 512:(n + 1) * 512], start=(k == 0), stop=(k == 1))
            ins.then_inc(products_done, 1)

        def qs_act1(act):
            for n in range(2):
                wait_products(act, C_UQ + n)
                for m in range(MT):
                    act.activation(qk[:, m, 4 * n:4 * n + 4, :], acc[bank(G_UQ + n, m)][:, 0:384].rearrange(
                        "p (h d) -> p h d", h=4), ACT.Copy).then_inc(acc_read[bank(G_UQ + n, m)], 1)
            wait_products(act, C_UKV)
            for n in range(2):
                for m in range(MT):
                    kv = acc[bank(G_UKV + n, m)][:, :].rearrange("p (h d) -> p h d", h=4)
                    act.activation(qk[:, m, H + 4 * n:H + 4 * n + 4, 0:NOPE], kv[:, :, 0:NOPE], ACT.Copy)
                    act.activation(vtok[:, m, 4 * n:4 * n + 4, :], kv[:, :, NOPE:NOPE + VD],
                                   ACT.Copy).then_inc(acc_read[bank(G_UKV + n, m)], 1)

        def qs_vec1(vec):
            for m in range(MT):
                wait_acc_read(vec, G_KV, m)
                vec.tensor_copy(qk[:, m, H:2 * H, NOPE:QKD], kpe[:, m, :].unsqueeze(1).broadcast_to([P, H, ROPE])
                                ).then_inc(qs.vec, 1)
            vec.wait_ge(qs.vec, 2)
            sq_v = sq.rearrange("p (h d) -> p h d", h=2 * H)
            for m in range(MT):
                for n in range(2):
                    wait_acc_read(vec, G_UQ + n, m)
                    wait_acc_read(vec, G_UKV + n, m)
                vec.tensor_tensor(sq_v, qk[:, m, :, :], qk[:, m, :, :], ALU.mult).then_inc(qs.vec, 1)
                vec.wait_ge(qs.vec, 3 + 2 * m)
                vec.tensor_reduce(stat[:, 0:16] if m == 0 else stat[:, 16:32], sq_v, AX, ALU.add).then_inc(qs.vec, 1)
                vec.wait_ge(qs.vec, 4 + 2 * m)
            vec.wait_ge(qs.act, 1)
            vec.reciprocal(qrs[:, 0:32], qrs[:, 0:32]).then_inc(qs.vec, 1)
            vec.wait_ge(qs.vec, 7)
            for m in range(MT):
                vec.tensor_tensor(qk[:, m, :, :], qk[:, m, :, :], over(qrs[:, 16 * m:16 * m + 16], 2 * H, QKD),
                                  ALU.mult).then_inc(qs.vec, 1)
            for m in range(MT):
                vec.wait_ge(qs.vec, 8 + m)
                qv = qk[:, m, :, :].rearrange("p (s h) d -> p s h d", s=2)
                vec.tensor_tensor(qv, qv, qk_gain[:, :, :].unsqueeze(2).broadcast_to([P, 2, H, QKD]),
                                  ALU.mult).then_inc(qs.vec, 1)

        def qs_vec2(vec):
            for m in range(MT):
                vec.wait_ge(qs.vec, 10 + m)
                x1, x2 = qk[:, m, :, NOPE:NOPE + 16], qk[:, m, :, NOPE + 16:QKD]
                c = cos[:, m, :].unsqueeze(1).broadcast_to([P, 2 * H, 16])
                s = sin[:, m, :].unsqueeze(1).broadcast_to([P, 2 * H, 16])
                r = rope_t[:, m]
                for i, (a, b) in enumerate(((x1, c), (x2, s), (x2, c), (x1, s))):
                    vec.tensor_tensor(r[:, i], a, b, ALU.mult).then_inc(qs.vec, 1)
                vec.wait_ge(qs.vec, 15 + 6 * m)
                vec.tensor_tensor(x1, r[:, 0], r[:, 1], ALU.subtract).then_inc(qs.vec, 1)
                vec.tensor_tensor(x2, r[:, 2], r[:, 3], ALU.add).then_inc(qs.vec, 1)

        def qs_act2(act):
            act.wait_ge(qs.vec, 6)
            act.activation(qrs[:, 0:32], stat[:, 0:32], ACT.Sqrt, bias=eps_col[:, 0:1], scale=1.0 / QKD).then_inc(qs.act, 1)

        def qs_turn_pe(pe):
            for m in range(MT):
                pe.wait_ge(qs.vec, 17 + 6 * m)
                for kind in range(2):
                    for hf in range(2):
                        r = 4 * m + 2 * kind + hf
                        if r >= 4:
                            pe.wait_ge(qs.vec, 24 + r - 4)
                        elif r >= 2:
                            pe.wait_ge(sd.vec, 28 + r)
                        for h in range(4):
                            ins = pe.transpose(turn[(r + 2) % 4][0:QKD, h * P:(h + 1) * P],
                                               qk[:, m, H * kind + 4 * hf + h, :], ident[:, :])
                        ins.then_inc(qs.pe, 1)

        def qs_vec3(vec):
            for r in range(8):
                m, kind, hf = r // 4, r // 2 % 2, r % 2
                vec.wait_ge(qs.pe, 1 + r)
                dst = (qT, kT)[kind]
                vec.tensor_copy(dst[0:QKD, 4 * hf:4 * hf + 4, m * P:(m + 1) * P],
                                turn[(r + 2) % 4][0:QKD, :].rearrange("p (h n) -> p h n", h=4)).then_inc(qs.vec, 1)

        def qs_scores_pe(pe):
            pe.wait_ge(qs.vec, 31)
            for m in range(MT):
                nk = P * (m + 1)
                for hp in range(4):
                    if m > 0:
                        pe.wait_ge(qs.vec, 32 + hp)
                    for h in range(2):
                        ins = pe.matmul(turn[hp][:, h * nk:(h + 1) * nk], qT[0:QKD, 2 * hp + h, m * P:(m + 1) * P],
                                        kT[0:QKD, 2 * hp + h, 0:nk], start=True, stop=True)
                    ins.then_inc(qs.pe, 1)

        def qs_vec4(vec):
            for m, sc in enumerate((sc0, sc1)):
                nk = P * (m + 1)
                for hp in range(4):
                    vec.wait_ge(qs.pe, 9 + 4 * m + hp)
                    vec.tensor_tensor(sc[:, 2 * hp:2 * hp + 2, :], turn[hp][:, 0:2 * nk].rearrange("p (h n) -> p h n", h=2),
                                      causal[:, TOK - nk:TOK].unsqueeze(1).broadcast_to([P, 2, nk]),
                                      ALU.add).then_inc(qs.vec, 1)
            for m, sc in enumerate((sc0, sc1)):
                vec.wait_ge(qs.vec, 35 + 4 * m)
                vec.tensor_reduce(att[:, 0, 8 * m:8 * m + 8], sc, AX, ALU.max).then_inc(qs.vec, 1)
            vec.wait_ge(qs.vec, 41)
            vec.tensor_scalar(att[:, 1, :], att[:, 0, :], -SCALE, None, ALU.mult).then_inc(qs.vec, 1)

        def qs_act3(act, m):
            act.wait_ge(qs.vec, 42)
            sc = (sc0, sc1)[m]
            for h in range(H):
                j = 8 * m + h
                act.activation(sc[:, h, :], sc[:, h, :], ACT.Exp, bias=att[:, 1, j:j + 1], scale=SCALE,
                               accum_out=att[:, 2, j:j + 1]).then_inc(qs.act, 1)

        def qs_vec5(vec):
            for m, sc in enumerate((sc0, sc1)):
                vec.wait_ge(qs.act, 9 + 8 * m)
                vec.reciprocal(att[:, 3, 8 * m:8 * m + 8], att[:, 2, 8 * m:8 * m + 8]).then_inc(qs.vec, 1)
                vec.wait_ge(qs.vec, 43 + 2 * m)
                vec.tensor_tensor(sc, sc, over(att[:, 3, 8 * m:8 * m + 8], H, P * (m + 1)), ALU.mult).then_inc(qs.vec, 1)

        TURNS = [(0, 0, 0), (0, 0, 1), (1, 0, 0), (1, 0, 1), (1, 1, 0), (1, 1, 1)]

        def qs_pt_pe(pe):
            for r, (m, kb, hf) in enumerate(TURNS):
                pe.wait_ge(qs.vec, 44 + 2 * m)
                if r >= 4:
                    pe.wait_ge(qs.vec, 47 + r - 4)
                for h in range(4):
                    ins = pe.transpose(turn[r % 4][:, h * P:(h + 1) * P],
                                       (sc0, sc1)[m][:, 4 * hf + h, kb * P:(kb + 1) * P], ident[:, :])
                ins.then_inc(qs.pe, 1)

        def qs_vec6(vec):
            for r, (m, kb, hf) in enumerate(TURNS):
                vec.wait_ge(qs.pe, 17 + r)
                dst = PT1[:, kb, 4 * hf:4 * hf + 4, :] if m else PT0[:, 4 * hf:4 * hf + 4, :]
                vec.tensor_copy(dst, turn[r % 4][:, :].rearrange("p (h n) -> p h n", h=4)).then_inc(qs.vec, 1)

        def qs_pv_pe(pe):
            pe.wait_ge(qs.vec, 52)
            for m in range(MT):
                for h in range(H):
                    o = turn[2 + m][64 * (h % 2):64 * (h % 2) + 64, (h // 2) * P:(h // 2 + 1) * P]
                    for kb in range(m + 1):
                        ins = pe.matmul(o, vtok[:, kb, h, :], PT1[:, kb, h, :] if m else PT0[:, h, :],
                                        start=(kb == 0), stop=(kb == m))
                ins.then_inc(qs.pe, 1)

        def qs_vec7(vec):
            for m in range(MT):
                vec.wait_ge(qs.pe, 23 + m)
                vec.tensor_copy(yT[:, 1, :, m * P:(m + 1) * P], heads(turn[2 + m][:, :], 4)).then_inc(qs.vec, 1)

        def gate_act(act, i):
            wait_products(act, C_GATE + 2 * i + 1)
            for m in range(MT):
                act.activation(gates[:, m, i * 512:(i + 1) * 512], acc[bank(G_GATE + i, m)][:, :],
                               ACT.Sigmoid).then_inc(acc_read[bank(G_GATE + i, m)], 1)

        BRANCH_IN = {0: (gm.vec, 7), 1: (qs.vec, 54), 2: (sd.vec, 31)}

        def branch_pe(pe, j):
            b = BRANCHES[j]
            pe.wait_ge(tail.vec, 2 + j)
            for n in range(2):
                split_group_pe(pe, tail, G_BR + 2 * j + n, C_BR + 2 * j + n, 2 + 2 * j + n, yT_hi[:, b], yT_lo[:, b],
                               part_hi, part_lo, 1)

        def branch_gate_vec(vec, j, ns=(0, 1)):
            b = BRANCHES[j]
            for n in ns:
                if j == 2:
                    vec.wait_ge(br.vec, 2 * n + 2)
                wait_acc_read(vec, G_GATE + 2 * b + n, 0)
                wait_acc_read(vec, G_GATE + 2 * b + n, 1)
                wait_products(vec, C_BR + 2 * j + n)
                for m in range(MT):
                    g = bank(G_BR + 2 * j + n, m)
                    dst = xn[:, m, n * 512:(n + 1) * 512] if j == 0 else br_t[:, n, m, :]
                    vec.tensor_tensor(dst, acc[g][:, :], gates[:, m, b * D + n * 512:b * D + (n + 1) * 512],
                                      ALU.mult).then_inc(acc_read[g], 1)

        def branch_add_vec(vec, j, ns=(0, 1)):
            for n in ns:
                for m in range(MT):
                    wait_acc_read(vec, G_BR + 2 * j + n, m)
                    wait_acc_read(vec, G_BR + n, m)
                    dst = xn[:, m, n * 512:(n + 1) * 512]
                    vec.tensor_tensor(dst, dst, br_t[:, n, m, :], ALU.add).then_inc(br.vec, 1)

        def merged_pe(pe):
            pe.wait_ge(br.vec, 8)
            for b in range(4):
                m, hf = b // 2, b % 2
                for k in range(4):
                    ins = pe.transpose(turn[b][:, k * P:(k + 1) * P],
                                       xn[:, m, (4 * hf + k) * P:(4 * hf + k + 1) * P], ident[:, :])
                ins.then_inc(mt.pe, 1)

        def merged_vec(vec):
            for b in range(4):
                m, hf = b // 2, b % 2
                vec.wait_ge(mt.pe, 1 + b)
                vec.tensor_copy(xT[:, 4 * hf:4 * hf + 4, m * P:(m + 1) * P], heads(turn[b][:, :], 4)).then_inc(mt.vec, 1)

        def tail_part_act(act, *es):
            for e in es:
                part_act(act, tail, C_SPLIT + e, e, part_hi)

        def tail_part_vec(vec, *es):
            for e in es:
                part_vec(vec, tail, C_SPLIT + e, e, part_hi, part_lo)

        def normed_act(act):
            act.wait_ge(sd.pe, 11)
            act.activation(normed_hi[:, :, :], xT[:, :, :], ACT.Copy).then_inc(tail.act, 1)
            act.wait_ge(qs.vec, 23)
            act.wait_ge(sd.vec, 20)
            act.wait_ge(sd.pe, 13)

        def normed_vec(vec):
            vec.wait_ge(tail.act, 1)
            wait_products(vec, C_SPLIT - 1)
            vec.tensor_tensor(xT_rest[:, :, :], xT[:, :, :], normed_hi[:, :, :].bitcast(F32), ALU.subtract).then_inc(tail.vec, 1)

        def branch_in_act(act, j):
            act.wait_ge(*BRANCH_IN[BRANCHES[j]])
            act.wait_ge(qs.pe, 16)
            b = BRANCHES[j]
            act.activation(yT_hi[:, b], yT[:, b], ACT.Copy).then_inc(tail.act, 1)

        def branch_in_vec(vec, j):
            b = BRANCHES[j]
            vec.wait_ge(tail.act, 2 + j)
            vec.tensor_tensor(yT_lo[:, b], yT[:, b], yT_hi[:, b].bitcast(F32), ALU.subtract).then_inc(tail.vec, 1)

        def merged_in_act(act):
            for b in range(4):
                act.wait_ge(mt.vec, 1 + b)
                act.activation(quarter(xT_hi, b), quarter(xT, b), ACT.Copy).then_inc(tail.act, 1)

        def merged_in_vec(vec):
            for b in range(4):
                vec.wait_ge(tail.act, 5 + b)
                vec.tensor_tensor(quarter(xT_rest, b), quarter(xT, b), quarter(xT_hi, b).bitcast(F32),
                                  ALU.subtract).then_inc(tail.vec, 1)

        def gate_pe(pe, i):
            group_pe(pe, G_GATE + i, C_GATE + 2 * i, xT, (4, 4), 512)

        def mixer_pe(pe):
            norm_pe(pe, mix_norm)
            pe.wait_ge(mix_norm.vec, NORM_DONE)
            group_pe(pe, G_U, C_U, xT, (4, 4), 512)
            group_pe(pe, G_V, C_V, xT, (4, 4), 512)
            group_pe(pe, G_CQ, C_CQ, xT, (4, 4), QR)
            gm_mix_pe(pe)
            group_pe(pe, G_KV, C_KV, xT, (4, 4), KVR + ROPE)
            turned_group_pe(pe, G_XBC0, C_XBC0, xT, 4, 512)
            cq_pe(pe)
            gm_turn_pe(pe)
            dt_pe(pe)
            turned_group_pe(pe, G_XBC1, C_XBC1, xT, 4, 520)
            group_pe(pe, G_Z, C_Z, xT, (4, 4), 512)
            sd_cs_pe(pe)
            qs_groups_pe(pe)
            sd_rows_pe(pe)
            gate_pe(pe, 0)
            sd_turn_pe(pe)
            gate_pe(pe, 1)
            sd_y_pe(pe)
            gate_pe(pe, 2)
            sd_off_pe(pe)
            gate_pe(pe, 3)
            sd_out_pe(pe)
            qs_turn_pe(pe)
            gate_pe(pe, 4)
            qs_scores_pe(pe)
            pe.wait_ge(tail.vec, 1)
            split_group_pe(pe, tail, G_GATE + 5, C_SPLIT, 0, normed_hi, xT_rest, part_hi, part_lo, 2)
            branch_pe(pe, 0)
            branch_pe(pe, 1)
            qs_pt_pe(pe)
            qs_pv_pe(pe)
            branch_pe(pe, 2)
            merged_pe(pe)
            pe.wait_ge(tail.vec, 8)
            for n in range(2):
                split_group_pe(pe, tail, G_WO + n, C_WO + 2 * n, 8 + 2 * n, xT_hi, xT_rest, part_hi, part_lo, 2,
                               for_x=(n == 1))

        def mixer_act(act):
            norm_act(act, mix_norm, wait_src=lambda e, m: wait_x(e, NFB, m))
            gm_act(act)
            cq_act(act)
            xbc_act1(act, 0)
            softplus_act(act, dts, dtw, 16, 2)
            xbc_act1(act, 1)
            xbc_act2(act)
            z_act(act)
            qs_act1(act)
            sd_act1(act)
            qs_act2(act)
            gate_act(act, 0)
            gate_act(act, 1)
            gate_act(act, 2)
            sd_act2(act)
            gate_act(act, 3)
            normed_act(act)
            tail_part_act(act, 0, 1)
            gate_act(act, 4)
            branch_in_act(act, 0)
            branch_in_act(act, 1)
            tail_part_act(act, 2, 3)
            gate_act(act, 5)
            tail_part_act(act, 4)
            qs_act3(act, 0)
            tail_part_act(act, 5)
            qs_act3(act, 1)
            tail_part_act(act, 6, 7)
            branch_in_act(act, 2)
            tail_part_act(act, 8, 9)
            merged_in_act(act)
            tail_part_act(act, 10, 11)

        def mixer_vec(vec):
            norm_vec(vec, mix_norm, col[:, R["mix"]:R["mix"] + 8])
            vec.memset(xpad[:, :, 0:3], 0.0).then_inc(xb.vec, 1)
            gm_vec1(vec)
            gm_vec2(vec)
            cq_vec1(vec)
            cq_vec2(vec)
            gm_vec3(vec)
            xbc_vec(vec, 0)
            dt_vec(vec)
            xbc_vec(vec, 1)
            sd_vec1(vec)
            qs_vec1(vec)
            sd_vec2(vec)
            qs_vec2(vec)
            sd_vec3(vec)
            sd_vec4(vec)
            sd_vec5(vec)
            qs_vec3(vec)
            tail_part_vec(vec, 0, 1)
            normed_vec(vec)
            qs_vec4(vec)
            branch_in_vec(vec, 0)
            tail_part_vec(vec, 2)
            branch_in_vec(vec, 1)
            tail_part_vec(vec, 3, 4)
            branch_gate_vec(vec, 0)
            tail_part_vec(vec, 5)
            qs_vec5(vec)
            tail_part_vec(vec, 6)
            qs_vec6(vec)
            branch_gate_vec(vec, 1)
            qs_vec7(vec)
            branch_in_vec(vec, 2)
            tail_part_vec(vec, 7)
            branch_add_vec(vec, 1)
            branch_gate_vec(vec, 2, (0,))
            branch_add_vec(vec, 2, (0,))
            tail_part_vec(vec, 8)
            branch_gate_vec(vec, 2, (1,))
            branch_add_vec(vec, 2, (1,))
            merged_vec(vec)
            merged_in_vec(vec)
            tail_part_vec(vec, 9, 10, 11)

        INV_FREQ = [float(v) for v in (np.float32(1.0) / (np.float32(10000.0) ** (np.arange(0, 32, 2, dtype=np.float32) / np.float32(32))))]
        TWO_PI = 2 * math.pi
        PI_HI = 6.28125
        PI_MID = float(np.float32(1.9350051879882812e-3))
        PI_LO = TWO_PI - PI_HI - PI_MID
        ROUND = 1.5 * 2.0 ** 23
        PI_F = 3.1415925

        def sincos_vec(vec, s, base, a, k, r, c):
            vec.tensor_scalar(k, a, 1 / TWO_PI, ROUND, ALU.mult, ALU.add).then_inc(s.vec, 1)
            vec.wait_ge(s.vec, base + 1)
            vec.tensor_scalar(k, k, ROUND, None, ALU.subtract).then_inc(s.vec, 1)
            vec.wait_ge(s.vec, base + 2)
            vec.scalar_tensor_tensor(out=r, in0=k, scalar=-PI_HI, in1=a, op0=ALU.mult, op1=ALU.add).then_inc(s.vec, 1)
            vec.wait_ge(s.vec, base + 3)
            vec.scalar_tensor_tensor(out=r, in0=k, scalar=-PI_MID, in1=r, op0=ALU.mult, op1=ALU.add).then_inc(s.vec, 1)
            vec.wait_ge(s.vec, base + 4)
            vec.scalar_tensor_tensor(out=r, in0=k, scalar=-PI_LO, in1=r, op0=ALU.mult, op1=ALU.add).then_inc(s.vec, 1)
            vec.wait_ge(s.vec, base + 5)
            vec.tensor_scalar(r, r, PI_F, -PI_F, ALU.min, ALU.max).then_inc(s.vec, 1)
            vec.wait_ge(s.vec, base + 6)
            vec.tensor_scalar(c, r, -1.0, None, ALU.mult).then_inc(s.vec, 1)
            vec.wait_ge(s.vec, base + 7)
            vec.tensor_tensor(c, c, r, ALU.max).then_inc(s.vec, 1)
            vec.wait_ge(s.vec, base + 8)
            vec.tensor_scalar(c, c, -1.0, math.pi / 2, ALU.mult, ALU.add).then_inc(s.vec, 1)

        SINCOS = 9

        pos_i = sb("pos_i", [P, MT], I32)
        pos = sb("pos", [P, MT])
        ang = sb("ang", [P, 4, MT * 16])
        qrs = sb("qrs", [P, 32])
        cst = steps("const", "act vec pool")
        pos_in, x_in = sem("positions_in"), sem("x_in")

        with nc.Block() as block:
            @block.sync
            def _(sync):
                sync.dma_start(pos_i[:, :], t["positions"].rearrange("o (m p) -> p (o m)", p=P),
                               allow_slow_non_contiguous=True).then_inc(pos_in, 16)
                sync.dma_start(x[:, :, :], t["x"].rearrange("o (m p) d -> p (o m) d", p=P)).then_inc(x_in, 16)
                sync.wait_ge(x_in, 16)

            @block.gpsimd
            def _(pool):
                pool.memset(ones[:, :], 1.0).then_inc(cst.pool, 1)
                pool.memset(causal[:, :], 0.0).then_inc(cst.pool, 1)
                pool.wait_ge(cst.pool, 2)
                pool.affine_select(out=ident[:, :], in_=ones[:, :], compare_op=ALU.is_equal, fill=0.0, base=0,
                                   pattern=[[-1, P]], channel_multiplier=1).then_inc(cst.pool, 1)
                pool.affine_select(out=upper[:, :], in_=ones[:, :], compare_op=ALU.is_ge, fill=0.0, base=0,
                                   pattern=[[1, P]], channel_multiplier=-1).then_inc(cst.pool, 1)
                pool.affine_select(out=causal[:, P:TOK], in_=causal[:, P:TOK], compare_op=ALU.is_ge, fill=-1e30, base=0,
                                   pattern=[[-1, P]], channel_multiplier=1).then_inc(cst.pool, 1)

            @block.vector
            def _(vec):
                vec.memset(eps_col[:, :], EPS)
                for i, f in enumerate(INV_FREQ):
                    ins = vec.memset(ang[:, 0, i:i + 1], f)
                ins.then_inc(cst.vec, 1)
                vec.wait_ge(pos_in, 16)
                vec.tensor_copy(pos[:, :], pos_i[:, :]).then_inc(cst.vec, 1)
                vec.wait_ge(cst.vec, 2)
                for m in range(MT):
                    vec.tensor_scalar(ang[:, 1, 16 * m:16 * m + 16], ang[:, 0, 0:16], pos[:, m:m + 1], None,
                                      ALU.mult).then_inc(cst.vec, 1)
                vec.wait_ge(cst.vec, 4)
                sincos_vec(vec, cst, 4, ang[:, 1, :], ang[:, 0, :], ang[:, 2, :], ang[:, 3, :])

            @block.scalar
            def _(act):
                act.wait_ge(cst.vec, 4 + SINCOS)
                act.activation(sin[:, :, :].rearrange("p m n -> p (m n)"), ang[:, 2, :], ACT.Sin).then_inc(cst.act, 1)
                act.activation(cos[:, :, :].rearrange("p m n -> p (m n)"), ang[:, 3, :], ACT.Sin).then_inc(cst.act, 1)

        def clear_semaphores():
            nc.all_engine_barrier()
            for s in all_sems:
                nc.sync.sem_clear(s)
            nc.all_engine_barrier()

        clear_semaphores()

        def ffn_views(name, l):
            w = lay(name + "_w_in", l)
            d = lay(name + "_w_out", l)
            def part(first):
                return lambda j: w[:, :, bass.ds(first + FB * j, FB)].rearrange("o (k p) n -> p (o k) n", p=P)
            return part(0), part(FF), lambda i: d[:, 2 * P * i:2 * P * (i + 1), :].rearrange("o (k p) n -> p (o k) n", p=P)

        with nc.Fori(0, DEPTH) as layer:
            with nc.Block() as block:
                @block.sync
                def _(sync):
                    ffn_sync(sync, f1, 0, *ffn_views("ffn1", layer), aside=lambda e: params_sync(e, layer))
                    mixer_sync(sync, layer)
                    ffn_sync(sync, f2, C_FFN2, *ffn_views("ffn2", layer))

                @block.scalar
                def _(act):
                    first_gain_act(act, layer)
                    norm_act(act, n1)
                    split_act(act, f1, 0, 0)
                    split_x_act(act, n1)
                    split_act(act, f1, 0, 1)
                    ffn_act(act, f1, 0, 0, aside=params_act)
                    mixer_act(act)
                    norm_act(act, n2, wait_src=lambda e, m: wait_x(e, G_WO, m))
                    split_act(act, f2, C_FFN2, 0)
                    split_x_act(act, n2)
                    split_act(act, f2, C_FFN2, 1)
                    ffn_act(act, f2, C_FFN2, G_FFN2)

                @block.vector
                def _(vec):
                    for i in range(4):
                        vec.sem_inc(acc_read[i], 1)
                    norm_vec(vec, n1, col[:, R["ffn1"]:R["ffn1"] + 8], between=first_gain_vec)
                    split_vec(vec, f1, 0, 0)
                    split_x_vec(vec, n1)
                    split_vec(vec, f1, 0, 1)
                    ffn_vec(vec, f1, 0, 0, 0.5, 1, aside=params_vec)
                    mixer_vec(vec)
                    add_to_x(vec, C_WO + 3, G_WO, 1.0, 2)
                    norm_vec(vec, n2, col[:, R["ffn2"]:R["ffn2"] + 8])
                    split_vec(vec, f2, C_FFN2, 0)
                    split_x_vec(vec, n2)
                    split_vec(vec, f2, C_FFN2, 1)
                    ffn_vec(vec, f2, C_FFN2, G_FFN2, 0.5, 3)

                @block.tensor
                def _(pe):
                    pe.sem_inc(products_done, RING)
                    norm_pe(pe, n1)
                    first_gain_pe(pe)
                    ffn_pe(pe, f1, n1, 0, 0, aside=params_pe)
                    mixer_pe(pe)
                    norm_pe(pe, n2)
                    ffn_pe(pe, f2, n2, C_FFN2, G_FFN2)
            clear_semaphores()


        DH = 4
        HD = 128
        CH = 64
        NS = 16
        (G_Q2, C_Q2), (G_K2, C_K2), (G_V2, C_V2), (G_Z2, C_Z2), (G_U2, C_U2) = [(i, 2 * i) for i in range(5)]
        G_MK, C_MK = 5, 10
        G_MV, C_MV = 7, 14
        G_GLU, C_GLU = 9, 18
        G_WO2, C_WO2 = 10, 19
        G_XQ, C_XQ = 12, 23
        G_XO, C_XO = 14, 27
        G_FFN3, C_FFN3 = 16, 31
        R2 = dict(mix=0, x=8, mem=16, ffn=24, convw=32, dng=80, bglu=81, d=85, are=89, aim=105)
        N_ROWS2 = 121

        rot_c = big(0, NS, TOK)
        rot_s = big(4096, NS, TOK)
        kmT = big(8192, KD, TOK)
        vm = big(10240, MT, D)
        z_s = big(12288, MT, 512)
        uT = big(13312, 4, TOK)
        A0 = 14336
        xpad2 = big(A0, 12, TOK + 3)
        conv2 = big(A0 + 3108, 12, TOK)
        b_in = big(A0, 2, NS, 16)
        c_in = big(A0 + 512, 2, 4, 64)
        bbt = big(A0 + 1024, 4, NS, 16)
        Zb = big(A0 + 2048, 2, NS, 32)
        Zc = big(A0 + 3072, 2, 4, P)
        same = big(A0 + 4096, 7, P)
        X = big(A0, 8, P)
        XT = big(A0 + 1024, 8, P)
        Y = big(A0 + 2048, 8, P)
        CT = big(A0 + 3072, 8, P)
        u_sol = big(A0 + 4096, 8, P)
        wT = big(A0 + 5120, 8, P)
        A1 = A0 + 6180
        q_tok = big(A1, MT, 512)
        k_tok = big(A1 + 1024, MT, 512)
        v_tok2 = big(A1 + 2048, MT, 512)
        kbe = big(A1 + 3072, MT, 512)
        knT = big(A1 + 4096, DH, TOK)
        kbT = big(A1 + 5120, DH, TOK)
        qnT = big(A1 + 6144, DH, TOK)
        qgT = big(A1 + 7168, DH, TOK)
        dec = big(A1 + 8192, 8, P)
        LT = big(A1 + 9216, 8, P)
        attnT = big(A1 + 10240, 8, P)
        kb = big(A1 + 10240, MT, 512)
        memx = big(A1 + 8192, MT, D)
        vnew = big(A1 + 4096, MT, 512)
        S2 = big(A1 + 5120, 512)
        sq2 = big(A1 + 5632, 512)
        o_s = big(A1 + 6144, MT, 512)
        lvl = big(A1 + 11264, 6, P)
        cTi = big(A1 + 12032, 4, P)
        bbT = (ws_in, wsT)
        cT = (gmv[:, :].rearrange("p (c n) -> p c n", c=4), cTi)
        memT = xn[:, :, :].rearrange("p m d -> p (m d)").rearrange("p (k n) -> p k n", k=KD)
        zin = big(A0, 2, 2, TOK)
        zsc = big(A0 + 1024, 2, 2, TOK)
        xst = big(A0 + 2048, 2, 2, TOK)
        tv = big(A0 + 3072, 2, 4, TOK)
        by_cos = big(A0 + 5120, 2, 2, TOK)
        by_sin = big(A1 + 2048, 2, 2, TOK)
        yg = big(A1, 4, TOK)
        ysig = big(A1 + 1024, 4, TOK)
        qcT = big(A0, KD, TOK)
        pc = big(A0 + 2048, 8, TOK)
        PTc = big(A0 + 4096, 2, 4, TOK)
        fin_g = xT[:, :, :].rearrange("p k n -> p (k n)")[:, 0:D]

        e_tmp = big(33060, 256)
        blk = big(33316, P)
        ublk = big(33444, P)
        s5w = big(33572, 26, NS)
        par2 = sb("par2", [P, 4])
        bet = sb("bet", [P, 8])
        cs2 = sb("cs2", [P, 40])
        st2 = sb("st2", [P, 96])
        small2 = sb("small2", [P, 8])

        p_in, gain2_in, mem_in, fin_in = sem("params2_in"), sem("first_gain2_in"), sem("memory_in"), sem("final_gain_in")
        p2, sp, dn, rc, dt2, xa = (steps(n) for n in ("params2", "s5_params", "delta", "recurrence", "dt2", "cross"))
        mk, c2, iv = steps("masks2", "vec pool"), steps("conv2", "vec act"), steps("inverse", "vec pe")
        s5, gl = steps("s5", "vec pool pe"), steps("glu", "vec act")
        rot = sem("rotations_ready")
        nm, nx, nmem, n3, nf = (steps(n) for n in ("mix2_norm", "cross_norm", "memory_norm", "ffn3_norm", "final_norm"))
        f3 = ffn_sems("ffn3")
        out_done = sem("out_done")

        def first_gain2_act(act):
            act.dma_start(vecs[0:8, :], t["norm_mix_g_2"].rearrange("o (k p) -> (o k) p", p=P)).then_inc(gain2_in, 16)

        def first_gain2_pe(pe):
            pe.wait_ge(gain2_in, 16)
            pe.transpose(acc[3][:, 0:8], vecs[0:8, :], ident[0:8, 0:8]).then_inc(p2.pe, 1)

        def first_gain2_vec(vec):
            vec.wait_ge(p2.pe, 1)
            vec.tensor_copy(col[:, 0:8], acc[3][:, 0:8]).then_inc(p2.vec, 1)
            vec.wait_ge(p2.vec, 1)

        def params2_sync(sync):
            for name, r in (("s5_a_re_2", "are"), ("s5_a_im_2", "aim")):
                sync.dma_start(vecs[R2[r]:R2[r] + NS, :],
                               t[name].rearrange("o (k g) p -> (o k) (g p)", g=2)).then_inc(p_in, 16)
            for i, name in enumerate(("s5_b_re_2", "s5_b_im_2")):
                sync.dma_start(b_in[:, i], t[name].rearrange("o (k g) p c -> (o g p) k c", g=2)).then_inc(p_in, 16)
            for i, name in enumerate(("s5_c_re_2", "s5_c_im_2")):
                sync.dma_start(c_in[:, i], t[name].rearrange("o (k g) c p -> (o g c) k p", g=8)).then_inc(p_in, 16)

        def params2_act(act):
            for g in range(2):
                act.dma_start(s5w[64 * g:64 * g + 64, 0, :],
                              t["s5_log_dt_2"].rearrange("o (k g) -> g (o k)", g=2)[g:g + 1, :].broadcast_to([64, NS]),
                              allow_slow_non_contiguous=True).then_inc(p_in, 16)
            act.dma_start(vecs[R2["convw"]:R2["convw"] + 48, :],
                          t["conv_w_2"].rearrange("o j (k p) -> (o j k) p", p=P)).then_inc(p_in, 16)
            act.dma_start(vecs[R2["d"]:R2["d"] + 4, :],
                          t["s5_d_2"].rearrange("o (k g) c -> (o k) (g c)", g=8)).then_inc(p_in, 16)
            for name, r, k in (("norm_x_g_2", "x", 8), ("norm_mem_g_2", "mem", 8), ("norm_ffn_g_2", "ffn", 8),
                               ("dn_norm_g_2", "dng", 1), ("s5_b_glu_2", "bglu", 4)):
                act.dma_start(vecs[R2[r]:R2[r] + k, :], t[name].rearrange("o (k p) -> (o k) p", p=P)).then_inc(p_in, 16)
            act.dma_start(small2[:, 0:4], t["dn_dt_bias_2"].broadcast_to([P, 4])).then_inc(p_in, 16)
            act.dma_start(small2[:, 4:8], t["dn_a_log_2"].broadcast_to([P, 4])).then_inc(p_in, 16)
            act.wait_ge(p_in, 16 * N_PAR2)
            act.activation(small2[:, 4:8], small2[:, 4:8], ACT.Exp).then_inc(p2.act, 1)

        N_PAR2 = 6 + 11

        def masks_pool(pool):
            pool.memset(Zb, 0.0).then_inc(mk.pool, 1)
            for i in range(1, 7):
                b = 2 ** i
                v = same[:, i].rearrange("p (n b) -> p n b", b=b)
                pool.affine_select(out=v, in_=ones[:, :].rearrange("p (n b) -> p n b", b=b), compare_op=ALU.is_ge,
                                   fill=0.0, base=0, pattern=[[-b, P // b], [0, b]], channel_multiplier=1).then_inc(mk.pool, 1)
            for i in range(1, 7):
                b = 2 ** i
                v = same[:, i].rearrange("p (n b) -> p n b", b=b)
                pool.wait_ge(mk.pool, 1 + i)
                pool.affine_select(out=v, in_=v, compare_op=ALU.is_ge, fill=0.0, base=b - 1,
                                   pattern=[[b, P // b], [0, b]], channel_multiplier=-1).then_inc(mk.pool, 1)

        def masks_vec(vec):
            vec.tensor_copy(same[:, 0], ident[:, :]).then_inc(mk.vec, 1)
            vec.wait_ge(mk.vec, 1)
            vec.wait_ge(mk.pool, 13)
            vec.tensor_copy(blk[:, :], same[:, 6]).then_inc(mk.vec, 1)
            vec.tensor_tensor(ublk[:, :], same[:, 6], upper[:, :], ALU.mult).then_inc(mk.vec, 1)
            vec.tensor_tensor(lvl, same[:, 1:7], same[:, 0:6], ALU.subtract).then_inc(mk.vec, 1)
            vec.wait_ge(mk.vec, 4)
            vec.tensor_tensor(lvl, lvl, upper[:, :].unsqueeze(1).broadcast_to([P, 6, P]), ALU.mult).then_inc(mk.vec, 1)
            vec.tensor_reduce(par2[:, 0:1], same[:, 4, 0:P:32], AX, ALU.add).then_inc(mk.vec, 1)
            vec.wait_ge(mk.vec, 6)
            vec.tensor_scalar(par2[:, 1:2], par2[:, 0:1], -1.0, 1.0, ALU.mult, ALU.add).then_inc(mk.vec, 1)
            vec.wait_ge(mk.vec, 7)
            vec.tensor_scalar(par2[:, 2:4], par2[:, 0:2], -1.0, None, ALU.mult).then_inc(mk.vec, 1)
            vec.wait_ge(mk.vec, 8)

        def params2_pe(pe):
            pe.wait_ge(p2.act, 1)
            pe.wait_ge(nm.vec, NORM_DONE)
            pe.transpose(turn[0][:, 0:N_ROWS2], vecs[0:N_ROWS2, :], ident[0:N_ROWS2, 0:N_ROWS2]).then_inc(p2.pe, 1)

        def params2_vec(vec):
            vec.wait_ge(p2.pe, 2)
            vec.tensor_copy(col[:, 8:N_ROWS2], turn[0][:, 8:N_ROWS2]).then_inc(p2.vec, 1)
            vec.tensor_scalar(small2[:, 4:8], small2[:, 4:8], -1.0, None, ALU.mult).then_inc(p2.vec, 1)
            vec.wait_ge(p2.vec, 3)

        LDT, DTS, AR, AI, MAG, KR, SR, CR, SI, CO, ABR, ABI, NR, DEN, T1, T2, COR, COI = range(18)
        PW = 18

        def s5p_act(act):
            act.wait_ge(p2.act, 1)
            act.activation(s5w[:, DTS], s5w[:, LDT], ACT.Exp).then_inc(sp.act, 1)
            act.wait_ge(sp.vec, 1)
            act.activation(s5w[:, MAG], s5w[:, AR], ACT.Exp).then_inc(sp.act, 1)
            act.wait_ge(sp.vec, 2 + SINCOS)
            act.activation(s5w[:, SI], s5w[:, SR], ACT.Sin).then_inc(sp.act, 1)
            act.activation(s5w[:, CO], s5w[:, CR], ACT.Sin).then_inc(sp.act, 1)

        def s5p_vec(vec):
            a_re, a_im = col[:, R2["are"]:R2["are"] + NS], col[:, R2["aim"]:R2["aim"] + NS]

            def w(i):
                return s5w[:, i]
            vec.wait_ge(sp.act, 1)
            vec.tensor_tensor(w(AR), a_re, w(DTS), ALU.mult).then_inc(sp.vec, 1)
            vec.tensor_tensor(w(AI), a_im, w(DTS), ALU.mult).then_inc(sp.vec, 1)
            vec.wait_ge(sp.vec, 2)
            sincos_vec(vec, sp, 2, w(AI), w(KR), w(SR), w(CR))
            vec.wait_ge(sp.act, 4)
            vec.tensor_tensor(w(ABR), w(MAG), w(CO), ALU.mult).then_inc(sp.vec, 1)
            vec.tensor_tensor(w(ABI), w(MAG), w(SI), ALU.mult).then_inc(sp.vec, 1)
            vec.tensor_tensor(w(T1), a_re, a_re, ALU.mult).then_inc(sp.vec, 1)
            vec.tensor_tensor(w(T2), a_im, a_im, ALU.mult).then_inc(sp.vec, 1)
            vec.wait_ge(sp.vec, 15)
            vec.tensor_scalar(w(NR), w(ABR), 1.0, None, ALU.subtract).then_inc(sp.vec, 1)
            vec.tensor_tensor(w(DEN), w(T1), w(T2), ALU.add).then_inc(sp.vec, 1)
            vec.wait_ge(sp.vec, 17)
            vec.reciprocal(w(DEN), w(DEN)).then_inc(sp.vec, 1)
            vec.tensor_tensor(w(T1), w(NR), a_re, ALU.mult).then_inc(sp.vec, 1)
            vec.tensor_tensor(w(T2), w(ABI), a_im, ALU.mult).then_inc(sp.vec, 1)
            vec.wait_ge(sp.vec, 20)
            vec.tensor_tensor(w(COR), w(T1), w(T2), ALU.add).then_inc(sp.vec, 1)
            vec.wait_ge(sp.vec, 21)
            vec.tensor_tensor(w(COR), w(COR), w(DEN), ALU.mult).then_inc(sp.vec, 1)
            vec.tensor_tensor(w(T1), w(ABI), a_re, ALU.mult).then_inc(sp.vec, 1)
            vec.tensor_tensor(w(T2), w(NR), a_im, ALU.mult).then_inc(sp.vec, 1)
            vec.wait_ge(sp.vec, 24)
            vec.tensor_tensor(w(COI), w(T1), w(T2), ALU.subtract).then_inc(sp.vec, 1)
            vec.wait_ge(sp.vec, 25)
            vec.tensor_tensor(w(COI), w(COI), w(DEN), ALU.mult).then_inc(sp.vec, 1)
            vec.wait_ge(sp.vec, 26)
            for i, (b, c) in enumerate(((0, COR), (1, COI), (1, COR), (0, COI))):
                vec.tensor_tensor(bbt[:, i], b_in[:, b], over(s5w[:, c], NS, 16), ALU.mult).then_inc(sp.vec, 1)
            vec.wait_ge(sp.vec, 30)
            vec.wait_ge(mk.pool, 1)
            for g in range(2):
                half = slice(64 * g, 64 * g + 64)
                for i, op in enumerate((ALU.subtract, ALU.add)):
                    vec.tensor_tensor(Zb[half, i, :, 16 * g:16 * g + 16], bbt[half, 2 * i], bbt[half, 2 * i + 1],
                                      op).then_inc(sp.vec, 1)
            for i in range(2):
                for g in range(2):
                    vec.tensor_scalar(Zc[:, i, :, 64 * g:64 * g + 64], c_in[:, i], par2[:, 2 * i + g:2 * i + g + 1], None,
                                      ALU.mult).then_inc(sp.vec, 1)

        def s5p_pe(pe):
            pe.wait_ge(sp.vec, 38)
            for i in range(2):
                for c in range(4):
                    ins = pe.transpose(turn[i][:, c * P:(c + 1) * P],
                                       Zb[:, i, 4 * c:4 * c + 4, :].rearrange("p k c -> p (k c)"), ident[:, :])
                ins.then_inc(sp.pe, 1)
            for i in range(2):
                for c in range(4):
                    ins = pe.transpose(turn[2 + i][:, c * P:(c + 1) * P], Zc[:, i, c, :], ident[:, :])
                ins.then_inc(sp.pe, 1)

        def s5p_vec2(vec):
            for i, dst in enumerate(bbT + cT):
                vec.wait_ge(sp.pe, 1 + i)
                vec.tensor_copy(dst[:, :, :], heads(turn[i][:, :], 4)).then_inc(sp.vec, 1)

        def rotations_pool(pool):
            pool.memset(rot_c[:, :, 0:1], 1.0).then_inc(rot, 1)
            pool.memset(rot_s[:, :, 0:1], 0.0).then_inc(rot, 1)
            pool.wait_ge(sp.act, 4)
            pool.tensor_copy(s5w[:, PW], s5w[:, CO]).then_inc(rot, 1)
            pool.tensor_copy(s5w[:, PW + 1], s5w[:, SI]).then_inc(rot, 1)
            done = 4
            pool.wait_ge(rot, done)
            for k in range(8):
                n = 2 ** k
                pr, pi = s5w[:, PW + 2 * (k % 2)], s5w[:, PW + 1 + 2 * (k % 2)]
                qr, qi = s5w[:, PW + 2 - 2 * (k % 2)], s5w[:, PW + 3 - 2 * (k % 2)]
                tiles = min(NS, 256 // n)
                for t0 in range(0, NS, tiles):
                    ts = slice(t0, t0 + tiles)
                    tmp = e_tmp[:, 0:tiles * n].rearrange("p (k n) -> p k n", k=tiles)
                    er, ei = rot_c[:, ts, 0:n], rot_s[:, ts, 0:n]
                    nr_, ni_ = rot_c[:, ts, n:2 * n], rot_s[:, ts, n:2 * n]
                    c_, s_ = over(pr[:, ts], tiles, n), over(pi[:, ts], tiles, n)
                    pool.tensor_tensor(nr_, er, c_, ALU.mult).then_inc(rot, 1)
                    pool.tensor_tensor(ni_, ei, c_, ALU.mult).then_inc(rot, 1)
                    pool.tensor_tensor(tmp, ei, s_, ALU.mult).then_inc(rot, 1)
                    done += 3
                    pool.wait_ge(rot, done)
                    pool.tensor_tensor(nr_, nr_, tmp, ALU.subtract).then_inc(rot, 1)
                    done += 1
                    pool.wait_ge(rot, done)
                    pool.tensor_tensor(tmp, er, s_, ALU.mult).then_inc(rot, 1)
                    done += 1
                    pool.wait_ge(rot, done)
                    pool.tensor_tensor(ni_, ni_, tmp, ALU.add).then_inc(rot, 1)
                    done += 1
                    pool.wait_ge(rot, done)
                if k < 7:
                    for i, (a, b) in enumerate(((pr, pr), (pi, pi), (pr, pi), (pr, pi))):
                        pool.tensor_tensor(s5w[:, PW + 4 + i], a, b, ALU.mult).then_inc(rot, 1)
                    done += 4
                    pool.wait_ge(rot, done)
                    pool.tensor_tensor(qr, s5w[:, PW + 4], s5w[:, PW + 5], ALU.subtract).then_inc(rot, 1)
                    pool.tensor_tensor(qi, s5w[:, PW + 6], s5w[:, PW + 7], ALU.add).then_inc(rot, 1)
                    done += 2
                    pool.wait_ge(rot, done)

        ROT_DONE = 4 + sum(6 * max(1, NS * 2 ** k // 256) for k in range(8)) + 6 * 7

        def second_sync(sync):
            def cols(name, lo, hi, k0, k1):
                return t[name][:, k0 * P:k1 * P, lo:hi].rearrange("o (k p) n -> p (o k) n", p=P)

            def two(c, name, lo, n):
                for i in range(2):
                    load(sync, c + i, cols(name, lo, lo + n, 4 * i, 4 * i + 4), 4, n)
            two(C_Q2, "w_in_2", 0, 512)
            params2_sync(sync)
            two(C_K2, "w_in_2", 512, 512)
            sync.dma_start(memx, t["mem_2"].rearrange("o (m p) d -> p (o m) d", p=P)).then_inc(mem_in, 16)
            two(C_V2, "w_in_2", 1024, 512)
            two(C_Z2, "w_in_2", 1536, 520)
            two(C_U2, "w_in_2", 2056, 512)
            for i in range(2):
                two(C_MK + 2 * i, "w_xk_2", 512 * i, 512)
            for i in range(2):
                two(C_MV + 2 * i, "w_xv_2", 512 * i, 512)
            load(sync, C_GLU, cols("s5_w_glu_2", 0, 512, 0, 4), 4, 512)
            for i in range(2):
                two(C_WO2 + 2 * i, "w_out_2", 512 * i, 512)
            for i in range(2):
                two(C_XQ + 2 * i, "w_xq_2", 512 * i, 512)
            for i in range(2):
                two(C_XO + 2 * i, "w_xo_2", 512 * i, 512)

            def part(name):
                return lambda j: t[name][:, :, bass.ds(FB * j, FB)].rearrange("o (k p) n -> p (o k) n", p=P)
            ffn_sync(sync, f3, C_FFN3, part("w_gate_2"), part("w_up_2"),
                     lambda i: t["w_down_2"][:, 2 * P * i:2 * P * (i + 1), :].rearrange("o (k p) n -> p (o k) n", p=P))

        CONV_GROUPS = ((G_Q2, C_Q2), (G_K2, C_K2), (G_V2, C_V2))

        def conv2_act1(act):
            act.wait_ge(sp.pe, 4)
            act.wait_ge(mk.vec, 8)
            act.wait_ge(c2.vec, 1)
            for i, (G, c) in enumerate(CONV_GROUPS):
                wait_products(act, c + 1)
                for q in range(2):
                    f = 4 * i + 2 * q
                    act.activation(xpad2[:, f:f + 2, 3:3 + TOK], heads(acc[bank(G, q)][:, :], 2),
                                   ACT.Copy).then_inc(acc_read[bank(G, q)], 1)

        def conv2_vec(vec):
            for j in range(4):
                for f in range(12):
                    w = col[:, R2["convw"] + 12 * j + f:R2["convw"] + 12 * j + f + 1]
                    if j == 0:
                        wait_acc_read(vec, CONV_GROUPS[f // 4][0], (f % 4) // 2)
                        vec.tensor_scalar(conv2[:, f, :], xpad2[:, f, 0:TOK], w, None, ALU.mult).then_inc(c2.vec, 1)
                    else:
                        vec.wait_ge(c2.vec, 1 + 12 * (j - 1) + f + 1)
                        vec.scalar_tensor_tensor(out=conv2[:, f, :], in0=xpad2[:, f, j:j + TOK], scalar=w,
                                                 in1=conv2[:, f, :], op0=ALU.mult, op1=ALU.add).then_inc(c2.vec, 1)

        def conv2_act2(act):
            for i in range(3):
                act.wait_ge(c2.vec, 37 + 4 * i + 4)
                act.activation(conv2[:, 4 * i:4 * i + 4, :], conv2[:, 4 * i:4 * i + 4, :], ACT.Silu).then_inc(c2.act, 1)

        def ab_pe(pe):
            wait_chunk(pe, C_Z2)
            wait_chunk(pe, C_Z2 + 1)
            for m in range(MT):
                for k in range(KD):
                    ins = pe.matmul(turn[m][:, 0:8], xT[:, k, m * P:(m + 1) * P],
                                    slot(C_Z2 + k // 4, 4, 520)[:, k % 4, 512:520], start=(k == 0), stop=(k == KD - 1))
                ins.then_inc(dt2.pe, 1)

        def ab_vec(vec):
            for m in range(MT):
                vec.wait_ge(dt2.pe, 1 + m)
                vec.tensor_tensor(dtw[:, 0, 4 * m:4 * m + 4], turn[m][:, 0:4], small2[:, 0:4], ALU.add).then_inc(dt2.vec, 1)
            softplus_vec(vec, dt2, dtw, 8, 2)
            vec.tensor_tensor(heads(dtw[:, 11, 0:8], MT), heads(dtw[:, 10, 0:8], MT),
                              small2[:, 4:8].unsqueeze(1).broadcast_to([P, MT, 4]), ALU.mult).then_inc(dt2.vec, 1)

        def ab_act(act):
            softplus_act(act, dt2, dtw, 8, 2)
            for m in range(MT):
                act.activation(bet[:, 4 * m:4 * m + 4], turn[m][:, 4:8], ACT.Sigmoid).then_inc(dt2.act, 1)

        g2 = dtw[:, 11, 0:8]
        GC, TOT, ALC, EG, ED = 0, 8, 16, 32, 8

        def dn_cs_pe(pe):
            pe.wait_ge(dt2.vec, 16)
            pe.wait_ge(dt2.act, 4)
            pe.wait_ge(sp.vec, 42)
            pe.matmul(turn[2][:, 0:8], ublk[:, :], g2, start=True, stop=True)
            pe.matmul(turn[2][:, 8:16], blk[:, :], g2, start=True, stop=True)
            for b in range(2):
                ins = pe.matmul(turn[2][:, 16 + 8 * b:24 + 8 * b], blk[:, CH * b:CH * b + 1].broadcast_to([P, P]), g2,
                                start=True, stop=True)
            ins.then_inc(dn.pe, 1)
            for m in range(MT):
                for h in range(DH):
                    j = 4 * m + h
                    ins = pe.matmul(turn[m][:, h * P:(h + 1) * P], g2[:, j:j + 1].broadcast_to([P, P]), ublk[:, :],
                                    start=True, stop=True)
                ins.then_inc(dn.pe, 1)

        def dn_cs_vec(vec):
            vec.wait_ge(dn.pe, 1)
            vec.tensor_copy(cs2[:, 0:32], turn[2][:, 0:32]).then_inc(dn.vec, 1)
            vec.wait_ge(dn.vec, 1)
            vec.tensor_tensor(cs2[:, 8:16], cs2[:, 8:16], cs2[:, 0:8], ALU.subtract).then_inc(dn.vec, 1)
            vec.wait_ge(nmem.pe, 4)
            for m in range(MT):
                vec.wait_ge(dn.pe, 2 + m)
                for h in range(DH):
                    j = 4 * m + h
                    ins = vec.tensor_scalar(dec[:, j, :], turn[m][:, h * P:(h + 1) * P], cs2[:, j:j + 1], 0.0,
                                            ALU.subtract, ALU.min)
                ins.then_inc(dn.vec, 1)

        def dn_cs_act(act):
            act.wait_ge(dn.vec, 2)
            act.activation(cs2[:, 32:40], cs2[:, 0:8], ACT.Exp).then_inc(dn.act, 1)
            act.activation(cs2[:, 8:32], cs2[:, 8:32], ACT.Exp).then_inc(dn.act, 1)
            for m in range(MT):
                act.wait_ge(dn.vec, 3 + m)
                act.activation(dec[:, 4 * m:4 * m + 4, :], dec[:, 4 * m:4 * m + 4, :], ACT.Exp).then_inc(dn.act, 1)

        def dn_turn_pe(pe):
            pe.wait_ge(dn.vec, 4)
            for kind in range(3):
                pe.wait_ge(c2.act, 1 + kind)
                for m in range(MT):
                    r = 2 * kind + m
                    if r >= 4:
                        pe.wait_ge(dn.vec, 5 + r - 4)
                    for f in range(4):
                        ins = pe.transpose(turn[r % 4][:, f * P:(f + 1) * P], conv2[:, 4 * kind + f, m * P:(m + 1) * P], ident[:, :])
                    ins.then_inc(dn.pe, 1)

        def dn_turn_vec(vec):
            for r in range(6):
                kind, m = r // 2, r % 2
                vec.wait_ge(dn.pe, 4 + r)
                vec.tensor_copy((q_tok, k_tok, v_tok2)[kind][:, m, :], turn[r % 4][:, :]).then_inc(dn.vec, 1)
            for r in range(4):
                vec.wait_ge(dn.act, 5 + r)
                vec.tensor_reduce(st2[:, 4 * r:4 * r + 4], heads((kbe, kb)[r // 2][:, r % 2, :], 4), AX, ALU.add).then_inc(dn.vec, 1)
            vec.wait_ge(dn.act, 9)
            vec.reciprocal(st2[:, 16:32], st2[:, 16:32]).then_inc(dn.vec, 1)
            vec.wait_ge(dn.vec, 15)
            vec.tensor_scalar(st2[:, 16:24], st2[:, 16:24], HD ** -0.5, None, ALU.mult).then_inc(dn.vec, 1)
            vec.wait_ge(dn.vec, 16)
            for r in range(4):
                d = (q_tok, k_tok)[r // 2][:, r % 2, :]
                vec.tensor_tensor(heads(d, 4), heads(d, 4), over(st2[:, 16 + 4 * r:20 + 4 * r], 4, P), ALU.mult).then_inc(dn.vec, 1)
            vec.wait_ge(dt2.act, 4)
            for m in range(MT):
                vec.wait_ge(dn.vec, 19 + m)
                vec.tensor_tensor(heads(kb[:, m, :], 4), heads(k_tok[:, m, :], 4), over(bet[:, 4 * m:4 * m + 4], 4, P),
                                  ALU.mult).then_inc(dn.vec, 1)
            vec.wait_ge(dn.act, 4)
            for m in range(MT):
                d = dec[:, 4 * m:4 * m + 4, :]
                vec.tensor_tensor(d, d, ublk[:, :].unsqueeze(1).broadcast_to([P, 4, P]), ALU.mult).then_inc(dn.vec, 1)

        def dn_turn_act(act):
            for r in range(4):
                act.wait_ge(dn.vec, 5 + r)
                act.activation((kbe, kb)[r // 2][:, r % 2, :], (q_tok, k_tok)[r // 2][:, r % 2, :], ACT.Square).then_inc(dn.act, 1)
            act.wait_ge(dn.vec, 14)
            act.activation(st2[:, 16:32], st2[:, 0:16], ACT.Sqrt, bias=eps_col[:, 0:1]).then_inc(dn.act, 1)

        def dn_turn2_pe(pe):
            for i, (src, w) in enumerate(((k_tok, 19), (kb, 21), (q_tok, 17))):
                for m in range(MT):
                    r = 2 * i + m
                    pe.wait_ge(dn.vec, w + m)
                    if r >= 4:
                        pe.wait_ge(dn.vec, 25 + r - 4)
                    for h in range(DH):
                        ins = pe.transpose(turn[r % 4][:, h * P:(h + 1) * P], src[:, m, h * P:(h + 1) * P], ident[:, :])
                    ins.then_inc(dn.pe, 1)

        def dn_turn2_vec(vec):
            for r in range(6):
                vec.wait_ge(dn.pe, 10 + r)
                vec.tensor_copy((knT, kbT, qnT)[r // 2][:, :, (r % 2) * P:(r % 2 + 1) * P], heads(turn[r % 4][:, :], 4)).then_inc(dn.vec, 1)
            vec.wait_ge(dn.act, 2)
            for m in range(MT):
                eg = over(cs2[:, EG + 4 * m:EG + 4 * m + 4], 4, P)
                vec.tensor_tensor(heads(q_tok[:, m, :], 4), heads(q_tok[:, m, :], 4), eg, ALU.mult).then_inc(dn.vec, 1)
                vec.tensor_tensor(heads(kbe[:, m, :], 4), heads(kb[:, m, :], 4), eg, ALU.mult).then_inc(dn.vec, 1)
                vec.tensor_tensor(heads(k_tok[:, m, :], 4), heads(k_tok[:, m, :], 4),
                                  over(cs2[:, ED + 4 * m:ED + 4 * m + 4], 4, P), ALU.mult).then_inc(dn.vec, 1)
                vec.tensor_tensor(heads(v_tok2[:, m, :], 4), heads(v_tok2[:, m, :], 4),
                                  over(bet[:, 4 * m:4 * m + 4], 4, P), ALU.mult).then_inc(dn.vec, 1)

        def dn_kk_pe(pe):
            pe.wait_ge(dn.vec, 30)
            for m in range(MT):
                for h in range(DH):
                    ins = pe.matmul(turn[m][:, h * P:(h + 1) * P], knT[:, h, m * P:(m + 1) * P], kbT[:, h, m * P:(m + 1) * P],
                                    start=True, stop=True)
                ins.then_inc(dn.pe, 1)
            for m in range(MT):
                for h in range(DH):
                    ins = pe.matmul(turn[2 + m][:, h * P:(h + 1) * P], knT[:, h, m * P:(m + 1) * P], qnT[:, h, m * P:(m + 1) * P],
                                    start=True, stop=True)
                ins.then_inc(dn.pe, 1)

        def dn_kk_vec(vec):
            vec.wait_ge(dn.vec, 36)
            for m in range(MT):
                vec.wait_ge(dn.pe, 16 + m)
                vec.tensor_tensor(LT[:, 4 * m:4 * m + 4, :], dec[:, 4 * m:4 * m + 4, :], heads(turn[m][:, :], 4),
                                  ALU.mult).then_inc(dn.vec, 1)
            for m in range(MT):
                vec.wait_ge(dn.pe, 18 + m)
                vec.tensor_tensor(attnT[:, 4 * m:4 * m + 4, :], dec[:, 4 * m:4 * m + 4, :], heads(turn[2 + m][:, :], 4),
                                  ALU.mult).then_inc(dn.vec, 1)

        def dn_qg_pe(pe):
            pe.wait_ge(dn.vec, 42)
            for m in range(MT):
                for h in range(DH):
                    ins = pe.transpose(turn[2 + m][:, h * P:(h + 1) * P], q_tok[:, m, h * P:(h + 1) * P], ident[:, :])
                ins.then_inc(dn.pe, 1)

        def dn_qg_vec(vec):
            for m in range(MT):
                vec.wait_ge(dn.pe, 20 + m)
                vec.tensor_copy(qgT[:, :, m * P:(m + 1) * P], heads(turn[2 + m][:, :], 4)).then_inc(dn.vec, 1)

        def memory_values_pe(pe, part):
            n, i, m, k0 = part // 8, part // 4 % 2, part // 2 % 2, 2 * (part % 2)
            G, c = G_MV + n, C_MV + 2 * n + i
            if part % 4 == 0:
                wait_chunk(pe, c)
            if i == 0 and k0 == 0:
                wait_acc_free(pe, G, m)
            for k in range(k0, k0 + 2):
                ins = pe.matmul(acc[bank(G, m)][:, :], memT[:, 4 * i + k, m * P:(m + 1) * P], slot(c, 4, 512)[:, k, :],
                                start=(i == 0 and k == 0), stop=(i == 1 and k == 3))
            if part % 4 == 3:
                ins.then_inc(products_done, 1)

        def mlvl(i):
            return lvl[:, i].unsqueeze(1).broadcast_to([P, 4, P])

        def quad(a, m):
            return a[:, 4 * m:4 * m + 4, :]

        def inv_vec(vec):
            vec.wait_ge(dn.vec, 42)
            for m in range(MT):
                vec.tensor_tensor(quad(CT, m), quad(LT, m), mlvl(0), ALU.mult).then_inc(iv.vec, 1)
                vec.wait_ge(iv.vec, 1 + 2 * m)
                vec.tensor_tensor(quad(XT, m), ident[:, :].unsqueeze(1).broadcast_to([P, 4, P]), quad(CT, m),
                                  ALU.subtract).then_inc(iv.vec, 1)
            for m in range(MT):
                vec.wait_ge(iv.pe, 1 + m)
                vec.tensor_copy(quad(X, m), heads(turn[m][:, :], 4)).then_inc(iv.vec, 1)
            for i in range(1, 6):
                v, p = 6 + 8 * (i - 1), 2 + 4 * (i - 1)
                for m in range(MT):
                    vec.tensor_tensor(quad(CT, m), quad(LT, m), mlvl(i), ALU.mult).then_inc(iv.vec, 1)
                for m in range(MT):
                    vec.wait_ge(iv.pe, p + 1 + m)
                    vec.tensor_copy(quad(Y, m), heads(turn[m][:, :], 4)).then_inc(iv.vec, 1)
                for m in range(MT):
                    vec.wait_ge(iv.pe, p + 3 + m)
                    vec.tensor_tensor(quad(XT, m), quad(XT, m), heads(turn[2 + m][:, :], 4), ALU.subtract).then_inc(iv.vec, 1)
                    vec.tensor_tensor(quad(X, m), quad(X, m), heads(turn[m][:, :], 4), ALU.subtract).then_inc(iv.vec, 1)

        INV_DONE = 6 + 8 * 5

        def inv_pe(pe):
            for m in range(MT):
                pe.wait_ge(iv.vec, 2 + 2 * m)
                for h in range(DH):
                    ins = pe.transpose(turn[m][:, h * P:(h + 1) * P], XT[:, 4 * m + h, :], ident[:, :])
                ins.then_inc(iv.pe, 1)
            for i in range(1, 6):
                v = 6 + 8 * (i - 1)
                for m in range(MT):
                    pe.wait_ge(iv.vec, v + 1 + m)
                    for h in range(DH):
                        j = 4 * m + h
                        ins = pe.matmul(turn[m][:, h * P:(h + 1) * P], CT[:, j, :], X[:, j, :], start=True, stop=True)
                    ins.then_inc(iv.pe, 1)
                for m in range(MT):
                    pe.wait_ge(iv.vec, v + 3 + m)
                    if i == 1:
                        pe.wait_ge(dn.vec, 44)
                    for h in range(DH):
                        j = 4 * m + h
                        pe.matmul(turn[2 + m][:, h * P:(h + 1) * P], Y[:, j, :], XT[:, j, :], start=True, stop=True)
                    for h in range(DH):
                        j = 4 * m + h
                        ins = pe.matmul(turn[m][:, h * P:(h + 1) * P], XT[:, j, :], Y[:, j, :], start=True, stop=True)
                    ins.then_inc(iv.pe, 1)

        def rc_pe(pe):
            pe.wait_ge(iv.vec, INV_DONE)
            for m in range(MT):
                for h in range(DH):
                    ins = pe.matmul(turn[m][:, h * P:(h + 1) * P], XT[:, 4 * m + h, :], v_tok2[:, m, h * P:(h + 1) * P],
                                    start=True, stop=True)
                ins.then_inc(rc.pe, 1)
            for m in range(MT):
                for h in range(DH):
                    ins = pe.matmul(turn[2 + m][:, h * P:(h + 1) * P], kbe[:, m, h * P:(h + 1) * P], XT[:, 4 * m + h, :],
                                    start=True, stop=True)
                ins.then_inc(rc.pe, 1)
            for n in range(4):
                m, b = n // 2, n % 2
                rows = slice(CH * b, CH * b + CH)
                if n > 0:
                    pe.wait_ge(rc.vec, 6 if n == 1 else 3 * n + 3)
                    for h in range(DH):
                        ins = pe.matmul(turn[0][rows, h * P:(h + 1) * P], wT[:, 4 * m + h, rows], S2[:, h * P:(h + 1) * P],
                                        start=True, stop=True)
                    ins.then_inc(rc.pe, 1)
                pe.wait_ge(rc.vec, 5 + 3 * n)
                for h in range(DH):
                    o = turn[1][rows, h * P:(h + 1) * P]
                    if n > 0:
                        pe.matmul(o, qgT[:, h, m * P + CH * b:m * P + CH * b + CH], S2[:, h * P:(h + 1) * P],
                                  start=True, stop=False)
                    ins = pe.matmul(o, attnT[rows, 4 * m + h, rows], vnew[rows, m, h * P:(h + 1) * P],
                                    start=(n == 0), stop=True)
                ins.then_inc(rc.pe, 1)
                if n < 3:
                    for h in range(DH):
                        ins = pe.matmul(turn[2][:, h * P:(h + 1) * P], k_tok[rows, m, h * P:(h + 1) * P],
                                        vnew[rows, m, h * P:(h + 1) * P], start=True, stop=True)
                    ins.then_inc(rc.pe, 1)

        def rc_vec(vec):
            for m in range(MT):
                vec.wait_ge(rc.pe, 1 + m)
                vec.tensor_copy(quad(u_sol, m), heads(turn[m][:, :], 4)).then_inc(rc.vec, 1)
            for m in range(MT):
                vec.wait_ge(rc.pe, 3 + m)
                vec.tensor_copy(quad(wT, m), heads(turn[2 + m][:, :], 4)).then_inc(rc.vec, 1)
            vec.wait_ge(rc.vec, 4)
            for n in range(4):
                m, b = n // 2, n % 2
                rows = slice(CH * b, CH * b + CH)
                v = vnew[rows, m, :].rearrange("p (h d) -> p h d", h=4)
                u = u_sol[rows, 4 * m:4 * m + 4, :]
                if n == 0:
                    vec.tensor_copy(v, u).then_inc(rc.vec, 1)
                else:
                    vec.wait_ge(rc.pe, 4 + 3 * n)
                    vec.tensor_tensor(v, u, turn[0][rows, :].rearrange("p (h d) -> p h d", h=4), ALU.subtract).then_inc(rc.vec, 1)
                if n < 3:
                    vec.wait_ge(rc.pe, 6 + 3 * n)
                    if n == 0:
                        ins = vec.tensor_copy(S2, turn[2][:, :])
                    else:
                        for h in range(DH):
                            a = ALC + 8 * b + 4 * m + h
                            sh = S2[:, h * P:(h + 1) * P]
                            ins = vec.scalar_tensor_tensor(out=sh, in0=sh, scalar=cs2[:, a:a + 1],
                                                           in1=turn[2][:, h * P:(h + 1) * P], op0=ALU.mult, op1=ALU.add)
                    ins.then_inc(rc.vec, 1)
                else:
                    vec.wait_ge(rc.pe, 14)
                vec.tensor_copy(o_s[rows, m, :], turn[1][rows, :]).then_inc(rc.vec, 1)
            for m in range(MT):
                vec.wait_ge(rc.act, 1 + m)
                vec.tensor_reduce(st2[:, 32 + 4 * m:36 + 4 * m], heads(kbe[:, m, :], 4), AX, ALU.add).then_inc(rc.vec, 1)
            vec.wait_ge(rc.act, 3)
            vec.reciprocal(st2[:, 40:48], st2[:, 40:48]).then_inc(rc.vec, 1)
            vec.wait_ge(rc.vec, 18)
            for m in range(MT):
                vec.tensor_tensor(heads(o_s[:, m, :], 4), heads(o_s[:, m, :], 4), over(st2[:, 40 + 4 * m:44 + 4 * m], 4, P),
                                  ALU.mult).then_inc(rc.vec, 1)
            for m in range(MT):
                vec.wait_ge(rc.vec, 19 + m)
                wait_acc_read(vec, G_Z2, m)
                vec.tensor_tensor(o_s[:, m, :], o_s[:, m, :], z_s[:, m, :], ALU.mult).then_inc(rc.vec, 1)
            for m in range(MT):
                vec.wait_ge(rc.pe, 15 + m)
                vec.tensor_tensor(xT[:, 0:4, m * P:(m + 1) * P], heads(turn[m][:, :], 4),
                                  col[:, R2["dng"]:R2["dng"] + 1].unsqueeze(2).broadcast_to([P, 4, P]), ALU.mult).then_inc(rc.vec, 1)

        def rc_act(act):
            act.wait_ge(rc.vec, 15)
            for m in range(MT):
                act.activation(kbe[:, m, :], o_s[:, m, :], ACT.Square).then_inc(rc.act, 1)
            act.wait_ge(rc.vec, 17)
            act.activation(st2[:, 40:48], st2[:, 32:40], ACT.Sqrt, bias=eps_col[:, 0:1], scale=1.0 / HD).then_inc(rc.act, 1)

        def rc_out_pe(pe):
            for m in range(MT):
                pe.wait_ge(rc.vec, 21 + m)
                for h in range(DH):
                    ins = pe.transpose(turn[m][:, h * P:(h + 1) * P], o_s[:, m, h * P:(h + 1) * P], ident[:, :])
                ins.then_inc(rc.pe, 1)

        def y_step(k):
            return 3 + 2 * k if k < 15 else 32

        def bu_step(k):
            return 1 + k if k < 2 else 2 * k

        def s5_bu_pe(pe, k):
            c, j = k // 4, k % 4
            rows = slice(32 * j, 32 * j + 32)
            pe.wait_ge(s5.vec, 7 * (k - 2) + 2) if k >= 2 else pe.wait_ge(rc.vec, 24)
            for i in range(2):
                ins = pe.matmul(turn[k % 2][:, i * TOK:(i + 1) * TOK], bbT[i][rows, c, :], uT[rows, c, :], start=True, stop=True)
            ins.then_inc(s5.pe, 1)

        def s5_pe(pe):
            for q in range(2):
                wait_acc_read(pe, G_U2, q)
            s5_bu_pe(pe, 0)
            s5_bu_pe(pe, 1)
            for k in range(NS):
                c, j = k // 4, k % 4
                if j == 0 and c >= 2:
                    pe.wait_ge(gl.vec, c - 1)
                pe.wait_ge(s5.pool, 3 * k + 3)
                for i in range(2):
                    ins = pe.matmul(turn[2 + c % 2][32 * j:32 * j + 32, 0:TOK], cT[i][:, c, 32 * j:32 * j + 32],
                                    xst[:, k % 2, i, :], start=(i == 0), stop=(i == 1))
                ins.then_inc(s5.pe, 1)
                if k + 2 < NS:
                    s5_bu_pe(pe, k + 2)
                memory_values_pe(pe, k)

        def s5_y_vec(vec, c):
            vec.wait_ge(s5.pe, y_step(4 * c + 3))
            vec.scalar_tensor_tensor(out=yg[:, c, :], in0=uT[:, c, :], scalar=col[:, R2["d"] + c:R2["d"] + c + 1],
                                     in1=turn[2 + c % 2][:, 0:TOK], op0=ALU.mult, op1=ALU.add).then_inc(gl.vec, 1)

        def s5_vec(vec):
            vec.wait_ge(rot, ROT_DONE)
            for k in range(NS):
                b = k % 2
                bu = turn[b][:, :].rearrange("p (i n) -> p i n", i=2)
                vec.wait_ge(s5.pe, bu_step(k))
                vec.tensor_tensor(tv[:, b, 0:2, :], bu, rot_c[:, k, :].unsqueeze(1).broadcast_to([P, 2, TOK]), ALU.mult).then_inc(s5.vec, 1)
                vec.tensor_tensor(tv[:, b, 2:4, :], bu, rot_s[:, k, :].unsqueeze(1).broadcast_to([P, 2, TOK]), ALU.mult).then_inc(s5.vec, 1)
                vec.wait_ge(s5.vec, 7 * k + 2)
                vec.tensor_tensor(zin[:, b, 0, :], tv[:, b, 0, :], tv[:, b, 3, :], ALU.add).then_inc(s5.vec, 1)
                vec.tensor_tensor(zin[:, b, 1, :], tv[:, b, 1, :], tv[:, b, 2, :], ALU.subtract).then_inc(s5.vec, 1)
                if k >= 2:
                    vec.wait_ge(s5.pool, 3 * (k - 2) + 1)
                for i in range(2):
                    vec.wait_ge(s5.vec, 7 * k + 3 + i)
                    vec.tensor_tensor_scan(zsc[:, b, i, :], s5w[:, MAG, k:k + 1].broadcast_to([P, TOK]), zin[:, b, i, :],
                                           0.0, ALU.mult, ALU.add).then_inc(s5.vec, 1)
                vec.wait_ge(s5.vec, 7 * k + 6)
                if k >= 2:
                    vec.wait_ge(s5.pool, 3 * (k - 2) + 3)
                vec.tensor_tensor(by_sin[:, b], zsc[:, b], rot_s[:, k, :].unsqueeze(1).broadcast_to([P, 2, TOK]),
                                  ALU.mult).then_inc(s5.vec, 1)
                if k >= 5 and k % 4 == 1:
                    s5_y_vec(vec, (k - 5) // 4)
            s5_y_vec(vec, 3)

        def s5_pool(pool):
            for k in range(NS):
                b = k % 2
                pool.wait_ge(s5.vec, 7 * k + 6)
                pool.tensor_tensor(by_cos[:, b], zsc[:, b], rot_c[:, k, :].unsqueeze(1).broadcast_to([P, 2, TOK]), ALU.mult).then_inc(s5.pool, 1)
                pool.wait_ge(s5.pool, 3 * k + 1)
                pool.wait_ge(s5.vec, 7 * k + 7)
                if k >= 2:
                    pool.wait_ge(s5.pe, y_step(k - 2))
                pool.tensor_tensor(xst[:, b, 0, :], by_cos[:, b, 0, :], by_sin[:, b, 1, :], ALU.subtract).then_inc(s5.pool, 1)
                pool.tensor_tensor(xst[:, b, 1, :], by_cos[:, b, 1, :], by_sin[:, b, 0, :], ALU.add).then_inc(s5.pool, 1)

        def glu_act(act):
            for c in range(4):
                act.wait_ge(gl.vec, 1 + c)
                act.activation(yg[:, c, :], yg[:, c, :], ACT.Gelu_apprx_tanh).then_inc(gl.act, 1)
                if c in (1, 3):
                    mv_act(act, c // 2)
            wait_products(act, C_GLU)
            for f in range(4):
                ins = act.activation(ysig[:, f, :], acc[bank(G_GLU, f // 2)][:, (f % 2) * TOK:(f % 2 + 1) * TOK], ACT.Sigmoid,
                                     bias=col[:, R2["bglu"] + f:R2["bglu"] + f + 1])
                if f % 2 == 1:
                    ins.then_inc(acc_read[bank(G_GLU, f // 2)], 1)

        def glu_vec(vec):
            for q in range(2):
                wait_acc_read(vec, G_GLU, q)
                vec.tensor_tensor(xT[:, 4 + 2 * q:6 + 2 * q, :], yg[:, 2 * q:2 * q + 2, :], ysig[:, 2 * q:2 * q + 2, :],
                                  ALU.mult).then_inc(gl.vec, 1)

        XS = 256 ** -0.5

        def feat_act(act, G, c, dst, f):
            wait_products(act, c + 1)
            for q in range(2):
                act.activation(dst[:, f + 2 * q:f + 2 * q + 2, :], heads(acc[bank(G, q)][:, :], 2),
                               ACT.Copy).then_inc(acc_read[bank(G, q)], 1)

        def mv_act(act, n):
            wait_products(act, C_MV + 2 * n + 1)
            for m in range(MT):
                act.activation(vm[:, m, n * 512:(n + 1) * 512], acc[bank(G_MV + n, m)][:, :],
                               ACT.Copy).then_inc(acc_read[bank(G_MV + n, m)], 1)

        def xa_scores_pe(pe):
            for G in (G_MK, G_MK + 1, G_XQ, G_XQ + 1):
                for q in range(2):
                    wait_acc_read(pe, G, q)
            for r in range(4):
                m, hp = r // 2, r % 2
                for h2 in range(2):
                    f = 2 * (2 * hp + h2)
                    for k in range(2):
                        ins = pe.matmul(turn[r][:, h2 * TOK:(h2 + 1) * TOK], qcT[:, f + k, m * P:(m + 1) * P], kmT[:, f + k, :],
                                        start=(k == 0), stop=(k == 1))
                ins.then_inc(xa.pe, 1)

        def xa_vec1(vec):
            for m in range(MT):
                for r in range(2 * m, 2 * m + 2):
                    vec.wait_ge(xa.pe, 1 + r)
                    vec.tensor_reduce(st2[:, 48 + 2 * r:50 + 2 * r], heads(turn[r][:, :], 2), AX, ALU.max).then_inc(xa.vec, 1)
                vec.wait_ge(xa.vec, 3 * m + 2)
                vec.tensor_scalar(st2[:, 56 + 4 * m:60 + 4 * m], st2[:, 48 + 4 * m:52 + 4 * m], -XS, None,
                                  ALU.mult).then_inc(xa.vec, 1)
            for m in range(MT):
                vec.wait_ge(xa.act, 4 * m + 4)
                vec.reciprocal(st2[:, 72 + 4 * m:76 + 4 * m], st2[:, 64 + 4 * m:68 + 4 * m]).then_inc(xa.vec, 1)
                vec.wait_ge(xa.vec, 7 + 2 * m)
                vec.tensor_tensor(quad(pc, m), quad(pc, m), over(st2[:, 72 + 4 * m:76 + 4 * m], 4, TOK), ALU.mult).then_inc(xa.vec, 1)

        def xa_act(act):
            for j in range(8):
                act.wait_ge(xa.vec, 3 + 3 * (j // 4))
                act.activation(pc[:, j, :], turn[j // 2][:, (j % 2) * TOK:(j % 2 + 1) * TOK], ACT.Exp,
                               bias=st2[:, 56 + j:57 + j], scale=XS, accum_out=st2[:, 64 + j:65 + j]).then_inc(xa.act, 1)

        def xa_turn_pe(pe):
            for r in range(4):
                m, kb_ = r // 2, r % 2
                pe.wait_ge(xa.vec, 8 + 2 * m)
                for h in range(4):
                    ins = pe.transpose(turn[r][:, h * P:(h + 1) * P], pc[:, 4 * m + h, kb_ * P:(kb_ + 1) * P], ident[:, :])
                ins.then_inc(xa.pe, 1)

        def xa_vec2(vec):
            for r in range(4):
                m, kb_ = r // 2, r % 2
                vec.wait_ge(xa.pe, 5 + r)
                vec.tensor_copy(PTc[:, kb_, :, m * P:(m + 1) * P], heads(turn[r][:, :], 4)).then_inc(xa.vec, 1)
            for r in range(4):
                vec.wait_ge(xa.pe, 9 + r)
                vec.tensor_copy(xT[:, 2 * r:2 * r + 2, :], heads(turn[r][:, :], 2)).then_inc(xa.vec, 1)

        def xa_pv_pe(pe):
            pe.wait_ge(xa.vec, 14)
            for f in range(8):
                for k in range(2):
                    ins = pe.matmul(turn[f // 2][:, (f % 2) * TOK:(f % 2 + 1) * TOK], vm[:, k, f * P:(f + 1) * P],
                                    PTc[:, k, f // 2, :], start=(k == 0), stop=(k == 1))
                if f % 2 == 1:
                    ins.then_inc(xa.pe, 1)

        def second_pe(pe):
            pe.sem_inc(products_done, RING)
            norm_pe(pe, nm)
            first_gain2_pe(pe)
            pe.wait_ge(nm.vec, NORM_DONE)
            turned_group_pe(pe, G_Q2, C_Q2, xT, 4, 512)
            params2_pe(pe)
            pe.wait_ge(p2.vec, 3)
            turned_group_pe(pe, G_K2, C_K2, xT, 4, 512)
            s5p_pe(pe)
            norm_pe(pe, nmem, nb=memx)
            turned_group_pe(pe, G_V2, C_V2, xT, 4, 512)
            pe.wait_ge(nmem.vec, NORM_DONE)
            ab_pe(pe)
            group_pe(pe, G_Z2, C_Z2, xT, (4, 4), 520, n_used=512)
            turned_group_pe(pe, G_U2, C_U2, xT, 4, 512)
            dn_cs_pe(pe)
            turned_group_pe(pe, G_MK, C_MK, memT, 4, 512)
            dn_turn_pe(pe)
            turned_group_pe(pe, G_MK + 1, C_MK + 2, memT, 4, 512)
            dn_turn2_pe(pe)
            dn_kk_pe(pe)
            dn_qg_pe(pe)
            inv_pe(pe)
            rc_pe(pe)
            rc_out_pe(pe)
            s5_pe(pe)
            pe.wait_ge(gl.act, 4)
            turned_group_pe(pe, G_GLU, C_GLU, yg, 4, 512, K=4)
            pe.wait_ge(gl.vec, 6)
            group_pe(pe, G_WO2, C_WO2, xT, (4, 4), 512)
            group_pe(pe, G_WO2 + 1, C_WO2 + 2, xT, (4, 4), 512, for_x=True)
            norm_pe(pe, nx)
            pe.wait_ge(nx.vec, NORM_DONE)
            turned_group_pe(pe, G_XQ, C_XQ, xT, 4, 512)
            turned_group_pe(pe, G_XQ + 1, C_XQ + 2, xT, 4, 512)
            xa_scores_pe(pe)
            xa_turn_pe(pe)
            xa_pv_pe(pe)
            pe.wait_ge(xa.vec, 18)
            group_pe(pe, G_XO, C_XO, xT, (4, 4), 512)
            group_pe(pe, G_XO + 1, C_XO + 2, xT, (4, 4), 512, for_x=True)
            norm_pe(pe, n3)
            ffn_pe(pe, f3, n3, C_FFN3, G_FFN3)

        def second_act(act):
            first_gain2_act(act)
            norm_act(act, nm)
            params2_act(act)
            s5p_act(act)

            def memory_there(e, m):
                e.wait_ge(mem_in, 16)
                e.wait_ge(nm.pe, 4)
            norm_act(act, nmem, src=memx, wait_src=memory_there)
            conv2_act1(act)
            wait_products(act, C_Z2 + 1)
            for m in range(MT):
                act.activation(z_s[:, m, :], acc[bank(G_Z2, m)][:, :], ACT.Silu).then_inc(acc_read[bank(G_Z2, m)], 1)
            ab_act(act)
            conv2_act2(act)
            feat_act(act, G_U2, C_U2, uT, 0)
            dn_cs_act(act)
            feat_act(act, G_MK, C_MK, kmT, 0)
            dn_turn_act(act)
            feat_act(act, G_MK + 1, C_MK + 2, kmT, 4)
            rc_act(act)
            glu_act(act)
            norm_act(act, nx, wait_src=lambda e, m: wait_x(e, G_WO2, m))
            feat_act(act, G_XQ, C_XQ, qcT, 0)
            feat_act(act, G_XQ + 1, C_XQ + 2, qcT, 4)
            xa_act(act)
            first_split_act(act, f3, C_FFN3)
            norm_act(act, n3, wait_src=lambda e, m: wait_x(e, G_XO, m))
            split_x_act(act, n3)
            ffn_act(act, f3, C_FFN3, G_FFN3)
            norm_act(act, nf, wait_src=lambda e, m: wait_x(e, G_FFN3 + NFB, m))

        def second_vec(vec):
            for i in range(4):
                vec.sem_inc(acc_read[i], 1)
            norm_vec(vec, nm, col[:, R2["mix"]:R2["mix"] + 8], between=first_gain2_vec)
            masks_vec(vec)
            params2_vec(vec)
            s5p_vec(vec)
            s5p_vec2(vec)
            vec.memset(xpad2[:, :, 0:3], 0.0).then_inc(c2.vec, 1)
            norm_vec(vec, nmem, col[:, R2["mem"]:R2["mem"] + 8], src=memx, nb=memx, dst=memT)
            conv2_vec(vec)
            ab_vec(vec)
            dn_cs_vec(vec)
            dn_turn_vec(vec)
            dn_turn2_vec(vec)
            dn_kk_vec(vec)
            dn_qg_vec(vec)
            inv_vec(vec)
            rc_vec(vec)
            s5_vec(vec)
            glu_vec(vec)
            add_to_x(vec, C_WO2 + 3, G_WO2, 1.0, 1)
            norm_vec(vec, nx, col[:, R2["x"]:R2["x"] + 8])
            xa_vec1(vec)
            xa_vec2(vec)
            first_split_vec(vec, f3, C_FFN3)
            add_to_x(vec, C_XO + 3, G_XO, 1.0, 2)
            norm_vec(vec, n3, col[:, R2["ffn"]:R2["ffn"] + 8])
            split_x_vec(vec, n3)
            ffn_vec(vec, f3, C_FFN3, G_FFN3, 1.0, 3)
            vec.wait_ge(fin_in, 16)
            for m in range(MT):
                vec.wait_ge(nf.act, 2 * m + 2)
                vec.reciprocal(stat[:, 4 + m:5 + m], stat[:, 2 + m:3 + m]).then_inc(nf.vec, 1)
                vec.wait_ge(nf.vec, 2 * m + 1)
                vec.scalar_tensor_tensor(out=xn[:, m, :], in0=x[:, m, :], scalar=stat[:, 4 + m:5 + m], in1=fin_g,
                                         op0=ALU.mult, op1=ALU.mult).then_inc(nf.vec, 1)

        with nc.Block() as block:
            @block.sync
            def _(sync):
                second_sync(sync)
                sync.wait_ge(n3.vec, SPLIT_DONE)
                sync.dma_start(fin_g, t["norm_final_g_2"].rearrange("(o d) -> o d", o=1).broadcast_to([P, D])).then_inc(fin_in, 16)
                for m in range(MT):
                    sync.wait_ge(nf.vec, 2 * m + 2)
                    sync.dma_start(out[0, m * P:(m + 1) * P, :], xn[:, m, :]).then_inc(out_done, 16)
                sync.wait_ge(out_done, 16 * MT)

            @block.gpsimd
            def _(pool):
                masks_pool(pool)
                rotations_pool(pool)
                s5_pool(pool)

            @block.scalar
            def _(act):
                second_act(act)

            @block.vector
            def _(vec):
                second_vec(vec)

            @block.tensor
            def _(pe):
                second_pe(pe)


def kernel(**inputs):
    import concourse.bacc as bacc
    from concourse.bass_utils import run_bass_kernel_spmd

    nc = bacc.Bacc("TRN2", target_bir_lowering=False, num_devices=1)
    arrays, tensors = {}, {}
    for name in INPUTS:
        a = np.ascontiguousarray(inputs[name])
        arrays["in_" + name] = a
        tensors[name] = nc.dram_tensor("in_" + name, a.shape, mybir.dt.from_np(a.dtype), kind="ExternalInput").ap()
    out = nc.dram_tensor("out_0", (1, TOK, D), F32, kind="ExternalOutput").ap()
    build(nc, tensors, out)
    r = run_bass_kernel_spmd(nc, [arrays], core_ids=[0])
    return r.results[0]["out_0"]
```
